# Optimizing a Trainium2 kernel written in Bass

```python
import math
import jax, jax.numpy as jnp
from jax import lax
import numpy as np

D_MODEL = 1024
BATCH = 1
SEQ = 512
DEPTH = 2

CHUNK = 64
Q_BLOCK = 128
PLE_DIM = 256
RMS_EPS = 1e-6

SB_HEADS = 8
SB_HEAD_DIM = 64
SB_WIDTH = SB_HEADS * SB_HEAD_DIM

DA_HEADS = 4
DA_HEAD_DIM = 64
DA_V_DIM = 2 * DA_HEAD_DIM
DA_QK_WIDTH = DA_HEADS * 2 * DA_HEAD_DIM
DA_WIDTH = DA_HEADS * DA_V_DIM

ROPE_THETA = 500000.0
ROPE_DIM = DA_HEAD_DIM // 4

N_GROUPS = 4
EXPERTS_PER_GROUP = 8
N_EXPERTS = N_GROUPS * EXPERTS_PER_GROUP
TOP_K = 2
EXPERT_HIDDEN = 256
MOE_BLOCK = 256

IN_SIZES = (SB_WIDTH, SB_WIDTH, SB_WIDTH, DA_QK_WIDTH, DA_QK_WIDTH, DA_WIDTH, D_MODEL, D_MODEL)
IN_WIDTH = sum(IN_SIZES)
IN_OFFSETS = tuple(int(o) for o in np.cumsum(IN_SIZES)[:-1])


def rmsnorm(x, g):
    xf = x.astype(jnp.float32)
    y = xf * lax.rsqrt(jnp.mean(xf * xf, axis=-1, keepdims=True) + RMS_EPS)
    return (y * g.astype(jnp.float32)).astype(x.dtype)

def apply_partial_rope(t, cos, sin):
    half = ROPE_DIM // 2
    r1 = t[..., :half]
    r2 = t[..., half:ROPE_DIM]
    rot = jnp.concatenate([r1 * cos - r2 * sin, r2 * cos + r1 * sin], axis=-1)
    return jnp.concatenate([rot, t[..., ROPE_DIM:]], axis=-1)

def stick_breaking_attention(q, k, v):
    B, H, S, d = q.shape
    scale = d ** -0.5
    key_idx = jnp.arange(S)

    def block(j):
        start = j * Q_BLOCK
        qb = lax.dynamic_slice_in_dim(q, start, Q_BLOCK, axis=2)
        z = jnp.einsum('bhqd,bhkd->bhqk', qb, k, preferred_element_type=jnp.float32) * scale
        q_idx = start + jnp.arange(Q_BLOCK)
        strict = key_idx[None, :] < q_idx[:, None]
        log_stay = jnp.where(strict, jax.nn.log_sigmoid(-z), 0.0)
        between = lax.cumsum(log_stay, axis=3, reverse=True) - log_stay
        w = jnp.where(strict, jnp.exp(jax.nn.log_sigmoid(z) + between), 0.0)
        return jnp.einsum('bhqk,bhkd->bhqd', w.astype(v.dtype), v)

    out = lax.map(block, jnp.arange(S // Q_BLOCK))
    return out.transpose(1, 0, 3, 2, 4).reshape(B, S, H, d)

def differential_attention(q, k, v, lam):
    B, H, _, S, d = q.shape
    dv = v.shape[-1]
    scale = d ** -0.5
    key_chunk = jnp.arange(S) // CHUNK
    neg = jnp.finfo(jnp.float32).min

    def block(j):
        start = j * Q_BLOCK
        qb = lax.dynamic_slice_in_dim(q, start, Q_BLOCK, axis=3)
        s = jnp.einsum('bhmqd,bhmkd->bhmqk', qb, k, preferred_element_type=jnp.float32) * scale
        q_chunk = (start + jnp.arange(Q_BLOCK)) // CHUNK
        allowed = key_chunk[None, :] <= q_chunk[:, None]
        a = jax.nn.softmax(jnp.where(allowed, s, neg), axis=-1)
        a = a[:, :, 0] - lam * a[:, :, 1]
        return jnp.einsum('bhqk,bhkd->bhqd', a.astype(v.dtype), v)

    out = lax.map(block, jnp.arange(S // Q_BLOCK))
    return out.transpose(1, 0, 3, 2, 4).reshape(B, S, H, dv)

def hierarchical_moe(h, w_rg, b_rg, w_re, b_re, w_gate, w_up, w_down):
    B, S, D = h.shape
    N = B * S
    t = h.reshape(N, D)
    rows = jnp.arange(N)
    g_logits = (t @ w_rg).astype(jnp.float32) + b_rg.astype(jnp.float32)
    g_prob = jax.nn.softmax(g_logits, axis=-1)
    g_sel = jnp.argmax(g_logits, axis=-1)
    g_p = g_prob[rows, g_sel]
    e_logits = ((t @ w_re).astype(jnp.float32) + b_re.astype(jnp.float32)).reshape(N, N_GROUPS, EXPERTS_PER_GROUP)
    e_prob = jax.nn.softmax(e_logits[rows, g_sel], axis=-1)
    top_p, top_i = lax.top_k(e_prob, TOP_K)
    gates = g_p[:, None] * top_p / jnp.sum(top_p, axis=-1, keepdims=True)

    expert_id = (g_sel[:, None] * EXPERTS_PER_GROUP + top_i).reshape(-1)
    token_id = jnp.repeat(rows, TOP_K)
    gate_flat = gates.reshape(-1)
    A = N * TOP_K

    order = jnp.argsort(expert_id)
    se, st, sg = expert_id[order], token_id[order], gate_flat[order]
    counts = jnp.zeros((N_EXPERTS,), jnp.int32).at[expert_id].add(1)
    pcounts = (counts + MOE_BLOCK - 1) // MOE_BLOCK * MOE_BLOCK
    starts = jnp.cumsum(counts) - counts
    pends = jnp.cumsum(pcounts)
    pstarts = pends - pcounts
    dest = pstarts[se] + jnp.arange(A) - starts[se]
    P = ((A + MOE_BLOCK - 1) // MOE_BLOCK) * MOE_BLOCK + N_EXPERTS * MOE_BLOCK
    n_blk = P // MOE_BLOCK
    slot_tok = jnp.full((P,), N, jnp.int32).at[dest].set(st)
    slot_gate = jnp.zeros((P,), jnp.float32).at[dest].set(sg)
    blk_e = jnp.minimum(jnp.searchsorted(pends, jnp.arange(n_blk) * MOE_BLOCK, side='right'), N_EXPERTS - 1)
    xs = jnp.concatenate([t, jnp.zeros((1, D), t.dtype)], axis=0)[slot_tok].reshape(n_blk, MOE_BLOCK, D)

    def expert_block(args):
        xb, e = args
        hid = jax.nn.silu(xb @ w_gate[e]) * (xb @ w_up[e])
        return hid @ w_down[e]

    ys = lax.map(expert_block, (xs, blk_e)).reshape(P, D)
    ys = ys * slot_gate[:, None].astype(ys.dtype)
    out = jax.ops.segment_sum(ys, slot_tok, num_segments=N + 1)[:N]
    return out.reshape(B, S, D)

def first_inputs(seed: int = 0) -> dict:
    key = jax.random.key(seed)
    ks = jax.random.split(key, 26)
    D = D_MODEL

    def nrm(k, shape, scale):
        return jax.random.normal(k, shape, jnp.float32) * scale

    def gain(k, shape):
        return 1.0 + 0.02 * jax.random.normal(k, shape, jnp.float32)

    offset = jax.random.randint(ks[2], (BATCH, 1), 0, 4096, dtype=jnp.int32)
    positions = (offset + jnp.arange(SEQ, dtype=jnp.int32)[None, :]).astype(jnp.int32)
    return {
        "x": nrm(ks[0], (BATCH, SEQ, D), 1.0),
        "p": nrm(ks[1], (DEPTH, BATCH, SEQ, PLE_DIM), 1.0),
        "positions": positions,
        "g_mix": gain(ks[3], (DEPTH, D)),
        "w_in": nrm(ks[4], (DEPTH, D, IN_WIDTH), D ** -0.5),
        "lam_q1": nrm(ks[5], (DEPTH, DA_HEAD_DIM), 0.1),
        "lam_k1": nrm(ks[6], (DEPTH, DA_HEAD_DIM), 0.1),
        "lam_q2": nrm(ks[7], (DEPTH, DA_HEAD_DIM), 0.1),
        "lam_k2": nrm(ks[8], (DEPTH, DA_HEAD_DIM), 0.1),
        "g_subln": gain(ks[9], (DEPTH, DA_V_DIM)),
        "w_br_a": nrm(ks[10], (DEPTH, SB_WIDTH, D), SB_WIDTH ** -0.5),
        "w_br_b": nrm(ks[11], (DEPTH, DA_WIDTH, D), DA_WIDTH ** -0.5),
        "w_o": nrm(ks[12], (DEPTH, D, D), D ** -0.5),
        "g_ffn": gain(ks[13], (DEPTH, D)),
        "w_router_group": nrm(ks[14], (DEPTH, D, N_GROUPS), D ** -0.5),
        "b_router_group": nrm(ks[15], (DEPTH, N_GROUPS), 0.01),
        "w_router_expert": nrm(ks[16], (DEPTH, D, N_EXPERTS), D ** -0.5),
        "b_router_expert": nrm(ks[17], (DEPTH, N_EXPERTS), 0.01),
        "w_exp_gate": nrm(ks[18], (DEPTH, N_EXPERTS, D, EXPERT_HIDDEN), D ** -0.5),
        "w_exp_up": nrm(ks[19], (DEPTH, N_EXPERTS, D, EXPERT_HIDDEN), D ** -0.5),
        "w_exp_down": nrm(ks[20], (DEPTH, N_EXPERTS, EXPERT_HIDDEN, D), EXPERT_HIDDEN ** -0.5),
        "g_ple": gain(ks[21], (DEPTH, D)),
        "w_ple": nrm(ks[22], (DEPTH, PLE_DIM, D), PLE_DIM ** -0.5),
        "w_ple_gate": nrm(ks[23], (DEPTH, D, D), D ** -0.5),
        "g_final": gain(ks[24], (D,)),
    }

def first_block(x, p, positions, g_mix, w_in, lam_q1, lam_k1, lam_q2, lam_k2, g_subln,
              w_br_a, w_br_b, w_o, g_ffn, w_router_group, b_router_group,
              w_router_expert, b_router_expert, w_exp_gate, w_exp_up, w_exp_down,
              g_ple, w_ple, w_ple_gate, g_final):
    B, S, D = x.shape
    inv_freq = ROPE_THETA ** (-jnp.arange(0, ROPE_DIM, 2, dtype=jnp.float32) / ROPE_DIM)
    ang = positions.astype(jnp.float32)[..., None] * inv_freq
    cos = jnp.cos(ang)[:, :, None, None, :].astype(x.dtype)
    sin = jnp.sin(ang)[:, :, None, None, :].astype(x.dtype)

    for i in range(DEPTH):
        lam_init = 0.8 - 0.6 * math.exp(-0.3 * i)
        h = rmsnorm(x, g_mix[i])
        u = h @ w_in[i]
        sb_q, sb_k, sb_v, da_q, da_k, da_v, gate_a, gate_b = jnp.split(u, IN_OFFSETS, axis=-1)

        to_heads = lambda t: t.reshape(B, S, SB_HEADS, SB_HEAD_DIM).transpose(0, 2, 1, 3)
        y_a = stick_breaking_attention(to_heads(sb_q), to_heads(sb_k), to_heads(sb_v))
        y_a = y_a.reshape(B, S, SB_WIDTH) @ w_br_a[i]

        dq = apply_partial_rope(da_q.reshape(B, S, DA_HEADS, 2, DA_HEAD_DIM), cos, sin)
        dk = apply_partial_rope(da_k.reshape(B, S, DA_HEADS, 2, DA_HEAD_DIM), cos, sin)
        dq = dq.transpose(0, 2, 3, 1, 4)
        dk = dk.transpose(0, 2, 3, 1, 4)
        dv = da_v.reshape(B, S, DA_HEADS, DA_V_DIM).transpose(0, 2, 1, 3)
        lam = (jnp.exp(jnp.sum(lam_q1[i].astype(jnp.float32) * lam_k1[i].astype(jnp.float32)))
               - jnp.exp(jnp.sum(lam_q2[i].astype(jnp.float32) * lam_k2[i].astype(jnp.float32)))
               + lam_init)
        y_b = differential_attention(dq, dk, dv, lam)
        y_b = rmsnorm(y_b, g_subln[i]) * (1.0 - lam_init)
        y_b = y_b.reshape(B, S, DA_WIDTH) @ w_br_b[i]

        merged = jax.nn.sigmoid(gate_a) * y_a + jax.nn.sigmoid(gate_b) * y_b
        x = x + merged @ w_o[i]

        x = x + hierarchical_moe(rmsnorm(x, g_ffn[i]), w_router_group[i], b_router_group[i],
                                 w_router_expert[i], b_router_expert[i],
                                 w_exp_gate[i], w_exp_up[i], w_exp_down[i])

        ple_gate = jax.nn.sigmoid(rmsnorm(x, g_ple[i]) @ w_ple_gate[i])
        x = x + (p[i] @ w_ple[i]) * ple_gate

    return rmsnorm(x, g_final)


DEPTH_2 = 1

EPS = 1e-6
D_FF = 2816
MLA_HEADS = 8
MLA_Q_RANK = 384
MLA_KV_RANK = 256
MLA_NOPE = 64
MLA_ROPE = 32
MLA_V = 64
MLA_THETA = 10000.0
MLA_WIDTH = MLA_HEADS * MLA_V
DIL_HEADS = 8
DIL_HEAD_DIM = 64
DIL_PATTERNS = ((128, 1), (512, 4), (2048, 16))
DIL_WIDTH = DIL_HEADS * DIL_HEAD_DIM
ROPE_DIM_2 = DIL_HEAD_DIM // 4
N_BRANCH = 2
NEG = -1e30
IN_SPLITS = (MLA_Q_RANK, MLA_KV_RANK, MLA_ROPE, DIL_WIDTH, DIL_WIDTH, DIL_WIDTH, N_BRANCH * D_MODEL)
IN_DIM = int(sum(IN_SPLITS))


def rms_norm(x, g):
    xf = x.astype(jnp.float32)
    y = xf * lax.rsqrt(jnp.mean(xf * xf, axis=-1, keepdims=True) + EPS)
    return (y * g.astype(jnp.float32)).astype(x.dtype)

def rope(x, positions, theta, rot_dim):
    half = rot_dim // 2
    inv = 1.0 / (jnp.float32(theta) ** (jnp.arange(half, dtype=jnp.float32) / half))
    ang = positions.astype(jnp.float32)[:, :, None] * inv
    cos = jnp.cos(ang)[:, :, None, :]
    sin = jnp.sin(ang)[:, :, None, :]
    xr = x[..., :rot_dim].astype(jnp.float32)
    x1, x2 = xr[..., :half], xr[..., half:]
    rot = jnp.concatenate([x1 * cos - x2 * sin, x2 * cos + x1 * sin], axis=-1).astype(x.dtype)
    return jnp.concatenate([rot, x[..., rot_dim:]], axis=-1)

def swiglu(x, w_gate, w_up, w_down):
    return (jax.nn.silu(x @ w_gate) * (x @ w_up)) @ w_down

def dense_attention(q, k, v):
    B, S, H, Dk = q.shape
    scale = Dk ** -0.5
    nqb = S // Q_BLOCK
    qb = q.reshape(B, nqb, Q_BLOCK, H, Dk).transpose(1, 0, 2, 3, 4)

    def block(qi):
        s = jnp.einsum('bqhd,bkhd->bhqk', qi, k, preferred_element_type=jnp.float32) * scale
        p = jax.nn.softmax(s, axis=-1)
        return jnp.einsum('bhqk,bkhd->bqhd', p, v.astype(jnp.float32)).astype(v.dtype)

    o = lax.map(block, qb)
    return o.transpose(1, 0, 2, 3, 4).reshape(B, S, H, v.shape[-1])

def dilated_pattern(q, k, v, window, dilation):
    B, S, H, D = q.shape
    half = window // (2 * dilation)
    blk = half
    L = -(-S // dilation)
    Sp = L * dilation
    nb = -(-L // blk)
    Lp = nb * blk

    def split(t):
        t = jnp.pad(t, ((0, 0), (0, Sp - S), (0, 0), (0, 0)))
        return t.reshape(B, L, dilation, H, t.shape[-1]).transpose(0, 2, 3, 1, 4)

    def pad_l(t, lo, hi):
        return jnp.pad(t, ((0, 0), (0, 0), (0, 0), (lo, hi), (0, 0)))

    qs = pad_l(split(q), 0, Lp - L).reshape(B, dilation, H, nb, blk, D)

    def windows(t):
        dt = t.shape[-1]
        t = pad_l(split(t), blk, Lp - L + blk).reshape(B, dilation, H, nb + 2, blk, dt)
        return jnp.concatenate([t[:, :, :, :-2], t[:, :, :, 1:-1], t[:, :, :, 2:]], axis=-2)

    kw = windows(k)
    vw = windows(v)
    s = jnp.einsum('brhnqd,brhnkd->brhnqk', qs, kw, preferred_element_type=jnp.float32) * (D ** -0.5)
    a = jnp.arange(blk)[:, None]
    c = jnp.arange(3 * blk)[None, :]
    band = jnp.abs(c - blk - a) <= half
    jk = jnp.arange(nb)[:, None] * blk - blk + jnp.arange(3 * blk)[None, :]
    pos_k = jk[None] * dilation + jnp.arange(dilation)[:, None, None]
    valid = (jk[None] >= 0) & (pos_k < S)
    mask = band[None, None] & valid[:, :, None, :]
    s = jnp.where(mask[None, :, None], s, NEG)
    m = jnp.max(s, axis=-1, keepdims=True)
    p = jnp.exp(s - m)
    den = jnp.sum(p, axis=-1, keepdims=True)
    num = jnp.einsum('brhnqk,brhnkd->brhnqd', p, vw.astype(jnp.float32))

    def merge(t):
        x_ = t.shape[-1]
        t = t.reshape(B, dilation, H, Lp, x_)[:, :, :, :L]
        return t.transpose(0, 3, 1, 2, 4).reshape(B, Sp, H, x_)[:, :S]

    return merge(m), merge(den), merge(num)

def dilated_mixture(q, k, v):
    parts = [dilated_pattern(q, k, v, w, d) for (w, d) in DIL_PATTERNS]
    m_all = jnp.max(jnp.concatenate([pm for pm, _, _ in parts], axis=-1), axis=-1, keepdims=True)
    num = None
    den = None
    for pm, ps, pn in parts:
        wgt = jnp.exp(pm - m_all)
        num = wgt * pn if num is None else num + wgt * pn
        den = wgt * ps if den is None else den + wgt * ps
    return (num / den).astype(q.dtype)

def hybrid_mixer(u, positions, w_in, b_gate, q_norm_g, w_uq, kv_norm_g, w_uk, w_uv,
                 w_branch_a, w_branch_b, w_out):
    B, S, _ = u.shape
    proj = u @ w_in
    cq, ckv, kr, dq, dk, dv, g = jnp.split(proj, np.cumsum(IN_SPLITS)[:-1].tolist(), axis=-1)

    q = (rms_norm(cq, q_norm_g) @ w_uq).reshape(B, S, MLA_HEADS, MLA_NOPE + MLA_ROPE)
    q = jnp.concatenate([q[..., :MLA_NOPE], rope(q[..., MLA_NOPE:], positions, MLA_THETA, MLA_ROPE)], axis=-1)
    k_rope = rope(kr[:, :, None, :], positions, MLA_THETA, MLA_ROPE)
    c_kv = rms_norm(ckv, kv_norm_g)
    k_nope = (c_kv @ w_uk).reshape(B, S, MLA_HEADS, MLA_NOPE)
    v_a = (c_kv @ w_uv).reshape(B, S, MLA_HEADS, MLA_V)
    k_a = jnp.concatenate([k_nope, jnp.broadcast_to(k_rope, (B, S, MLA_HEADS, MLA_ROPE))], axis=-1)
    o_a = dense_attention(q, k_a, v_a).reshape(B, S, MLA_WIDTH)

    qd = rope(dq.reshape(B, S, DIL_HEADS, DIL_HEAD_DIM), positions, ROPE_THETA, ROPE_DIM_2)
    kd = rope(dk.reshape(B, S, DIL_HEADS, DIL_HEAD_DIM), positions, ROPE_THETA, ROPE_DIM_2)
    vd = dv.reshape(B, S, DIL_HEADS, DIL_HEAD_DIM)
    o_b = dilated_mixture(qd, kd, vd).reshape(B, S, DIL_WIDTH)

    gates = jax.nn.sigmoid((g + b_gate).reshape(B, S, N_BRANCH, D_MODEL))
    merged = gates[:, :, 0] * (o_a @ w_branch_a) + gates[:, :, 1] * (o_b @ w_branch_b)
    return merged @ w_out

def second_inputs(seed: int = 0) -> dict:
    key = jax.random.key(seed)
    ks = iter(jax.random.split(key, 32))

    def w(shape, fan_in):
        return jax.random.normal(next(ks), (DEPTH_2,) + shape, jnp.float32) * (fan_in ** -0.5)

    def gain(n):
        return 1.0 + 0.05 * jax.random.normal(next(ks), (DEPTH_2, n), jnp.float32)

    x = jax.random.normal(next(ks), (BATCH, SEQ, D_MODEL), jnp.float32)
    offset = jax.random.randint(next(ks), (BATCH, 1), 0, 4096, dtype=jnp.int32)
    positions = (offset + jnp.arange(SEQ, dtype=jnp.int32)[None, :]).astype(jnp.int32)
    return {
        'x': x,
        'positions': positions,
        'ffn1_pre_g': gain(D_MODEL),
        'ffn1_post_g': gain(D_MODEL),
        'ffn1_w_gate': w((D_MODEL, D_FF), D_MODEL),
        'ffn1_w_up': w((D_MODEL, D_FF), D_MODEL),
        'ffn1_w_down': w((D_FF, D_MODEL), D_FF),
        'mix_pre_g': gain(D_MODEL),
        'w_in': w((D_MODEL, IN_DIM), D_MODEL),
        'b_gate': 0.1 * jax.random.normal(next(ks), (DEPTH_2, N_BRANCH * D_MODEL), jnp.float32),
        'q_norm_g': gain(MLA_Q_RANK),
        'w_uq': w((MLA_Q_RANK, MLA_HEADS * (MLA_NOPE + MLA_ROPE)), MLA_Q_RANK),
        'kv_norm_g': gain(MLA_KV_RANK),
        'w_uk': w((MLA_KV_RANK, MLA_HEADS * MLA_NOPE), MLA_KV_RANK),
        'w_uv': w((MLA_KV_RANK, MLA_HEADS * MLA_V), MLA_KV_RANK),
        'w_branch_a': w((MLA_WIDTH, D_MODEL), MLA_WIDTH),
        'w_branch_b': w((DIL_WIDTH, D_MODEL), DIL_WIDTH),
        'w_out': w((D_MODEL, D_MODEL), D_MODEL),
        'mix_post_g': gain(D_MODEL),
        'ffn2_pre_g': gain(D_MODEL),
        'ffn2_post_g': gain(D_MODEL),
        'ffn2_w_gate': w((D_MODEL, D_FF), D_MODEL),
        'ffn2_w_up': w((D_MODEL, D_FF), D_MODEL),
        'ffn2_w_down': w((D_FF, D_MODEL), D_FF),
    }

def second_block(x, positions, ffn1_pre_g, ffn1_post_g, ffn1_w_gate, ffn1_w_up, ffn1_w_down,
              mix_pre_g, w_in, b_gate, q_norm_g, w_uq, kv_norm_g, w_uk, w_uv,
              w_branch_a, w_branch_b, w_out, mix_post_g,
              ffn2_pre_g, ffn2_post_g, ffn2_w_gate, ffn2_w_up, ffn2_w_down):
    h = x
    for l in range(DEPTH_2):
        f1 = swiglu(rms_norm(h, ffn1_pre_g[l]), ffn1_w_gate[l], ffn1_w_up[l], ffn1_w_down[l])
        h = h + 0.5 * rms_norm(f1, ffn1_post_g[l])
        mix = hybrid_mixer(rms_norm(h, mix_pre_g[l]), positions, w_in[l], b_gate[l],
                           q_norm_g[l], w_uq[l], kv_norm_g[l], w_uk[l], w_uv[l],
                           w_branch_a[l], w_branch_b[l], w_out[l])
        h = h + rms_norm(mix, mix_post_g[l])
        f2 = swiglu(rms_norm(h, ffn2_pre_g[l]), ffn2_w_gate[l], ffn2_w_up[l], ffn2_w_down[l])
        h = h + 0.5 * rms_norm(f2, ffn2_post_g[l])
    return h


def setup_inputs(seed=0):
    out = dict(first_inputs(seed))
    for name, value in second_inputs(seed + 1).items():
        if name != "x":
            out[name + "_2"] = value
    return out


def reference(
    x, p, positions, g_mix, w_in, lam_q1, lam_k1, lam_q2, lam_k2, g_subln, w_br_a, w_br_b, w_o,
    g_ffn, w_router_group, b_router_group, w_router_expert, b_router_expert, w_exp_gate,
    w_exp_up, w_exp_down, g_ple, w_ple, w_ple_gate, g_final, positions_2, ffn1_pre_g_2,
    ffn1_post_g_2, ffn1_w_gate_2, ffn1_w_up_2, ffn1_w_down_2, mix_pre_g_2, w_in_2, b_gate_2,
    q_norm_g_2, w_uq_2, kv_norm_g_2, w_uk_2, w_uv_2, w_branch_a_2, w_branch_b_2, w_out_2,
    mix_post_g_2, ffn2_pre_g_2, ffn2_post_g_2, ffn2_w_gate_2, ffn2_w_up_2, ffn2_w_down_2,
):
    x = first_block(
        x, p, positions, g_mix, w_in, lam_q1, lam_k1, lam_q2, lam_k2, g_subln, w_br_a, w_br_b,
        w_o, g_ffn, w_router_group, b_router_group, w_router_expert, b_router_expert,
        w_exp_gate, w_exp_up, w_exp_down, g_ple, w_ple, w_ple_gate, g_final,
    )
    return second_block(
        x, positions_2, ffn1_pre_g_2, ffn1_post_g_2, ffn1_w_gate_2, ffn1_w_up_2, ffn1_w_down_2,
        mix_pre_g_2, w_in_2, b_gate_2, q_norm_g_2, w_uq_2, kv_norm_g_2, w_uk_2, w_uv_2,
        w_branch_a_2, w_branch_b_2, w_out_2, mix_post_g_2, ffn2_pre_g_2, ffn2_post_g_2,
        ffn2_w_gate_2, ffn2_w_up_2, ffn2_w_down_2,
    )


_drawn_inputs = setup_inputs


def setup_inputs(seed=0):
    import zlib

    import numpy as np

    out = dict(_drawn_inputs(seed))
    spreads = {}
    factors = {'b_router_group': 3.806, 'g_ple': 4.359, 'q_norm_g_2': 6.069, 'ffn2_post_g_2': 3.583}
    for name, (base, spread) in spreads.items():
        noise = np.random.default_rng([zlib.crc32(name.encode()), seed]).standard_normal(out[name].shape)
        drawn = base * np.exp(spread * noise) if base else spread * noise
        out[name] = __import__('jax').numpy.asarray(drawn.astype(out[name].dtype))
    for name, factor in factors.items():
        out[name] = (out[name] * factor).astype(out[name].dtype)
    return out
```

```python
from contextlib import ExitStack
import math

import numpy as np
import concourse.bass as bass
from concourse import mybir

F32 = mybir.dt.float32
I32 = mybir.dt.int32
U32 = mybir.dt.uint32
ALU = mybir.AluOpType
ACT = mybir.ActivationFunctionType
AX = mybir.AxisListType.X

P = 128
S = 512
D = 1024
KD = D // P
TT = S // P
LAYERS = 2
UNIT = 2048
RING = 6
EPS = 1e-6

SB_H, DA_H, HD = 8, 4, 64
W_IN = 5120
NG, NEG_, NE = 4, 8, 32
EH = 256
CAP = 128
NB = 39
NBP = NB + 1
PLE = 256
FF = 2816
KF = FF // P
MLA_H, QR, KVR, NOPE, ROPE_M = 8, 384, 256, 64, 32
DQK = NOPE + ROPE_M
BIG_NEG = -1e30
N_CONST = 16 * 14

GAINS = ([(f"{n}{i}", l) for i in range(LAYERS) for n, l in
          (("g_mix", D), ("g_ffn", D), ("g_ple", D), ("g_subln", P))]
         + [("g_final", D)]
         + [(n, l) for n, l in (("ffn1_pre", D), ("ffn1_post", D), ("mix_pre", D), ("q_norm", QR),
                                ("kv_norm", KVR), ("mix_post", D), ("ffn2_pre", D), ("ffn2_post", D),
                                ("b_gate", 2 * D))])
GCOL = {}
_c = 0
for _n, _l in GAINS:
    GCOL[_n] = _c
    _c += _l // P
NGC = _c


def unit_of(w, k0, k1, c0, c1):
    nk = (k1 - k0) // P
    a = w[k0:k1, c0:c1].reshape(nk, P, c1 - c0).transpose(1, 0, 2).reshape(P, nk * (c1 - c0))
    u = np.zeros((P, UNIT), w.dtype)
    u[:, :a.shape[1]] = a
    return u


def cut(w, width):
    return [unit_of(w, 0, w.shape[0], c, c + width) for c in range(0, w.shape[1], width)]


def ffn_units(wg, wu, wd):
    out = []
    for c in range(0, FF, 256):
        out += [unit_of(wg, 0, D, c, c + 256), unit_of(wu, 0, D, c, c + 256)]
    for c in range(0, D, 256):
        for k in range(0, FF, D):
            out.append(unit_of(wd, k, min(k + D, FF), c, c + 256))
    return out


def layer_units(w_in, w_a, w_b, w_o):
    return cut(w_in, 256) + cut(w_a, 512) + cut(w_b, 512) + cut(w_o, 256)


def ple_units(w_gate, w_ple):
    return cut(w_gate, 256) + cut(w_ple, 1024)


def mixer_units(w_in, w_uq, w_uk, w_uv, w_a, w_b, w_o):
    u = [unit_of(w_in, 0, D, 0, 256), unit_of(w_in, 0, D, 256, 384), unit_of(w_in, 0, D, 384, 640),
         unit_of(w_in, 0, D, 576, 672)]
    u += [unit_of(w_in, 0, D, c, c + 256) for c in range(672, w_in.shape[1], 256)]
    return (u + cut(w_uq, 384) + cut(w_uk, 512) + cut(w_uv, 512)
            + cut(w_a, 512) + cut(w_b, 512) + cut(w_o, 256))


N_LAYER_U = 20 + 2 + 2 + 4
N_PLE_U = 4 + 1
N_FFN_U = 22 + 12
N_MIX_U = 4 + 14 + 2 + 1 + 1 + 2 + 2 + 4
N_STREAM = LAYERS * (N_LAYER_U + N_PLE_U) + 2 * N_FFN_U + N_MIX_U


def shape_constants():
    i = np.arange(P)
    ident = (i[:, None] == i[None, :]).astype(np.float32)
    ones = np.ones((P, P), np.float32)
    ntri = -(i[:, None] >= i[None, :]).astype(np.float32)
    before = (i[:, None] < i[None, :]).astype(np.float32)

    def rotation(n, first, block, half):
        r = np.zeros((P, P), np.float32)
        for b in range(first, n, block):
            for d in range(half):
                r[b + d + half, b + d] = -1.0
                r[b + d, b + d + half] = 1.0
        return r
    rot = rotation(P, 0, HD, 8)
    rotm = rotation(DQK, NOPE, P, 16)
    mats = np.concatenate([ident, ones, -ones, ntri, before, rot, rotm], axis=1)
    da = np.zeros((P, S), np.float32)
    da[0:64, S - 64:] = BIG_NEG
    x = np.arange(S + 384)[None, :] - 384 - i[:, None]
    n = ((np.abs(x) <= 64).astype(int) + ((x % 4 == 0) & (np.abs(x) <= 256))
         + (x % 16 == 0))
    lnc = np.where(n > 0, np.log(np.maximum(n, 1)), BIG_NEG).astype(np.float32)
    inv1 = (np.float32(500000.0) ** (-np.arange(0, 16, 2, dtype=np.float32) / np.float32(16))).astype(np.float32)
    inv2 = (np.float32(1) / np.float32(500000.0) ** (np.arange(8, dtype=np.float32) / np.float32(8))).astype(np.float32)
    inv3 = (np.float32(1) / np.float32(10000.0) ** (np.arange(16, dtype=np.float32) / np.float32(16))).astype(np.float32)
    freq = np.zeros((P, 3), np.float32)
    for b in (0, 64):
        for h in (0, 8):
            freq[b + h:b + h + 8, 0] = inv1
            freq[b + h:b + h + 8, 1] = inv2
    freq[64:80, 2] = inv3
    freq[80:96, 2] = inv3
    rev = np.zeros((P, NG + NE), np.float32)
    rev[:, :NG] = NG - np.arange(NG)
    rev[:, NG:] = NE - np.arange(NE)
    blk = np.arange(NB, dtype=np.float32)[None, :]
    eps = np.tile(np.array([EPS, math.pi / 2], np.float32), (P, 1))
    tok = (np.arange(TT, dtype=np.int32)[None, :] * P + i[:, None]).astype(np.int32)
    return {"c_mats": mats, "c_da": da, "c_lnc": lnc, "c_freq": freq, "c_rev": rev, "c_blk": blk, "c_eps": eps, "c_tok": tok}


def build_program(nc, A, out):
    with ExitStack() as ctx:
        def sb(name, shape, dt=F32):
            return ctx.enter_context(nc.sbuf_tensor(name, shape, dt))

        XT = sb("XT", [P, KD, S])
        HT = sb("HT", [P, KD, S])
        ring = sb("ring", [P, RING, UNIT])
        BIG = sb("BIG", [P, 24, S])
        G = sb("G", [P, 16, S])
        ATT = sb("ATT", [P, 14 * S])
        MATS = sb("MATS", [P, 7 * P])
        DAM = sb("DAM", [P, S])
        COS = sb("COS", [P, S])
        SIN = sb("SIN", [P, S])
        RSTD = sb("RSTD", [P, S])
        TMP = sb("TMP", [P, 2, S])
        GC = sb("GC", [P, NGC])
        FREQ = sb("FREQ", [P, 3])
        WR = sb("WR", [P, LAYERS, KD, NG + NE])
        BR = sb("BR", [P, LAYERS, NG + NE])
        LAM = sb("LAM", [P, 8])
        SM = sb("SM", [P, 16])
        NBG = sb("NBG", [P, 16])
        IDENT, ONES, NONES, NTRI, BEFORE, ROT, ROTM = (MATS[:, i * P:(i + 1) * P] for i in range(7))
        PS = ctx.enter_context(nc.psum_tensor("PS", [P, 8, 512], F32))
        PSF = PS[:, :, :].rearrange("p b n -> p (b n)")

        SBQ, SBK, SBV = (BIG[:, 4 * i:4 * i + 4, :] for i in range(3))
        DAQ, DAK, DAV = (BIG[:, 12 + 4 * i:16 + 4 * i, :] for i in range(3))
        KT, VA, MB = BIG[:, 0:8, :], BIG[:, 8:12, :], BIG[:, 0:8, :]
        DQ, DK, DV = (BIG[:, 12 + 4 * i:16 + 4 * i, :] for i in range(3))
        A3 = ATT[:, :].rearrange("p (a b) -> p a b", b=S)
        CQ, CKV, KR, COSM, SINM = A3[:, 3:6, :], A3[:, 6:8, :], A3[0:DQK, 8, :], A3[:, 9, :], A3[:, 10, :]
        E_ = ATT[:, 8 * S:12 * S]
        TOEP = ATT[:, 12 * S:12 * S + S + 384]
        SQ = ATT[:, 0:2 * S].rearrange("p (a b) -> p a b", a=2)
        ACC = ATT[:, 2 * S:3 * S]
        BIGF = BIG[:, :, :].rearrange("p a b -> p (a b)")
        GF = G[:, :, :].rearrange("p a b -> p (a b)")

        HDR = nc.dram_tensor("h_tokens", (S, D), F32, kind="Internal").ap()
        YDR = nc.dram_tensor("expert_rows", (NB * CAP, D), F32, kind="Internal").ap()
        SLOTS = nc.dram_tensor("slot_tokens", (NBP * CAP, 1), I32, kind="Internal").ap()

        names = ("const_landed lin_ready lin_free gate_ready gate_free sq_ready sq_used rstd_ready h_ready "
                 "dve_step act_step pool_step z_ready soft_ready sp_ready sp_masked suffix_ready lw_ready "
                 "w_ready w_masked pv_even sc_ready mx_ready e_ready p_ready tr_ready tr_done raw_ready "
                 "sub_sq sub_rs sub_ready x_ready lg_ready lg_free route_exp rank_ready cnt_ready mask_ready "
                 "slots_ready tok_scattered h_stored idx_landed idx_ready x_gather0 x_gather1 x_turned x_copied "
                 "gu_ready e_gate hid_ready hid_turned hidT_ready dn_ready y_ready y_store0 y_store1 y_gathered "
                 "comb_ready blk_ready table_landed stored_out ang_ready trig_ready kr_ready kr_copied pl_landed "
                 "toep_landed pos_landed pos2_landed lam_exp zero_ready zero_stored").split()
        Q = {n: ctx.enter_context(nc.semaphore(n)) for n in names}
        w_landed = [ctx.enter_context(nc.semaphore(f"w_landed{i}")) for i in range(RING)]
        block = ctx.enter_context(nc.Block())

        class Ring:

            def __init__(self):
                self.place, self.fills = 0, [0] * RING

            def next(self):
                p = self.place
                self.fills[p] += 1
                self.place = (p + 1) % RING
                return p, self.fills[p]

            def align(self):
                while self.place % 3:
                    self.place = (self.place + 1) % RING

            def blocks(self):
                p, before = self.place, list(self.fills)
                for b in range(NB):
                    for j in range(3):
                        self.fills[(p + 3 * b + j) % RING] += 1
                self.place = (p + 3 * NB) % RING
                return p, before

        class Counts:

            def __init__(self):
                self.n, self.last = {"const_landed": N_CONST}, "const_landed"

            def count(self, name):
                return self.n.get(name, 0)

            def inc(self, name):
                self.n[name] = self.count(name) + 1
                self.last = name
                return 1

            def next(self, name, k=1):
                self.n[name] = self.count(name) + k
                return self.n[name]

            def prev(self):
                return Q[self.last], self.n[self.last]

            def skip(self, name, k=1):
                self.n[name] = self.count(name) + k

            def enter(self, i, per):
                self.saved, self.per = dict(self.n), per
                for k, d in per.items():
                    self.n[k] = i * d + self.count(k)

            def leave(self, turns):
                for k, d in self.per.items():
                    self.n[k] = self.saved.get(k, 0) + turns * d

        used = {}
        at = {}

        RT = {}
        _o = 0
        for _n, _w in (("mask", 128), ("logit", 144), ("gmax", 4), ("ge", 20), ("gsum", 4), ("eq", 16), ("pen", 16),
                       ("one1", 128), ("one2", 128), ("tmp", 128), ("m1", 4), ("m2", 4), ("s4", 4), ("rank", 128),
                       ("cnt", 32), ("nblk", 32), ("end", 32), ("over", 128), ("gate", 8), ("sum8", 8), ("adr", 8),
                       ("sloti", 8), ("adri", 8), ("idx", NBP), ("blkf", NB), ("blki", NB), ("one32", 32),
                       ("cmp", NB * NE)):
            RT[_n] = ATT[:, _o:_o + _w]
            _o += _w
        assert _o <= 14 * S
        TOK = ctx.enter_context(nc.sbuf_tensor("TOK", [P, TT], I32))
        XG = BIGF[:, 0:2 * D].rearrange("p (a d) -> p a d", a=2)
        XGT = BIGF[:, 2 * D:4 * D].rearrange("p (a n) -> p a n", a=2)
        YB = BIGF[:, 4 * D:6 * D].rearrange("p (a n) -> p a n", a=2)
        HID = BIGF[:, 6 * D:6 * D + 512].rearrange("p (a n) -> p a n", a=2)
        HIDT = BIGF[:, 6 * D + 512:7 * D].rearrange("p (a n) -> p a n", a=2)
        COMB = BIGF[:, 8 * D:12 * D].rearrange("p (t d) -> p t d", t=TT)
        HTOK = GF[:, 0:4 * D].rearrange("p (t d) -> p t d", t=TT)
        YG = GF[:, :].rearrange("p (j d) -> p j d", j=2 * TT)
        PLT = BIGF[:, 0:2 * S].rearrange("p (k t) -> p k t", k=2)
        REV = sb("REV", [P, NG + NE])
        BLK = sb("BLK", [1, NB])
        EPS_C = sb("EPS_C", [P, 2])

        @block.tensor
        def _(pe):
            now = Counts()
            st = {}
            plan = Ring()

            def unit():
                st["unit"] = plan.next()
                place, fill = st["unit"]
                pe.wait_ge(w_landed[place], 16 * fill)
                return ring[:, place, :]

            def unit_used(name, unit=None):
                used[unit or st["unit"]] = (name, now.count(name))

            def lin_open():
                t = now.count("lin_ready")
                if t >= 2:
                    pe.wait_ge(Q["lin_free"], t - 1)
                return PS[:, t % 2, :]

            def gate_open():
                t = now.count("gate_ready")
                if t >= 2:
                    pe.wait_ge(Q["gate_free"], t - 1)
                return PS[:, 2 + t % 2, :]

            opened = {"lin_ready": lin_open, "gate_ready": gate_open}

            def drained(name):
                pe.wait_ge(Q[{"lin_ready": "lin_free", "gate_ready": "gate_free"}[name]], now.count(name))

            def norm_sum(nt):
                ps = gate_open()
                pe.wait_ge(Q["sq_used"], now.next("sq_used", nt))
                pe.matmul(ps, ONES, ATT[:, 2 * S:3 * S], start=True, stop=True)\
                    .then_inc(Q["gate_ready"], now.inc("gate_ready"))

            def project(w, nk, width, rhs, ring_name, m=P, h_wait=False):
                wv = w[:, 0:nk * width].rearrange("p (k c) -> p k c", k=nk)
                for c in range(0, width, m):
                    ps = opened[ring_name]()
                    for k in range(nk):
                        if h_wait and c == 0:
                            pe.wait_ge(Q["h_ready"], now.next("h_ready"))
                        mm = pe.matmul(ps[0:m, :], wv[:, k, c:c + m], rhs[:, k, :], start=k == 0, stop=k == nk - 1)
                    mm.then_inc(Q[ring_name], now.inc(ring_name))
                unit_used(ring_name)

            def project_tokens(w, nk, width, lhs):
                wv = w[:, 0:nk * width].rearrange("p (k c) -> p k c", k=nk)
                for t in range(TT):
                    ps = lin_open()
                    for k in range(nk):
                        mm = pe.matmul(ps[:, 0:width], lhs[:, k, t * P:(t + 1) * P], wv[:, k, :],
                                       start=k == 0, stop=k == nk - 1)
                    mm.then_inc(Q["lin_ready"], now.inc("lin_ready"))
                unit_used("lin_ready")

            def rotate(tiles, mat, rows=P):
                for t in tiles:
                    ps = lin_open()
                    pe.matmul(ps[0:rows, :], mat[0:rows, 0:rows], t, start=True, stop=True)\
                        .then_inc(Q["lin_ready"], now.inc("lin_ready"))

            def stick_breaking():
                at[f"sb{L}"] = now.count("lin_ready")

                def z_bank(h):
                    return (2 + 3 * (h % 2)) * 512

                def off(kb, qb):
                    d = qb - kb
                    return (kb * P, 512 + kb * P, 1024 + kb * P, 896)[d]
                blocks = [(kb, kb + d) for d in (0, 1, 3, 2) for kb in range(4 - d)]

                def logits(h):
                    r = slice(64 * (h % 2), 64 * (h % 2) + 64)
                    if h >= 2:
                        pe.wait_ge(Q["w_ready"], base_w + h - 1)
                    for kb, qb in blocks:
                        o = off(kb, qb)
                        mm = pe.matmul(PSF[:, z_bank(h) + o:z_bank(h) + o + P],
                                       SBK[r, h // 2, kb * P:(kb + 1) * P], SBQ[r, h // 2, qb * P:(qb + 1) * P],
                                       start=o % 512 == 0, stop=False, skip_group_check=True)
                    mm.then_inc(Q["z_ready"], now.inc("z_ready"))

                def log_weights(h):
                    z = z_bank(h)
                    sp = ATT[:, (1280 * (1 + h % 2)):(1280 * (2 + h % 2))]
                    rd = ATT[:, 6400:6784]
                    pe.wait_ge(Q["suffix_ready"], now.next("suffix_ready"))
                    for a, b in ((0, 512), (512, 1024), (1024, 1280)):
                        pe.matmul(PSF[:, z + a:z + b], NTRI, sp[:, a:b], start=False, stop=False, skip_group_check=True)
                    for a, b, src in ((512, 896, sp[:, P:512]), (896, 1024, rd[:, 256:384]), (1024, 1280, rd[:, 0:256])):
                        mm = pe.matmul(PSF[:, z + a:z + b], NONES, src, start=False, stop=True, skip_group_check=True)
                    mm.then_inc(Q["lw_ready"], now.inc("lw_ready"))

                def values(h):
                    r = slice(64 * (h % 2), 64 * (h % 2) + 64)
                    w = ATT[:, (1280 * (3 + h % 2)):(1280 * (4 + h % 2))]
                    if h % 2 == 0:
                        st["o"] = lin_open()
                    pe.wait_ge(Q["w_masked"], now.next("w_masked"))
                    first = True
                    for kb in range(TT):
                        for qb in range(kb, TT):
                            mm = pe.matmul(st["o"][r, qb * P:(qb + 1) * P], SBV[:, kb, h * HD:(h + 1) * HD],
                                           w[:, off(kb, qb):off(kb, qb) + P], start=first,
                                           stop=kb == qb, skip_group_check=True)
                            first = False
                    mm\
                        .then_inc(Q["pv_even" if h % 2 == 0 else "lin_ready"], now.inc("pv_even" if h % 2 == 0 else "lin_ready"))

                base_w = now.count("w_ready")
                drained("gate_ready")
                drained("lin_ready")
                logits(0)
                for h in range(SB_H):
                    if h + 1 < SB_H:
                        logits(h + 1)
                    log_weights(h)
                    if h >= 1:
                        values(h - 1)
                values(SB_H - 1)
                now.skip("w_ready", SB_H)

            def attention(heads, score, nkeys, ahead, maps, values, taken):
                jobs = [(h, qb) for h in range(heads) for qb in range(TT)]
                base = {k: now.count(k) for k in ("mx_ready", "e_ready", "tr_done", "p_ready")}

                def scores(u):
                    slots = 4 // maps
                    if u >= slots:
                        pe.wait_ge(Q[taken], base[taken] + u - slots + 1)
                    h, qb = jobs[u]
                    for m in range(maps):
                        b = 4 + (u % slots) * maps + m
                        mm = score(PS[:, b, 0:nkeys(qb)], h, m, qb)
                    mm.then_inc(Q["sc_ready"], now.inc("sc_ready"))

                def turn(u):
                    h, qb = jobs[u]
                    if u >= 2:
                        pe.wait_ge(Q["tr_done"], base["tr_done"] + u - 1)
                    pe.wait_ge(Q["p_ready"], now.next("p_ready"))
                    for kb in range(nkeys(qb) // P):
                        mm = pe.transpose(PS[:, 2 + u % 2, kb * P:(kb + 1) * P],
                                          E_[:, (u % 2) * maps * S + kb * P:(u % 2) * maps * S + (kb + 1) * P], IDENT)
                    mm.then_inc(Q["tr_ready"], now.inc("tr_ready"))

                def head_values(h):
                    pe.wait_ge(Q["tr_done"], base["tr_done"] + TT * (h + 1))
                    values(h, ATT[:, (h % 2) * 4 * S:(h % 2 + 1) * 4 * S].rearrange("p (k q) -> p k q", k=TT))

                drained("gate_ready")
                drained("lin_ready")
                for u in range(ahead):
                    scores(u)
                for u in range(len(jobs)):
                    if u + ahead < len(jobs):
                        scores(u + ahead)
                    turn(u)
                    if u % TT == 1 and u > TT:
                        head_values(u // TT - 1)
                head_values(heads - 1)
                now.skip("tr_done", len(jobs))
                now.skip("mx_ready", len(jobs))
                now.skip("e_ready", len(jobs))

            def pair_values(v):
                def run(h, pt):
                    r = slice(64 * (h % 2), 64 * (h % 2) + 64)
                    if h % 2 == 0:
                        st["o"] = lin_open()
                    for kb in range(TT):
                        mm = pe.matmul(st["o"][r, :], v[:, kb, h * HD:(h + 1) * HD], pt[:, kb, :],
                                       start=kb == 0, stop=kb == TT - 1, skip_group_check=True)
                    mm\
                        .then_inc(Q["pv_even" if h % 2 == 0 else "lin_ready"], now.inc("pv_even" if h % 2 == 0 else "lin_ready"))
                return run

            def differential():
                def score(o, h, m, qb):
                    r = slice(64 * m, 64 * m + 64)
                    return pe.matmul(o, DAQ[r, h, qb * P:(qb + 1) * P], DAK[r, h, 0:(qb + 1) * P],
                                     start=True, stop=True)

                def values(h, pt):
                    ps = lin_open()
                    for kb in range(TT):
                        mm = pe.matmul(ps[:, kb * P:S], DAV[:, kb, h * P:(h + 1) * P], pt[:, kb, kb * P:S],
                                       start=kb == 0, stop=kb == TT - 1, skip_group_check=True)
                    mm.then_inc(Q["lin_ready"], now.inc("lin_ready"))
                attention(DA_H, score, lambda qb: (qb + 1) * P, 1, 2, values, "mx_ready")
                for h in range(DA_H):
                    ps = gate_open()
                    pe.wait_ge(Q["sub_sq"], now.next("sub_sq"))
                    pe.matmul(ps, ONES, ATT[:, h * S:(h + 1) * S], start=True, stop=True)\
                        .then_inc(Q["gate_ready"], now.inc("gate_ready"))

            def branch(src):
                for _ in range(2):
                    project(unit(), 4, 512, src, "lin_ready")

            def moe(L):
                for t in range(TT):
                    for k in range(KD):
                        if t == 0:
                            pe.wait_ge(Q["h_ready"], now.next("h_ready"))
                        mm = pe.matmul(PS[:, 4, t * (NG + NE):(t + 1) * (NG + NE)], HT[:, k, t * P:(t + 1) * P],
                                       WR[:, L, k, :], start=(k == 0 and t == 0), stop=k == KD - 1,
                                       skip_group_check=True)
                mm.then_inc(Q["lg_ready"], now.inc("lg_ready"))
                for t in range(TT):
                    for f in range(0, KD, 4):
                        ps = lin_open()
                        for j in range(4):
                            mm = pe.transpose(ps[:, j * P:(j + 1) * P], HT[:, f + j, t * P:(t + 1) * P], IDENT)
                        mm.then_inc(Q["lin_ready"], now.inc("lin_ready"))
                pe.wait_ge(Q["mask_ready"], now.next("mask_ready"))
                M = ATT[:, 0:TT * NE].rearrange("p (t x) -> p t x", t=TT)
                first = True
                for t in range(TT):
                    for s in range(t + 1):
                        mm = pe.matmul(PS[:, 5, t * NE:(t + 1) * NE], BEFORE if s == t else ONES, M[:, s, :],
                                       start=first, stop=s == t, skip_group_check=True)
                        first = False
                for t in range(TT):
                    mm = pe.matmul(PS[:, 5, TT * NE:(TT + 1) * NE], ONES, M[:, t, :],
                                   start=False, stop=t == TT - 1, skip_group_check=True)
                mm.then_inc(Q["rank_ready"], now.inc("rank_ready"))
                drained("lin_ready")
                drained("gate_ready")

                plan.align()
                p0, before = plan.blocks()

                def landed(i, par, j):
                    place = (p0 + 3 * par + j) % RING
                    pe.wait_ge(w_landed[place], i * 16 + 16 * (before[place] + 1))
                    return ring[:, place, :]

                def turn_x(par):
                    g = f"x_gather{par}"
                    pe.wait_ge(Q[g], now.next(g, 16))
                    for k in range(KD):
                        mm = pe.transpose(PSF[:, 1024 + k * P:1024 + (k + 1) * P], XG[:, par, k * P:(k + 1) * P], IDENT)
                    mm.then_inc(Q["x_turned"], now.inc("x_turned"))

                def gate_up(i, par):
                    pe.wait_ge(Q["x_copied"], now.next("x_copied"))
                    landed(i, par, 0)
                    landed(i, par, 1)
                    s = (p0 + 3 * par) % RING
                    for k in range(KD):
                        w = ring[:, s:s + 2, k * EH:(k + 1) * EH]
                        mm = pe.matmul(PS[:, 4 + par, :], XGT[:, par, k * P:(k + 1) * P], w, start=k == 0, stop=k == KD - 1)
                    mm.then_inc(Q["gu_ready"], now.inc("gu_ready"))

                def turn_hidden(par):
                    pe.wait_ge(Q["hid_ready"], now.next("hid_ready"))
                    for j in range(2):
                        mm = pe.transpose(PS[:, 6, j * P:(j + 1) * P], HID[:, par, j * P:(j + 1) * P], IDENT)
                    mm.then_inc(Q["hid_turned"], now.inc("hid_turned"))

                def down(i, par, first=False):
                    w = landed(i, par, 2)
                    pe.wait_ge(Q["hidT_ready"], now.next("hidT_ready"))
                    if not first:
                        pe.wait_ge(Q["y_ready"], now.next("y_ready"))
                    for n in range(2):
                        for j in range(2):
                            mm = pe.matmul(PS[:, n, :], HIDT[:, par, j * P:(j + 1) * P],
                                           w[:, j * D + n * 512:j * D + (n + 1) * 512], start=j == 0, stop=j == 1)
                    mm.then_inc(Q["dn_ready"], now.inc("dn_ready"))

                for par in range(2):
                    for j in range(3):
                        place = (p0 + 3 * par + j) % RING
                        name = "dn_ready" if j == 2 else "gu_ready"
                        used[(place, plan.fills[place])] = (name, now.count(name) + NB - par)
                at[f"moe{L}"] = {n: now.count(n) for n in ("gu_ready", "dn_ready", "x_turned")}
                turn_x(0)
                gate_up(0, 0)
                turn_x(1)
                turn_hidden(0)
                gate_up(0, 1)
                down(0, 0, first=True)
                turn_x(0)
                turn_hidden(1)
                gate_up(1, 0)
                down(0, 1)
                turn_x(1)
                per = dict(x_gather0=16, x_gather1=16, x_turned=2, x_copied=2, gu_ready=2, hid_ready=2,
                           hid_turned=2, hidT_ready=2, dn_ready=2, y_ready=2)
                turns = (NB - 3) // 2
                with pe.Fori(0, turns) as i:
                    now.enter(i, per)
                    turn_hidden(0)
                    gate_up(i + 1, 1)
                    down(i + 1, 0)
                    turn_x(0)
                    turn_hidden(1)
                    gate_up(i + 2, 0)
                    down(i + 1, 1)
                    turn_x(1)
                now.leave(turns)
                turn_hidden(0)
                down((NB - 1) // 2, 0)
                pe.wait_ge(Q["y_ready"], now.next("y_ready"))
                pe.wait_ge(Q["x_copied"], now.next("x_copied"))
                pe.wait_ge(Q["comb_ready"], now.next("comb_ready", TT))
                for f in range(KD):
                    ps = lin_open()
                    for t in range(TT):
                        mm = pe.transpose(ps[:, t * P:(t + 1) * P], COMB[:, t, f * P:(f + 1) * P], IDENT)
                    mm.then_inc(Q["lin_ready"], now.inc("lin_ready"))

            def ffn():
                norm_sum(KD)
                at[f"ffn{st.setdefault('ffn', 0)}"] = now.count("lin_ready")
                st["ffn"] += 1
                for c in range(KF // 2):
                    for j in range(2):
                        w = unit()
                        wv = w.rearrange("p (k c) -> p k c", k=KD)
                        for m in range(2):
                            name = ("gate_ready", "lin_ready")[j]
                            ps = opened[name]()
                            for k in range(KD):
                                if c == 0 and j == 0 and m == 0:
                                    pe.wait_ge(Q["h_ready"], now.next("h_ready"))
                                mm = pe.matmul(ps, wv[:, k, m * P:(m + 1) * P], HT[:, k, :],
                                               start=k == 0, stop=k == KD - 1)
                            mm.then_inc(Q[name], now.inc(name))
                        unit_used(name)
                drained("lin_ready")
                for c in range(4):
                    tiles, units = [], []
                    for q in range(3):
                        w = unit()
                        units.append(st["unit"])
                        nk = min(KD, KF - q * KD)
                        wv = w[:, 0:nk * 256].rearrange("p (k c) -> p k c", k=nk)
                        for m in range(2):
                            if q == 0:
                                t = now.count("lin_ready") + m
                                if t >= 2:
                                    pe.wait_ge(Q["lin_free"], t - 1)
                                tiles.append(PS[:, t % 2, :])
                            for k in range(nk):
                                mm = pe.matmul(tiles[m], wv[:, k, m * P:(m + 1) * P], BIG[:, q * KD + k, :],
                                               start=(q == 0 and k == 0), stop=(q == 2 and k == nk - 1),
                                               skip_group_check=True)
                            if q == 2:
                                mm.then_inc(Q["lin_ready"], now.inc("lin_ready"))
                    for x in units:
                        unit_used("lin_ready", x)
                norm_sum(KD)

            pe.wait_ge(Q["const_landed"], N_CONST)
            for L in range(LAYERS):
                norm_sum(KD)
                for n in range(4):
                    project(unit(), KD, 256, HT, "lin_ready", h_wait=n == 0)
                for n in range(2):
                    project_tokens(unit(), KD, 256, HT)
                for n in range(4):
                    project(unit(), KD, 256, HT, "lin_ready")
                qk = now.count("lin_ready")
                for n in range(2):
                    project_tokens(unit(), KD, 256, HT)
                pe.wait_ge(Q["lin_free"], qk)
                rotate([DAQ[:, t, :] for t in range(4)] + [DAK[:, t, :] for t in range(4)], ROT)
                for n in range(8):
                    project(unit(), KD, 256, HT, "gate_ready")
                stick_breaking()
                differential()
                drained("lin_ready")
                branch(SBQ)
                pe.wait_ge(Q["sub_ready"], now.next("sub_ready", DA_H))
                branch(DAQ)
                drained("lin_ready")
                for n in range(4):
                    project(unit(), KD, 256, HT, "lin_ready")
                norm_sum(KD)
                moe(L)
                norm_sum(KD)
                for n in range(4):
                    project(unit(), KD, 256, HT, "gate_ready", h_wait=n == 0)
                pe.wait_ge(Q["pl_landed"], now.next("pl_landed", 16))
                project(unit(), 2, 1024, PLT, "lin_ready")
            norm_sum(KD)
            ffn()
            norm_sum(KD)
            project(unit(), KD, 256, HT, "lin_ready", h_wait=True)
            project(unit(), KD, 128, HT, "lin_ready")
            project(unit(), KD, 256, HT, "lin_ready")
            project(unit(), KD, 96, HT, "lin_ready", m=96)
            for n in range(4):
                project(unit(), KD, 256, HT, "lin_ready")
            qk = now.count("lin_ready")
            for n in range(2):
                project_tokens(unit(), KD, 256, HT)
            pe.wait_ge(Q["lin_free"], qk)
            rotate([DQ[:, t, :] for t in range(4)] + [DK[:, t, :] for t in range(4)], ROT)
            rotate([KR], ROTM, DQK)
            for n in range(8):
                project(unit(), KD, 256, HT, "gate_ready")
            norm_sum(QR // P)
            norm_sum(KVR // P)
            pe.wait_ge(Q["h_ready"], now.next("h_ready", (QR + KVR) // P))
            for n in range(2):
                project(unit(), 3, 384, CQ, "lin_ready", m=96)
            drained("lin_ready")
            rotate([HT[0:DQK, h, :] for h in range(MLA_H)], ROTM, DQK)
            project(unit(), 2, 512, CKV, "lin_ready")
            project_tokens(unit(), 2, 512, CKV)
            pe.wait_ge(Q["kr_copied"], now.next("kr_copied", MLA_H))

            def mla_score(o, h, m, qb):
                return pe.matmul(o, HT[0:DQK, h, qb * P:(qb + 1) * P], KT[0:DQK, h, :], start=True, stop=True)

            def dil_score(o, h, m, qb):
                r = slice(64 * (h % 2), 64 * (h % 2) + 64)
                return pe.matmul(o, DQ[r, h // 2, qb * P:(qb + 1) * P], DK[r, h // 2, :], start=True, stop=True)
            at["pairs0"] = now.count("lin_ready")
            at["pairs1"] = at["pairs0"] + MLA_H // 2
            attention(MLA_H, mla_score, lambda qb: S, 2, 1, pair_values(VA), "e_ready")
            attention(MLA_H, dil_score, lambda qb: S, 2, 1, pair_values(DV), "mx_ready")
            drained("lin_ready")
            branch(HT[:, 0:4, :])
            branch(DQ)
            drained("lin_ready")
            for n in range(4):
                project(unit(), KD, 256, MB, "lin_ready")
            norm_sum(KD)
            ffn()
            at["pe"] = dict(now.n)

        @block.vector
        def _(v):
            now = Counts()
            st = {"norm": 0}

            def lin_take():
                t = now.count("lin_ready")
                v.wait_ge(Q["lin_ready"], now.next("lin_ready"))
                return PS[:, t % 2, :]

            def gate_tile():
                t = now.count("gate_ready")
                v.wait_ge(Q["gate_ready"], now.next("gate_ready"))
                return PS[:, 2 + t % 2, :]

            def norm(src, nt, gain, source, dst=None, name="h_ready", add=None):
                at[f"norm{st['norm']}"] = (source, now.count(source) - nt)
                st["norm"] += 1
                for k in range(nt):
                    v.wait_ge(Q["sq_ready"], now.next("sq_ready"))
                    if k == 0:
                        v.wait_ge(*now.prev())
                        v.tensor_copy(ACC, SQ[:, 0, :]).then_inc(Q["sq_used"], now.inc("sq_used"))
                    else:
                        v.wait_ge(*now.prev())
                        v.tensor_tensor(ACC, ACC, SQ[:, k % 2, :], ALU.add).then_inc(Q["sq_used"], now.inc("sq_used"))
                now.skip("gate_ready")
                now.skip("gate_free")
                v.wait_ge(Q["rstd_ready"], now.next("rstd_ready"))
                for k in range(nt):
                    g = GC[:, GCOL[gain] + k:GCOL[gain] + k + 1]
                    if add is None:
                        v.wait_ge(*now.prev())
                        v.scalar_tensor_tensor(out=dst[:, k, :], in0=src[:, k, :], scalar=g, in1=RSTD[:, :],
                                               op0=ALU.mult, op1=ALU.mult)\
                            .then_inc(Q[name], now.inc(name))
                    else:
                        v.wait_ge(*now.prev())
                        v.scalar_tensor_tensor(out=TMP[:, 0, :], in0=src[:, k, :], scalar=g, in1=RSTD[:, :],
                                               op0=ALU.mult, op1=ALU.mult)\
                            .then_inc(Q["dve_step"], now.inc("dve_step"))
                        v.wait_ge(*now.prev())
                        v.scalar_tensor_tensor(out=XT[:, k, :], in0=TMP[:, 0, :], scalar=add, in1=XT[:, k, :],
                                               op0=ALU.mult, op1=ALU.add)\
                            .then_inc(Q["x_ready"], now.inc("x_ready"))

            def store(dst, n, rows=P, scale=None):
                for k in range(n):
                    ps = lin_take()
                    if scale is None:
                        v.wait_ge(*now.prev())
                        v.tensor_copy(dst[0:rows, k, :], ps[0:rows, :]).then_inc(Q["lin_free"], now.inc("lin_free"))
                    else:
                        v.wait_ge(*now.prev())
                        v.tensor_scalar(dst[0:rows, k, :], ps[0:rows, :], scale, None, ALU.mult)\
                            .then_inc(Q["lin_free"], now.inc("lin_free"))

            def store_tokens(dst, units, width):
                for n in range(units):
                    for t in range(TT):
                        ps = lin_take()
                        v.wait_ge(*now.prev())
                        v.tensor_copy(dst[:, t, n * width:(n + 1) * width], ps[:, 0:width])\
                            .then_inc(Q["lin_free"], now.inc("lin_free"))

            def rope(tiles, cos, sin, rows=P):
                for t in tiles:
                    ps = lin_take()
                    v.wait_ge(*now.prev())
                    v.tensor_tensor(TMP[0:rows, 0, :], ps[0:rows, :], sin[0:rows, :], ALU.mult)\
                        .then_inc(Q["dve_step"], now.inc("dve_step"))
                    v.wait_ge(*now.prev())
                    v.tensor_tensor(t, t, cos[0:rows, :], ALU.mult).then_inc(Q["dve_step"], now.inc("dve_step"))
                    v.wait_ge(*now.prev())
                    v.tensor_tensor(t, t, TMP[0:rows, 0, :], ALU.add).then_inc(Q["lin_free"], now.inc("lin_free"))

            def trig(cos, sin, col):
                two_pi = 2 * math.pi
                c1 = 6.28125
                c2 = float(np.float32(np.float32((two_pi - c1) * 2 ** 20).astype(np.int32) / 2 ** 20))
                c3 = two_pi - c1 - c2
                big = 12582912.0
                v.wait_ge(*now.prev())
                v.tensor_copy(cos, sin.bitcast(I32)).then_inc(Q["dve_step"], now.inc("dve_step"))
                v.wait_ge(*now.prev())
                v.tensor_scalar(TMP[:, 0, :], cos, FREQ[:, col:col + 1], None, ALU.mult)\
                    .then_inc(Q["dve_step"], now.inc("dve_step"))
                v.wait_ge(*now.prev())
                v.tensor_scalar(TMP[:, 1, :], TMP[:, 0, :], 1.0 / two_pi, None, ALU.mult)\
                    .then_inc(Q["dve_step"], now.inc("dve_step"))
                v.wait_ge(*now.prev())
                v.tensor_scalar(TMP[:, 1, :], TMP[:, 1, :], big, None, ALU.add)\
                    .then_inc(Q["dve_step"], now.inc("dve_step"))
                v.wait_ge(*now.prev())
                v.tensor_scalar(TMP[:, 1, :], TMP[:, 1, :], -big, None, ALU.add)\
                    .then_inc(Q["dve_step"], now.inc("dve_step"))
                for c in (c1, c2, c3):
                    v.wait_ge(*now.prev())
                    v.scalar_tensor_tensor(out=TMP[:, 0, :], in0=TMP[:, 1, :], scalar=-c, in1=TMP[:, 0, :],
                                           op0=ALU.mult, op1=ALU.add)\
                        .then_inc(Q["dve_step"], now.inc("dve_step"))
                v.wait_ge(*now.prev())
                v.tensor_scalar(TMP[:, 0, :], TMP[:, 0, :], 3.1415925, -3.1415925, ALU.min, ALU.max)\
                    .then_inc(Q["ang_ready"], now.inc("ang_ready"))
                v.wait_ge(Q["trig_ready"], now.next("trig_ready"))

            def sigmoid_tail(n):
                for k in range(n):
                    v.wait_ge(Q["gate_ready"], now.next("gate_ready"))
                    v.wait_ge(Q["gate_free"], now.next("gate_free"))
                    v.wait_ge(*now.prev())
                    v.tensor_scalar(G[:, k, :], G[:, k, :], 1.0, None, ALU.add)\
                        .then_inc(Q["dve_step"], now.inc("dve_step"))
                    v.wait_ge(*now.prev())
                    v.reciprocal(G[:, k, :], G[:, k, :]).then_inc(Q["dve_step"], now.inc("dve_step"))

            def branches(dst, between=lambda: None):
                for k in range(KD):
                    ps = lin_take()
                    v.wait_ge(*now.prev())
                    v.tensor_tensor(dst[:, k, :], ps, G[:, k, :], ALU.mult).then_inc(Q["lin_free"], now.inc("lin_free"))
                between()
                for k in range(KD):
                    ps = lin_take()
                    v.wait_ge(*now.prev())
                    v.tensor_tensor(TMP[:, 0, :], ps, G[:, KD + k, :], ALU.mult)\
                        .then_inc(Q["dve_step"], now.inc("dve_step"))
                    v.wait_ge(*now.prev())
                    v.tensor_tensor(dst[:, k, :], dst[:, k, :], TMP[:, 0, :], ALU.add)\
                        .then_inc(Q["lin_free"], now.inc("lin_free"))

            def add_to_x():
                for k in range(KD):
                    ps = lin_take()
                    v.wait_ge(*now.prev())
                    v.tensor_tensor(XT[:, k, :], ps, XT[:, k, :], ALU.add).then_inc(Q["lin_free"], now.inc("lin_free"))

            def stick_breaking():
                base = now.count("lw_ready")
                at_sp = now.count("sp_masked")

                def softplus(h):
                    z = (2 + 3 * (h % 2)) * 512
                    v.wait_ge(Q["z_ready"], now.next("z_ready"))
                    v.wait_ge(Q["soft_ready"], now.next("soft_ready"))
                    if h >= 2:
                        v.wait_ge(Q["lw_ready"], base + h - 1)
                    sp = ATT[:, (1280 * (1 + h % 2)):(1280 * (2 + h % 2))]
                    v.wait_ge(*now.prev())
                    v.scalar_tensor_tensor(out=sp, in0=PSF[:, z:z + 1280], scalar=0.0, in1=ATT[:, 0:1280],
                                           op0=ALU.max, op1=ALU.add)\
                        .then_inc(Q["sp_ready"], now.inc("sp_ready"))

                def suffix(h):
                    sp = ATT[:, (1280 * (1 + h % 2)):(1280 * (2 + h % 2))]
                    rd = ATT[:, 6400:6784]
                    v.wait_ge(Q["sp_masked"], now.next("sp_masked"))
                    if h >= 1:
                        v.wait_ge(Q["lw_ready"], base + h)
                    v.wait_ge(*now.prev())
                    v.tensor_tensor(rd[:, 0:256], sp[:, 640:896], sp[:, 256:512], ALU.add)\
                        .then_inc(Q["dve_step"], now.inc("dve_step"))
                    v.wait_ge(*now.prev())
                    v.tensor_tensor(rd[:, 256:384], sp[:, 1152:1280], rd[:, 128:256], ALU.add)\
                        .then_inc(Q["suffix_ready"], now.inc("suffix_ready"))

                def take_pair(h):
                    if h % 2:
                        ps = lin_take()
                        v.wait_ge(*now.prev())
                        v.tensor_copy(SBQ[:, h // 2, :], ps).then_inc(Q["lin_free"], now.inc("lin_free"))

                softplus(0)
                suffix(0)
                for h in range(SB_H):
                    if h + 1 < SB_H:
                        softplus(h + 1)
                        suffix(h + 1)
                    if h >= 1:
                        take_pair(h - 1)
                take_pair(SB_H - 1)
                now.skip("lw_ready", SB_H)

            def attention(heads, nkeys, maps, scale, mask, L, head_done):
                jobs = [(h, qb) for h in range(heads) for qb in range(TT)]
                tr0 = now.count("tr_ready")
                slots = 4 // maps

                def maxima(u):
                    h, qb = jobs[u]
                    n = nkeys(qb)
                    s = SM[:, 8 * (u % 2):8 * (u % 2) + 8]
                    v.wait_ge(Q["sc_ready"], now.next("sc_ready"))
                    for m in range(maps):
                        ps = PS[:, 4 + (u % slots) * maps + m, 0:n]
                        if mask is None:
                            v.wait_ge(*now.prev())
                            v.tensor_reduce(s[:, m:m + 1], ps, AX, ALU.max).then_inc(Q["dve_step"], now.inc("dve_step"))
                        else:
                            if u >= 2:
                                v.wait_ge(Q["tr_ready"], tr0 + u - 1)
                            x = E_[:, ((u % 2) * maps + m) * S:((u % 2) * maps + m) * S + n]
                            v.wait_ge(*now.prev())
                            v.tensor_tensor_reduce(out=x, in0=ps, in1=mask(qb), scale=1.0, scalar=-3e38,
                                                   op0=ALU.add, op1=ALU.max, accum_out=s[:, m:m + 1])\
                                .then_inc(Q["dve_step"], now.inc("dve_step"))
                    v.wait_ge(*now.prev())
                    v.tensor_scalar(s[:, 0:maps], s[:, 0:maps], -scale, None, ALU.mult)\
                        .then_inc(Q["mx_ready"], now.inc("mx_ready"))

                def normalise(u):
                    h, qb = jobs[u]
                    n = nkeys(qb)
                    s = SM[:, 8 * (u % 2):8 * (u % 2) + 8]
                    x = [E_[:, ((u % 2) * maps + m) * S:((u % 2) * maps + m) * S + n] for m in range(maps)]
                    v.wait_ge(Q["e_ready"], now.next("e_ready"))
                    v.wait_ge(*now.prev())
                    v.reciprocal(s[:, 4:4 + maps], s[:, 2:2 + maps]).then_inc(Q["dve_step"], now.inc("dve_step"))
                    if maps == 1:
                        v.wait_ge(*now.prev())
                        v.tensor_scalar(x[0], x[0], s[:, 4:5], None, ALU.mult)\
                            .then_inc(Q["p_ready"], now.inc("p_ready"))
                    else:
                        v.wait_ge(*now.prev())
                        v.tensor_tensor(s[:, 5:6], s[:, 5:6], LAM[:, L:L + 1], ALU.mult)\
                            .then_inc(Q["dve_step"], now.inc("dve_step"))
                        v.wait_ge(*now.prev())
                        v.tensor_scalar(x[0], x[0], s[:, 4:5], None, ALU.mult)\
                            .then_inc(Q["dve_step"], now.inc("dve_step"))
                        v.wait_ge(*now.prev())
                        v.scalar_tensor_tensor(out=x[0], in0=x[1], scalar=s[:, 5:6], in1=x[0], op0=ALU.mult,
                                               op1=ALU.add)\
                            .then_inc(Q["p_ready"], now.inc("p_ready"))

                maxima(0)
                for u in range(len(jobs)):
                    if u + 1 < len(jobs):
                        maxima(u + 1)
                    normalise(u)
                    if u % TT == 2 and u > TT:
                        head_done(u // TT - 1)
                head_done(heads - 1)
                now.skip("tr_ready", len(jobs))

            def pair_done(dst):
                def run(h):
                    if h % 2:
                        ps = lin_take()
                        v.wait_ge(*now.prev())
                        v.tensor_copy(dst[:, h // 2, :], ps).then_inc(Q["lin_free"], now.inc("lin_free"))
                return run

            def moe(L):
                r = {k: a for k, a in RT.items()}
                v3 = lambda a, t: a.rearrange("p (t x) -> p t x", t=t)
                v.wait_ge(Q["lg_ready"], now.next("lg_ready"))
                lg = v3(r["logit"], TT)
                for t in range(TT):
                    v.wait_ge(*now.prev())
                    v.tensor_tensor(lg[:, t, :], PS[:, 4, t * (NG + NE):(t + 1) * (NG + NE)], BR[:, L, :], ALU.add)\
                        .then_inc(Q["dve_step"], now.inc("dve_step"))
                gl, el = lg[:, :, 0:NG], lg[:, :, NG:NG + NE]
                wide = lambda a, n: a.unsqueeze(2).to_broadcast([P, TT, n])
                v.wait_ge(*now.prev())
                v.tensor_reduce(r["gmax"], gl, AX, ALU.max).then_inc(Q["dve_step"], now.inc("dve_step"))
                v.wait_ge(*now.prev())
                v.tensor_tensor(v3(r["ge"][:, 0:16], TT), gl, wide(r["gmax"], NG), ALU.subtract)\
                    .then_inc(Q["dve_step"], now.inc("dve_step"))
                v.wait_ge(*now.prev())
                v.tensor_tensor(v3(r["eq"], TT), gl, wide(r["gmax"], NG), ALU.is_ge)\
                    .then_inc(Q["dve_step"], now.inc("dve_step"))
                v.wait_ge(*now.prev())
                v.tensor_tensor(v3(r["eq"], TT), v3(r["eq"], TT),
                                REV[:, 0:NG].unsqueeze(1).to_broadcast([P, TT, NG]), ALU.mult)\
                    .then_inc(Q["dve_step"], now.inc("dve_step"))
                v.wait_ge(*now.prev())
                v.tensor_reduce(r["s4"], v3(r["eq"], TT), AX, ALU.max).then_inc(Q["dve_step"], now.inc("dve_step"))
                v.wait_ge(*now.prev())
                v.tensor_tensor(v3(r["pen"], TT), v3(r["eq"], TT), wide(r["s4"], NG), ALU.is_ge)\
                    .then_inc(Q["dve_step"], now.inc("dve_step"))
                v.wait_ge(*now.prev())
                v.tensor_scalar(r["pen"], r["pen"], 1e30, -1e30, ALU.mult, ALU.add)\
                    .then_inc(Q["dve_step"], now.inc("dve_step"))
                for t in range(TT):
                    em = el[:, t, :].rearrange("p (g x) -> p g x", g=NG)
                    pen = v3(r["pen"], TT)[:, t, :]
                    v.wait_ge(*now.prev())
                    v.tensor_tensor(em, em, pen.unsqueeze(2).to_broadcast([P, NG, NEG_]), ALU.add)\
                        .then_inc(Q["dve_step"], now.inc("dve_step"))
                rev = REV[:, NG:NG + NE].unsqueeze(1).to_broadcast([P, TT, NE])
                for mx, one in (("m1", "one1"), ("m2", "one2")):
                    o = v3(r[one], TT)
                    v.wait_ge(*now.prev())
                    v.tensor_reduce(r[mx], el, AX, ALU.max).then_inc(Q["dve_step"], now.inc("dve_step"))
                    v.wait_ge(*now.prev())
                    v.tensor_tensor(o, el, wide(r[mx], NE), ALU.is_ge).then_inc(Q["dve_step"], now.inc("dve_step"))
                    v.wait_ge(*now.prev())
                    v.tensor_tensor(o, o, rev, ALU.mult).then_inc(Q["dve_step"], now.inc("dve_step"))
                    v.wait_ge(*now.prev())
                    v.tensor_reduce(r["s4"], o, AX, ALU.max).then_inc(Q["dve_step"], now.inc("dve_step"))
                    v.wait_ge(*now.prev())
                    v.tensor_tensor(o, o, wide(r["s4"], NE), ALU.is_ge).then_inc(Q["dve_step"], now.inc("dve_step"))
                    if one == "one1":
                        for t in range(TT):
                            v.wait_ge(*now.prev())
                            v.scalar_tensor_tensor(out=el[:, t, :], in0=o[:, t, :], scalar=-3e30, in1=el[:, t, :],
                                                   op0=ALU.mult, op1=ALU.add)\
                                .then_inc(Q["dve_step"], now.inc("dve_step"))
                v.wait_ge(*now.prev())
                v.tensor_tensor(r["mask"], r["one1"], r["one2"], ALU.add)\
                    .then_inc(Q["mask_ready"], now.inc("mask_ready"))
                v.wait_ge(*now.prev())
                v.tensor_tensor(r["ge"][:, 16:20], r["m2"], r["m1"], ALU.subtract)\
                    .then_inc(Q["route_exp"], now.inc("route_exp"))
                for t in range(TT):
                    for f in range(2):
                        ps = lin_take()
                        v.wait_ge(*now.prev())
                        v.tensor_copy(HTOK[:, t, f * 512:(f + 1) * 512], ps)\
                            .then_inc(Q["lin_free"], now.inc("lin_free"))
                at[f"htok{L}"] = now.count("lin_free")
                v.wait_ge(Q["table_landed"], now.next("table_landed"))
                v.wait_ge(*now.prev())
                v.tensor_reduce(r["gsum"], v3(r["ge"][:, 0:16], TT), AX, ALU.add)\
                    .then_inc(Q["dve_step"], now.inc("dve_step"))
                v.wait_ge(*now.prev())
                v.tensor_scalar(r["s4"], r["ge"][:, 16:20], 1.0, None, ALU.add)\
                    .then_inc(Q["dve_step"], now.inc("dve_step"))
                v.wait_ge(*now.prev())
                v.tensor_tensor(r["gsum"], r["gsum"], r["s4"], ALU.mult).then_inc(Q["dve_step"], now.inc("dve_step"))
                gate = r["gate"].rearrange("p (t c) -> p t c", c=2)
                v.wait_ge(*now.prev())
                v.reciprocal(gate[:, :, 0], r["gsum"]).then_inc(Q["dve_step"], now.inc("dve_step"))
                v.wait_ge(*now.prev())
                v.tensor_tensor(gate[:, :, 1], gate[:, :, 0], r["ge"][:, 16:20], ALU.mult)\
                    .then_inc(Q["dve_step"], now.inc("dve_step"))
                v.wait_ge(Q["rank_ready"], now.next("rank_ready"))
                v.wait_ge(*now.prev())
                v.tensor_copy(r["rank"], PS[:, 5, 0:TT * NE]).then_inc(Q["dve_step"], now.inc("dve_step"))
                v.wait_ge(*now.prev())
                v.tensor_copy(r["cnt"], PS[:, 5, TT * NE:(TT + 1) * NE]).then_inc(Q["dve_step"], now.inc("dve_step"))
                v.wait_ge(*now.prev())
                v.tensor_scalar(r["nblk"], r["cnt"], 0.5, None, ALU.is_gt).then_inc(Q["dve_step"], now.inc("dve_step"))
                for j in range(1, TT):
                    v.wait_ge(*now.prev())
                    v.scalar_tensor_tensor(out=r["nblk"], in0=r["cnt"], scalar=j * CAP + 0.5, in1=r["nblk"],
                                           op0=ALU.is_gt, op1=ALU.add)\
                        .then_inc(Q["dve_step"], now.inc("dve_step"))
                v.wait_ge(*now.prev())
                v.tensor_scalar(r["one32"], r["cnt"], 0.0, None, ALU.mult).then_inc(Q["dve_step"], now.inc("dve_step"))
                v.wait_ge(*now.prev())
                v.tensor_tensor_scan(r["end"], r["nblk"], r["one32"], 0.0, ALU.add, ALU.add)\
                    .then_inc(Q["dve_step"], now.inc("dve_step"))
                cmp = r["cmp"][0:1, :].rearrange("p (b x) -> p b x", b=NB)
                v.wait_ge(*now.prev())
                v.tensor_tensor(cmp, BLK[0:1, :].unsqueeze(2).to_broadcast([1, NB, NE]),
                                r["end"][0:1, :].unsqueeze(1).to_broadcast([1, NB, NE]), ALU.is_ge)\
                    .then_inc(Q["dve_step"], now.inc("dve_step"))
                v.wait_ge(*now.prev())
                v.tensor_reduce(r["blkf"][0:1, :], cmp, AX, ALU.add).then_inc(Q["dve_step"], now.inc("dve_step"))
                v.wait_ge(*now.prev())
                v.tensor_scalar(r["blkf"][0:1, :], r["blkf"][0:1, :], float(NE - 1), None, ALU.min)\
                    .then_inc(Q["dve_step"], now.inc("dve_step"))
                v.wait_ge(*now.prev())
                v.tensor_copy(r["blki"][0:1, :].bitcast(I32), r["blkf"][0:1, :])\
                    .then_inc(Q["blk_ready"], now.inc("blk_ready"))
                v.wait_ge(*now.prev())
                v.tensor_tensor(r["end"], r["end"], r["nblk"], ALU.subtract)\
                    .then_inc(Q["dve_step"], now.inc("dve_step"))
                rank, over = r["rank"], r["over"]
                v.wait_ge(*now.prev())
                v.tensor_scalar(over, rank, CAP - 0.5, None, ALU.is_gt).then_inc(Q["dve_step"], now.inc("dve_step"))
                for j in range(2, TT):
                    v.wait_ge(*now.prev())
                    v.scalar_tensor_tensor(out=over, in0=rank, scalar=j * CAP - 0.5, in1=over, op0=ALU.is_gt,
                                           op1=ALU.add)\
                        .then_inc(Q["dve_step"], now.inc("dve_step"))
                start = r["end"].unsqueeze(1).to_broadcast([P, TT, NE])
                v.wait_ge(*now.prev())
                v.tensor_scalar(over, over, float(1 - CAP * NBP), None, ALU.mult)\
                    .then_inc(Q["dve_step"], now.inc("dve_step"))
                v.wait_ge(*now.prev())
                v.scalar_tensor_tensor(out=over, in0=rank, scalar=float(NBP), in1=over, op0=ALU.mult, op1=ALU.add)\
                    .then_inc(Q["dve_step"], now.inc("dve_step"))
                v.wait_ge(*now.prev())
                v.tensor_tensor(v3(over, TT), v3(over, TT), start, ALU.add).then_inc(Q["dve_step"], now.inc("dve_step"))
                for t in range(TT):
                    v.wait_ge(*now.prev())
                    v.scalar_tensor_tensor(out=v3(rank, TT)[:, t, :], in0=r["end"], scalar=float(CAP),
                                           in1=v3(rank, TT)[:, t, :], op0=ALU.mult, op1=ALU.add)\
                        .then_inc(Q["dve_step"], now.inc("dve_step"))
                for val, dst, ints in ((rank, "sum8", "sloti"), (over, "adr", "adri")):
                    d = r[dst].rearrange("p (t c) -> p t c", c=2)
                    for c, one in enumerate(("one1", "one2")):
                        v.wait_ge(*now.prev())
                        v.tensor_tensor(r["tmp"], val, r[one], ALU.mult).then_inc(Q["dve_step"], now.inc("dve_step"))
                        v.wait_ge(*now.prev())
                        v.tensor_reduce(d[:, :, c], v3(r["tmp"], TT), AX, ALU.add)\
                            .then_inc(Q["dve_step"], now.inc("dve_step"))
                    v.wait_ge(*now.prev())
                    v.tensor_copy(r[ints].bitcast(I32), r[dst])\
                        .then_inc(Q["dve_step" if ints == "sloti" else "slots_ready"], now.inc("dve_step" if ints == "sloti" else "slots_ready"))

                y0 = [now.count("y_store0"), now.count("y_store1")]

                def turned_hidden(par):
                    v.wait_ge(Q["hid_turned"], now.next("hid_turned"))
                    v.wait_ge(*now.prev())
                    v.tensor_copy(HIDT[:, par, :], PS[:, 6, 0:256]).then_inc(Q["hidT_ready"], now.inc("hidT_ready"))

                def hidden(par):
                    v.wait_ge(Q["gu_ready"], now.next("gu_ready"))
                    v.wait_ge(Q["e_gate"], now.next("e_gate"))
                    h = HID[:, par, :]
                    v.wait_ge(*now.prev())
                    v.tensor_scalar(h, h, 1.0, None, ALU.add).then_inc(Q["dve_step"], now.inc("dve_step"))
                    v.wait_ge(*now.prev())
                    v.reciprocal(h, h).then_inc(Q["dve_step"], now.inc("dve_step"))
                    v.wait_ge(*now.prev())
                    v.tensor_tensor(h, PS[:, 4 + par, 0:EH], h, ALU.mult).then_inc(Q["dve_step"], now.inc("dve_step"))
                    v.wait_ge(*now.prev())
                    v.tensor_tensor(h, PS[:, 4 + par, EH:2 * EH], h, ALU.mult)\
                        .then_inc(Q["hid_ready"], now.inc("hid_ready"))

                def rows(par, before):
                    v.wait_ge(Q["dn_ready"], now.next("dn_ready"))
                    if before is not None:
                        v.wait_ge(Q[f"y_store{par}"], before * 16 + y0[par])
                    v.wait_ge(*now.prev())
                    v.tensor_copy(YB[:, par, :], PSF[:, 0:D]).then_inc(Q["y_ready"], now.inc("y_ready"))

                hidden(0)
                turned_hidden(0)
                hidden(1)
                rows(0, None)
                turned_hidden(1)
                hidden(0)
                rows(1, None)
                turns = (NB - 3) // 2
                with v.Fori(0, turns) as i:
                    now.enter(i, dict(hid_turned=2, hidT_ready=2, gu_ready=2, e_gate=2, hid_ready=2, dve_step=6,
                                    dn_ready=2, y_ready=2))
                    turned_hidden(0)
                    hidden(1)
                    rows(0, i + 1)
                    turned_hidden(1)
                    hidden(0)
                    rows(1, i + 1)
                now.leave(turns)
                turned_hidden(0)
                rows(0, (NB - 1) // 2)
                now.skip("y_store0", 16 * ((NB + 1) // 2))
                now.skip("y_store1", 16 * (NB // 2))
                v.wait_ge(Q["y_gathered"], now.next("y_gathered", 16 * 2 * TT))
                for t in range(TT):
                    v.wait_ge(*now.prev())
                    v.tensor_scalar(COMB[:, t, :], YG[:, 2 * t, :], r["gate"][:, 2 * t:2 * t + 1], None, ALU.mult)\
                        .then_inc(Q["dve_step"], now.inc("dve_step"))
                    v.wait_ge(*now.prev())
                    v.scalar_tensor_tensor(out=COMB[:, t, :], in0=YG[:, 2 * t + 1, :],
                                           scalar=r["gate"][:, 2 * t + 1:2 * t + 2], in1=COMB[:, t, :],
                                           op0=ALU.mult, op1=ALU.add)\
                        .then_inc(Q["comb_ready"], now.inc("comb_ready"))
                add_to_x()

            def ffn(pre, post, source):
                norm(XT, KD, pre, source, HT)
                for c in range(0, KF, 2):
                    for m in range(2):
                        k = c + m
                        a = A3[:, 3 + k % 2, :]
                        g = gate_tile()
                        v.wait_ge(Q["e_gate"], now.next("e_gate"))
                        v.wait_ge(*now.prev())
                        v.tensor_scalar(a, a, 1.0, None, ALU.add).then_inc(Q["dve_step"], now.inc("dve_step"))
                        v.wait_ge(*now.prev())
                        v.reciprocal(a, a).then_inc(Q["dve_step"], now.inc("dve_step"))
                        v.wait_ge(*now.prev())
                        v.tensor_tensor(a, g, a, ALU.mult).then_inc(Q["gate_free"], now.inc("gate_free"))
                        u = lin_take()
                        v.wait_ge(*now.prev())
                        v.tensor_tensor(BIG[:, k, :], u, a, ALU.mult).then_inc(Q["lin_free"], now.inc("lin_free"))
                store(G, KD)
                norm(G, KD, post, "lin_free", add=0.5)

            v.wait_ge(Q["const_landed"], N_CONST)
            LV = BIGF[:, 0:4 * LAYERS * HD].rearrange("p (n x) -> p n x", x=HD)
            for L in range(LAYERS):
                for j in range(2):
                    v.wait_ge(*now.prev())
                    v.tensor_tensor_reduce( out=TMP[:, 0, 0:HD], in0=LV[:, (2 * j) * LAYERS + L, :],
                                           in1=LV[:, (2 * j + 1) * LAYERS + L, :], scale=1.0, scalar=0.0,
                                           op0=ALU.mult, op1=ALU.add,
                                           accum_out=LAM[:, 4 + 2 * L + j:5 + 2 * L + j])\
                        .then_inc(Q["dve_step"], now.inc("dve_step"))
            v.wait_ge(*now.prev())
            v.tensor_scalar(LAM[:, 0:1], LAM[:, 4:5], 0.0, None, ALU.mult)\
                .then_inc(Q["pos_landed"], now.inc("pos_landed"))
            v.wait_ge(Q["lam_exp"], now.next("lam_exp"))
            for L in range(LAYERS):
                init = 0.8 - 0.6 * math.exp(-0.3 * L)
                v.wait_ge(*now.prev())
                v.tensor_tensor(LAM[:, L:L + 1], LAM[:, 5 + 2 * L:6 + 2 * L], LAM[:, 4 + 2 * L:5 + 2 * L],
                                ALU.subtract)\
                    .then_inc(Q["dve_step"], now.inc("dve_step"))
                v.wait_ge(*now.prev())
                v.tensor_scalar(LAM[:, L:L + 1], LAM[:, L:L + 1], -init, None, ALU.add)\
                    .then_inc(Q["dve_step"], now.inc("dve_step"))
                v.wait_ge(*now.prev())
                v.tensor_scalar(LAM[:, 2 + L:3 + L], GC[:, GCOL[f"g_subln{L}"]:GCOL[f"g_subln{L}"] + 1],
                                1.0 - init, None, ALU.mult)\
                    .then_inc(Q["dve_step"], now.inc("dve_step"))
            v.wait_ge(*now.prev())
            v.tensor_scalar(NBG[:, :], GC[:, GCOL["b_gate"]:GCOL["b_gate"] + 16], -1.0, None, ALU.mult)\
                .then_inc(Q["raw_ready"], now.inc("raw_ready"))
            trig(COS[:, :], SIN[:, :], 0)
            v.wait_ge(Q["zero_stored"], now.next("zero_stored", 16))

            for L in range(LAYERS):
                if L == 0:
                    now.skip("const_tiles", KD)
                    norm(XT, KD, "g_mix0", "const_tiles", HT)
                else:
                    norm(XT, KD, f"g_mix{L}", "lin_free", HT)
                store(SBQ, 4, scale=0.125)
                store(SBK, 4)
                store_tokens(SBV, 2, 256)
                store(DAQ, 4, scale=0.125)
                store(DAK, 4)
                store_tokens(DAV, 2, 256)
                rope([DAQ[:, t, :] for t in range(4)] + [DAK[:, t, :] for t in range(4)], COS, SIN)
                sigmoid_tail(16)
                stick_breaking()

                def head_done(h):
                    ps = lin_take()
                    v.wait_ge(*now.prev())
                    v.tensor_copy(DAQ[:, h, :], ps).then_inc(Q["lin_free"], now.inc("lin_free"))
                attention(DA_H, lambda qb: (qb + 1) * P, 2, 1.0, lambda qb: DAM[:, (3 - qb) * P:S], L, head_done)
                at[f"da{L}"] = now.count("lin_free") - DA_H
                now.skip("gate_ready", DA_H)
                now.skip("gate_free", DA_H)

                def sub_norm():
                    for h in range(DA_H):
                        v.wait_ge(Q["sub_rs"], now.next("sub_rs"))
                        v.wait_ge(*now.prev())
                        v.scalar_tensor_tensor(out=DAQ[:, h, :], in0=DAQ[:, h, :], scalar=LAM[:, 2 + L:3 + L],
                                               in1=ATT[:, (4 + h) * S:(5 + h) * S], op0=ALU.mult, op1=ALU.mult)\
                            .then_inc(Q["sub_ready"], now.inc("sub_ready"))
                sub_norm()
                branches(HT)
                add_to_x()
                norm(XT, KD, f"g_ffn{L}", "lin_free", HT)
                moe(L)
                norm(XT, KD, f"g_ple{L}", "lin_free", HT)
                sigmoid_tail(KD)
                for k in range(KD):
                    ps = lin_take()
                    v.wait_ge(*now.prev())
                    v.tensor_tensor(TMP[:, 0, :], ps, G[:, k, :], ALU.mult).then_inc(Q["dve_step"], now.inc("dve_step"))
                    v.wait_ge(*now.prev())
                    v.tensor_tensor(XT[:, k, :], XT[:, k, :], TMP[:, 0, :], ALU.add)\
                        .then_inc(Q["lin_free"], now.inc("lin_free"))
            norm(XT, KD, "g_final", "lin_free", XT, "x_ready")
            v.wait_ge(Q["pos2_landed"], now.next("pos2_landed", 48))
            trig(COS[:, :], SIN[:, :], 1)
            trig(COSM, SINM, 2)
            ffn("ffn1_pre", "ffn1_post", "x_ready")
            norm(XT, KD, "mix_pre", "x_ready", HT)
            store(CQ, 3)
            store(CKV, 2)
            store(A3[:, 8:9, :], 1, rows=DQK)
            store(DQ, 4, scale=0.125)
            store(DK, 4)
            store_tokens(DV, 2, 256)
            rope([DQ[:, t, :] for t in range(4)] + [DK[:, t, :] for t in range(4)], COS, SIN)
            rope([KR], COSM, SINM, DQK)
            at["kr"] = now.count("lin_free")
            sigmoid_tail(16)
            norm(CQ, QR // P, "q_norm", "const_landed", CQ)
            norm(CKV, KVR // P, "kv_norm", "const_landed", CKV)
            store(HT, MLA_H, rows=DQK)
            rope([HT[0:DQK, h, :] for h in range(MLA_H)], COSM, SINM, DQK)
            for t in range(MLA_H // 2):
                ps = lin_take()
                v.wait_ge(*now.prev())
                v.tensor_copy(KT[0:HD, 2 * t, :], ps[0:HD, :]).then_inc(Q["dve_step"], now.inc("dve_step"))
                v.wait_ge(*now.prev())
                v.tensor_copy(KT[0:HD, 2 * t + 1, :], ps[HD:P, :]).then_inc(Q["lin_free"], now.inc("lin_free"))
            store_tokens(VA, 1, 512)
            attention(MLA_H, lambda qb: S, 1, float(DQK) ** -0.5, None, 0, pair_done(HT))
            attention(MLA_H, lambda qb: S, 1, 1.0, lambda qb: TOEP[:, (3 - qb) * P:(3 - qb) * P + S], 0, pair_done(DQ))
            branches(MB)
            store(G, KD)
            norm(G, KD, "mix_post", "lin_free", add=1.0)
            ffn("ffn2_pre", "ffn2_post", "x_ready")
            at["out"] = now.count("x_ready")
            at["dve"] = dict(now.n)

        @block.scalar
        def _(act):
            now = Counts()
            st = {"norm": 0, "sq": 0}

            def norm(src, nt, dim):
                sem, base = at[f"norm{st['norm']}"]
                st["norm"] += 1
                for k in range(nt):
                    if sem not in ("const_landed", "const_tiles"):
                        act.wait_ge(Q[sem], base + k + 1)
                    if now.count("sq_ready") >= 2:
                        act.wait_ge(Q["sq_used"], now.count("sq_ready") - 1)
                    act.wait_ge(*now.prev())
                    act.activation(SQ[:, k % 2, :], src[:, k, :], ACT.Square)\
                        .then_inc(Q["sq_ready"], now.inc("sq_ready"))
                t = now.count("gate_ready")
                act.wait_ge(Q["gate_ready"], now.next("gate_ready"))
                act.wait_ge(*now.prev())
                act.activation(RSTD[:, :], PS[:, 2 + t % 2, :], ACT.Ln, bias=EPS_C[:, 0:1], scale=1.0 / dim)\
                    .then_inc(Q["gate_free"], now.inc("gate_free"))
                act.wait_ge(*now.prev())
                act.activation(RSTD[:, :], RSTD[:, :], ACT.Exp, scale=-0.5)\
                    .then_inc(Q["rstd_ready"], now.inc("rstd_ready"))

            def gate_exp(n, bias=False):
                for k in range(n):
                    t = now.count("gate_ready")
                    act.wait_ge(Q["gate_ready"], now.next("gate_ready"))
                    kw = {"bias": NBG[:, k:k + 1]} if bias else {}
                    act.wait_ge(*now.prev())
                    act.activation(G[:, k, :], PS[:, 2 + t % 2, :], ACT.Exp, scale=-1.0, **kw)\
                        .then_inc(Q["gate_free"], now.inc("gate_free"))

            def stick_breaking():
                even0, lin0 = now.count("pv_even"), at[f"sb{st['L']}"]

                def soft(h):
                    z = (2 + 3 * (h % 2)) * 512
                    act.wait_ge(Q["z_ready"], now.next("z_ready"))
                    if h >= 1:
                        act.wait_ge(Q["sp_ready"], now.next("sp_ready"))
                    t = ATT[:, 0:1280]
                    act.wait_ge(*now.prev())
                    act.activation(t, PSF[:, z:z + 1280], ACT.Abs).then_inc(Q["act_step"], now.inc("act_step"))
                    act.wait_ge(*now.prev())
                    act.activation(t, t, ACT.Exp, scale=-1.0).then_inc(Q["act_step"], now.inc("act_step"))
                    act.wait_ge(*now.prev())
                    act.activation(t, t, ACT.Ln, bias=1.0).then_inc(Q["soft_ready"], now.inc("soft_ready"))

                def weights(h):
                    z = (2 + 3 * (h % 2)) * 512
                    act.wait_ge(Q["lw_ready"], now.next("lw_ready"))
                    if h >= 2 and h % 2 == 0:
                        act.wait_ge(Q["pv_even"], even0 + h // 2)
                    if h >= 2 and h % 2:
                        act.wait_ge(Q["lin_ready"], lin0 + h // 2)
                    act.wait_ge(*now.prev())
                    act.activation(ATT[:, (1280 * (3 + h % 2)):(1280 * (4 + h % 2))], PSF[:, z:z + 1280], ACT.Exp)\
                        .then_inc(Q["w_ready"], now.inc("w_ready"))
                soft(0)
                for h in range(SB_H):
                    if h + 1 < SB_H:
                        soft(h + 1)
                    weights(h)
                act.wait_ge(Q["sp_ready"], now.next("sp_ready"))
                now.skip("pv_even", SB_H // 2)

            def attention(heads, nkeys, maps, scale, masked, values_of):
                jobs = [(h, qb) for h in range(heads) for qb in range(TT)]
                slots = 4 // maps
                tr0 = now.count("tr_ready")

                def exps(u):
                    h, qb = jobs[u]
                    n = nkeys(qb)
                    s = SM[:, 8 * (u % 2):8 * (u % 2) + 8]
                    act.wait_ge(Q["mx_ready"], now.next("mx_ready"))
                    if u >= 2:
                        act.wait_ge(Q["tr_ready"], tr0 + u - 1)
                    for m in range(maps):
                        x = E_[:, ((u % 2) * maps + m) * S:((u % 2) * maps + m) * S + n]
                        src = x if masked else PS[:, 4 + (u % slots) * maps + m, 0:n]
                        act.wait_ge(*now.prev())
                        act.activation(x, src, ACT.Exp, bias=s[:, m:m + 1], scale=scale,
                                       accum_out=s[:, 2 + m:3 + m])\
                            .then_inc(Q["act_step" if m < maps - 1 else "e_ready"], now.inc("act_step" if m < maps - 1 else "e_ready"))

                def turned(u):
                    h, qb = jobs[u]
                    nk = nkeys(qb) // P
                    act.wait_ge(Q["tr_ready"], now.next("tr_ready"))
                    if qb == 0 and h >= 2:
                        name, value = values_of(h - 2)
                        act.wait_ge(Q[name], value)
                    pt = ATT[:, (h % 2) * 4 * S:(h % 2 + 1) * 4 * S].rearrange("p (k q) -> p k q", k=TT)
                    act.wait_ge(*now.prev())
                    act.activation(pt[:, 0:nk, qb * P:(qb + 1) * P],
                                   PS[:, 2 + u % 2, 0:nk * P].rearrange("p (k q) -> p k q", q=P), ACT.Copy)\
                        .then_inc(Q["tr_done"], now.inc("tr_done"))
                exps(0)
                for u in range(len(jobs)):
                    if u + 1 < len(jobs):
                        exps(u + 1)
                    turned(u)

            def moe(L):
                act.wait_ge(Q["route_exp"], L + 1)
                r = RT["ge"]
                act.wait_ge(*now.prev())
                act.activation(r[:, 0:20], r[:, 0:20], ACT.Exp).then_inc(Q["table_landed"], now.inc("table_landed"))

                def x_copy(par):
                    act.wait_ge(Q["x_turned"], now.next("x_turned"))
                    act.wait_ge(*now.prev())
                    act.activation(XGT[:, par, :], PSF[:, 1024:2048], ACT.Copy)\
                        .then_inc(Q["x_copied"], now.inc("x_copied"))

                def gate(par):
                    act.wait_ge(Q["gu_ready"], now.next("gu_ready"))
                    act.wait_ge(*now.prev())
                    act.activation(HID[:, par, :], PS[:, 4 + par, 0:EH], ACT.Exp, scale=-1.0)\
                        .then_inc(Q["e_gate"], now.inc("e_gate"))

                def store_rows(b, par):
                    act.wait_ge(Q["y_ready"], now.next("y_ready"))
                    act.wait_ge(Q["const_landed"], N_CONST)
                    if isinstance(b, int):
                        dst = YDR[b * CAP:(b + 1) * CAP, :]
                    else:
                        dst = YDR[bass.ds(b * CAP, CAP), :]
                    act.dma_start(dst, YB[:, par, :]).then_inc(Q[f"y_store{par}"], 16)
                x_copy(0)
                gate(0)
                x_copy(1)
                gate(1)
                x_copy(0)
                store_rows(0, 0)
                gate(0)
                x_copy(1)
                store_rows(1, 1)
                turns = (NB - 3) // 2
                with act.Fori(0, turns) as i:
                    now.enter(i, dict(x_turned=2, x_copied=2, gu_ready=2, e_gate=2, y_ready=2))
                    gate(1)
                    x_copy(0)
                    store_rows(i * 2 + 2, 0)
                    gate(0)
                    x_copy(1)
                    store_rows(i * 2 + 3, 1)
                now.leave(turns)
                store_rows(NB - 1, 0)

            def ffn(dim=D):
                norm(XT, KD, D)
                for k in range(KF):
                    t = now.count("gate_ready")
                    act.wait_ge(Q["gate_ready"], now.next("gate_ready"))
                    if k >= 2:
                        act.wait_ge(Q["lin_free"], at[f"ffn{st['ffn']}"] + k - 1)
                    act.wait_ge(*now.prev())
                    act.activation(A3[:, 3 + k % 2, :], PS[:, 2 + t % 2, :], ACT.Exp, scale=-1.0)\
                        .then_inc(Q["e_gate"], now.inc("e_gate"))
                now.skip("gate_free", KF)
                st["ffn"] += 1
                norm(G, KD, D)

            st["ffn"] = 0
            act.wait_ge(Q["const_landed"], N_CONST)
            act.wait_ge(Q["pos_landed"], 1)
            act.wait_ge(*now.prev())
            act.activation(LAM[:, 4:8], LAM[:, 4:8], ACT.Exp).then_inc(Q["lam_exp"], now.inc("lam_exp"))

            def trig(cos, sin):
                act.wait_ge(Q["ang_ready"], now.next("ang_ready"))
                act.wait_ge(*now.prev())
                act.activation(sin, TMP[:, 0, :], ACT.Sin).then_inc(Q["act_step"], now.inc("act_step"))
                act.wait_ge(*now.prev())
                act.activation(TMP[:, 1, :], TMP[:, 0, :], ACT.Abs).then_inc(Q["act_step"], now.inc("act_step"))
                act.wait_ge(*now.prev())
                act.activation(cos, TMP[:, 1, :], ACT.Sin, scale=-1.0, bias=EPS_C[:, 1:2])\
                    .then_inc(Q["trig_ready"], now.inc("trig_ready"))
            trig(COS[:, :], SIN[:, :])
            act.preload_act_table_set("natural_log_exp_and_others")
            for L in range(LAYERS):
                st["L"] = L
                norm(XT, KD, D)
                gate_exp(16)
                stick_breaking()
                attention(DA_H, lambda qb: (qb + 1) * P, 2, 1.0, True,
                          lambda h: ("lin_ready", at[f"da{L}"] + h + 1))
                for h in range(DA_H):
                    act.wait_ge(Q["lin_free"], at[f"da{L}"] + DA_H)
                    act.wait_ge(*now.prev())
                    act.activation(ATT[:, h * S:(h + 1) * S], DAQ[:, h, :], ACT.Square)\
                        .then_inc(Q["sub_sq"], now.inc("sub_sq"))
                for h in range(DA_H):
                    t = now.count("gate_ready")
                    act.wait_ge(Q["gate_ready"], now.next("gate_ready"))
                    a = ATT[:, (4 + h) * S:(5 + h) * S]
                    act.wait_ge(*now.prev())
                    act.activation(a, PS[:, 2 + t % 2, :], ACT.Ln, bias=EPS_C[:, 0:1], scale=1.0 / P)\
                        .then_inc(Q["gate_free"], now.inc("gate_free"))
                    act.wait_ge(*now.prev())
                    act.activation(a, a, ACT.Exp, scale=-0.5).then_inc(Q["sub_rs"], now.inc("sub_rs"))
                norm(XT, KD, D)
                moe(L)
                norm(XT, KD, D)
                gate_exp(KD)
            norm(XT, KD, D)
            trig(COS[:, :], SIN[:, :])
            trig(COSM, SINM)
            act.preload_act_table_set("natural_log_exp_and_others")
            ffn()
            norm(XT, KD, D)
            gate_exp(16, bias=True)
            norm(CQ, QR // P, QR)
            norm(CKV, KVR // P, KVR)
            even0 = now.count("pv_even")
            now.skip("pv_even", MLA_H)

            def used_pairs(n):
                return lambda h: (("pv_even", even0 + n * MLA_H // 2 + h // 2 + 1) if h % 2 == 0
                                  else ("lin_ready", at[f"pairs{n}"] + h // 2 + 1))
            attention(MLA_H, lambda qb: S, 1, float(DQK) ** -0.5, False, used_pairs(0))
            attention(MLA_H, lambda qb: S, 1, 1.0, True, used_pairs(1))
            norm(G, KD, D)
            ffn()

        @block.gpsimd
        def _(pool):
            now = Counts()

            pool.wait_ge(Q["const_landed"], N_CONST)
            pool.memset(RT["idx"].bitcast(I32), 0).then_inc(Q["zero_ready"], now.inc("zero_ready"))
            pool.wait_ge(*now.prev())
            pool.dma_start(SLOTS.rearrange("(p b) o -> p (b o)", p=P), RT["idx"].bitcast(I32)).then_inc(Q["zero_stored"], 16)
            pool.wait_ge(Q["zero_stored"], 16)

            def keep_later(a, name):
                pool.wait_ge(*now.prev())
                d = a[:, 0:512].rearrange("p (b q) -> p b q", b=TT)
                pool.affine_select(out=d, in_=d, compare_op=ALU.is_gt, fill=0.0, base=0,
                                   pattern=[[0, TT], [1, P]], channel_multiplier=-1)\
                    .then_inc(Q[name], now.inc(name))

            def softplus(h):
                pool.wait_ge(Q["sp_ready"], now.next("sp_ready"))
                keep_later(ATT[:, (1280 * (1 + h % 2)):(1280 * (2 + h % 2))], "sp_masked")

            def weights(h):
                pool.wait_ge(Q["w_ready"], now.next("w_ready"))
                keep_later(ATT[:, (1280 * (3 + h % 2)):(1280 * (4 + h % 2))], "w_masked")

            idx = RT["idx"].bitcast(U32)
            sloti, adri = RT["sloti"].bitcast(U32), RT["adri"].bitcast(U32)
            IOA = bass.IndirectOffsetOnAxis

            def gather(b):
                pool.indirect_dma_start(out=XG[:, b % 2, :], out_offset=None, in_=HDR,
                                        in_offset=IOA(ap=idx[:, b:b + 1], axis=0)).then_inc(Q[f"x_gather{b % 2}"], 16)

            for L in range(LAYERS):
                softplus(0)
                for h in range(SB_H):
                    if h + 1 < SB_H:
                        softplus(h + 1)
                    weights(h)
                pool.wait_ge(Q["lin_free"], at[f"htok{L}"])
                pool.dma_start(HDR.rearrange("(t p) d -> p t d", p=P), HTOK).then_inc(Q["h_stored"], 16)
                pool.wait_ge(Q["slots_ready"], now.next("slots_ready"))
                for j in range(2 * TT):
                    pool.indirect_dma_start(out=SLOTS, out_offset=IOA(ap=adri[:, j:j + 1], axis=0),
                                            in_=TOK[:, j // 2:j // 2 + 1], in_offset=None)\
                        .then_inc(Q["tok_scattered"], 16)
                pool.wait_ge(Q["tok_scattered"], now.next("tok_scattered", 16 * 2 * TT))
                pool.dma_start(RT["idx"].bitcast(I32), SLOTS.rearrange("(p b) o -> p (b o)", p=P))\
                    .then_inc(Q["idx_landed"], 16)
                pool.wait_ge(Q["idx_landed"], now.next("idx_landed", 16))
                pool.wait_ge(Q["h_stored"], now.next("h_stored", 16))
                x0 = at[f"moe{L}"]["x_turned"]
                for b in range(NBP):
                    if b >= 2:
                        pool.wait_ge(Q["x_turned"], x0 + b - 1)
                    gather(b)
                pool.wait_ge(Q["y_store0"], 16 * (L + 1) * ((NB + 1) // 2))
                pool.wait_ge(Q["y_store1"], 16 * (L + 1) * (NB // 2))
                for j in range(2 * TT):
                    pool.indirect_dma_start(out=YG[:, j, :], out_offset=None, in_=YDR,
                                            in_offset=IOA(ap=sloti[:, j:j + 1], axis=0))\
                        .then_inc(Q["y_gathered"], 16)
                pool.wait_ge(Q["x_turned"], x0 + NBP)
                pool.dma_start(PLT, A["pT"][L].rearrange("(k p) t -> p k t", p=P)).then_inc(Q["pl_landed"], 16)
            pos2 = A["positions_2"].rearrange("a t -> (a t)").partition_broadcast(P)
            pool.wait_ge(Q["x_ready"], KD)
            for dst in (SIN[:, :], SINM):
                pool.dma_start(dst.bitcast(I32), pos2).then_inc(Q["pos2_landed"], 16)
            pool.dma_start(TOEP, A["c_lnc"]).then_inc(Q["pos2_landed"], 16)
            pool.wait_ge(Q["pos2_landed"], 48)
            pool.wait_ge(Q["lin_free"], at["kr"])
            for h in range(MLA_H):
                pool.tensor_copy(KT[NOPE:DQK, h, :], KR[NOPE:DQK, :]).then_inc(Q["kr_copied"], now.inc("kr_copied"))

        @block.sync
        def _(sp):
            now = Counts()

            def const(dst, src):
                sp.dma_start(dst, src).then_inc(Q["const_landed"], 16)
                consts.append(1)
            consts = []
            xv = A["xT"].rearrange("(k p) t -> p k t", p=P)
            const(XT[:, 0:4, :], xv[:, 0:4, :])
            const(XT[:, 4:8, :], xv[:, 4:8, :])
            const(MATS[:, :], A["c_mats"])
            const(GC[:, :], A["gains"])
            const(FREQ[:, :], A["c_freq"])
            const(EPS_C[:, :], A["c_eps"])
            const(SIN[:, :].bitcast(I32), A["positions"].rearrange("a t -> (a t)").partition_broadcast(P))
            const(BIGF[:, 0:4 * LAYERS * HD], A["lam"].partition_broadcast(P))
            const(DAM[:, :], A["c_da"])
            const(REV[:, :], A["c_rev"])
            const(BLK[:, :], A["c_blk"])
            const(TOK[:, :], A["c_tok"])
            const(WR[:, :, :, :], A["w_router"])
            const(BR[:, :, :], A["b_router"].partition_broadcast(P))
            assert 16 * len(consts) == N_CONST
            plan = Ring()
            n = [0]

            def load():
                place, fill = plan.next()
                if fill > 1:
                    name, value = used[(place, fill - 1)]
                    sp.wait_ge(Q[name], value)
                sp.dma_start(ring[:, place, :], A["stream"][n[0]]).then_inc(w_landed[place], 16)
                n[0] += 1

            def experts(L):
                plan.align()
                p0, before = plan.blocks()
                first = at[f"moe{L}"]
                sp.wait_ge(Q["blk_ready"], L + 1)

                def block_load(i, par, prior):
                    if isinstance(i, int):
                        b = RT["blki"].bitcast(I32)[0:1, 2 * i + par:2 * i + par + 1]
                    else:
                        b = RT["blki"].bitcast(I32)[0:1, bass.ds(i * 2 + par, 1)]
                    x = sp.value_load(b, min_val=0, max_val=NE - 1)
                    for j in range(3):
                        place = (p0 + 3 * par + j) % RING
                        if prior is None:
                            if before[place]:
                                name, value = used[(place, before[place])]
                                sp.wait_ge(Q[name], value)
                        else:
                            name = "dn_ready" if j == 2 else "gu_ready"
                            sp.wait_ge(Q[name], prior * 2 + (first[name] + par + 1))
                            sp.wait_ge(Q["const_landed"], N_CONST)
                        src = A["experts"][L, bass.ds(x, 1), j, :, :].rearrange("a p n -> (a p) n")
                        sp.dma_start(ring[:, place, :], src).then_inc(w_landed[place], 16)
                block_load(0, 0, None)
                block_load(0, 1, None)
                with sp.Fori(0, NB // 2 - 1) as i:
                    block_load(i + 1, 0, i)
                    block_load(i + 1, 1, i)
                block_load(NB // 2, 0, NB // 2 - 1)

            for L in range(LAYERS):
                for _ in range(N_LAYER_U):
                    load()
                experts(L)
                for _ in range(N_PLE_U):
                    load()
            for _ in range(2 * N_FFN_U + N_MIX_U):
                load()
            assert n[0] == N_STREAM
            sp.wait_ge(Q["x_ready"], at["out"])
            sp.dma_start(out.rearrange("(k p) t -> p k t", p=P), XT[:, :, :]).then_inc(Q["stored_out"], 16)
            sp.wait_ge(Q["stored_out"], 16)
            sp.wait_ge(Q["y_store0"], 16 * LAYERS * ((NB + 1) // 2))
            sp.wait_ge(Q["y_store1"], 16 * LAYERS * (NB // 2))


def host_arrays(x):
    a = {k: np.ascontiguousarray(v) for k, v in x.items()}
    out = {"xT": a["x"][0].T, "pT": a["p"][:, 0].transpose(0, 2, 1), "positions": a["positions"],
           "positions_2": a["positions_2"]}
    stream = []
    for i in range(LAYERS):
        stream += layer_units(a["w_in"][i], a["w_br_a"][i], a["w_br_b"][i], a["w_o"][i])
        stream += ple_units(a["w_ple_gate"][i], a["w_ple"][i])
    f1 = ffn_units(a["ffn1_w_gate_2"][0], a["ffn1_w_up_2"][0], a["ffn1_w_down_2"][0])
    f2 = ffn_units(a["ffn2_w_gate_2"][0], a["ffn2_w_up_2"][0], a["ffn2_w_down_2"][0])
    mix = mixer_units(a["w_in_2"][0], a["w_uq_2"][0], a["w_uk_2"][0], a["w_uv_2"][0],
                      a["w_branch_a_2"][0], a["w_branch_b_2"][0], a["w_out_2"][0])
    out["stream"] = np.stack(stream + f1 + mix + f2)
    wg = a["w_exp_gate"].reshape(LAYERS, NE, KD, P, EH).transpose(0, 1, 3, 2, 4).reshape(LAYERS, NE, P, UNIT)
    wu = a["w_exp_up"].reshape(LAYERS, NE, KD, P, EH).transpose(0, 1, 3, 2, 4).reshape(LAYERS, NE, P, UNIT)
    wd = a["w_exp_down"].reshape(LAYERS, NE, 2, P, D).transpose(0, 1, 3, 2, 4).reshape(LAYERS, NE, P, UNIT)
    out["experts"] = np.stack([wg, wu, wd], axis=2)
    gains = []
    for name, length in GAINS:
        if name[-1].isdigit() and name[:-1] in ("g_mix", "g_ffn", "g_ple", "g_subln"):
            g = a[name[:-1]][int(name[-1])]
        elif name == "g_final":
            g = a[name]
        elif name == "b_gate":
            g = a["b_gate_2"][0]
        else:
            g = a[name + "_g_2"][0]
        gains.append(g.reshape(length // P, P).T)
    out["gains"] = np.concatenate(gains, axis=1)
    out["lam"] = np.concatenate([a[n].reshape(-1) for n in ("lam_q1", "lam_k1", "lam_q2", "lam_k2")])
    wr = np.concatenate([a["w_router_group"], a["w_router_expert"]], axis=2)
    out["w_router"] = wr.reshape(LAYERS, KD, P, NG + NE).transpose(2, 0, 1, 3)
    out["b_router"] = np.concatenate([a["b_router_group"], a["b_router_expert"]], axis=1)
    out.update(shape_constants())
    return {k: np.ascontiguousarray(v) for k, v in out.items()}


def kernel(**inputs):
    import concourse.bacc as bacc
    from concourse.bass_utils import run_bass_kernel_spmd

    nc = bacc.Bacc("TRN2", target_bir_lowering=False, num_devices=1)
    arrays, aps = {}, {}
    for name, a in host_arrays(inputs).items():
        arrays[f"in_{name}"] = a
        aps[name] = nc.dram_tensor(f"in_{name}", a.shape, mybir.dt.from_np(a.dtype), kind="ExternalInput").ap()
    out = nc.dram_tensor("out_T", (D, S), F32, kind="ExternalOutput").ap()
    build_program(nc, aps, out)
    r = run_bass_kernel_spmd(nc, [arrays], core_ids=[0])
    return np.ascontiguousarray(r.results[0]["out_T"].T).reshape(1, S, D)
```

```python
from contextlib import ExitStack
import math

import numpy as np
import concourse.bass as bass
from concourse import mybir

F32 = mybir.dt.float32
I32 = mybir.dt.int32
U32 = mybir.dt.uint32
ALU = mybir.AluOpType
ACT = mybir.ActivationFunctionType
AX = mybir.AxisListType.X

P = 128
S = 512
D = 1024
KD = D // P
TT = S // P
LAYERS = 2
UNIT = 2048
RING = 6
EPS = 1e-6

SB_H, DA_H, HD = 8, 4, 64
W_IN = 5120
NG, NEG_, NE = 4, 8, 32
EH = 256
CAP = 128
NB = 39
NBP = NB + 1
PLE = 256
SB_GATES = (2, 1, 1, 1, 2, 1, 1, 1)
DA_GATES = (0, 1, 2, 3, 4, 6)
DA_BRANCH = (7, 9, 10, 11, 13, 14)
DA_SIGMOID = (4, 7, 8, 11, 12, 15)
FF = 2816
KF = FF // P
MLA_H, QR, KVR, NOPE, ROPE_M = 8, 384, 256, 64, 32
DQK = NOPE + ROPE_M
BIG_NEG = -1e30
X_LANDED = 16 * 5
N_CONST = 16 * 9

GAINS = ([(f"{n}{i}", l) for i in range(LAYERS) for n, l in
          (("g_mix", D), ("g_ffn", D), ("g_ple", D), ("g_subln", P))]
         + [("g_final", D)]
         + [(n, l) for n, l in (("ffn1_pre", D), ("ffn1_post", D), ("mix_pre", D), ("q_norm", QR),
                                ("kv_norm", KVR), ("mix_post", D), ("ffn2_pre", D), ("ffn2_post", D),
                                ("b_gate", 2 * D))])
GCOL = {}
_c = 0
for _n, _l in GAINS:
    GCOL[_n] = _c
    _c += _l // P
NGC = _c


def unit_of(w, k0, k1, c0, c1):
    nk = (k1 - k0) // P
    a = w[k0:k1, c0:c1].reshape(nk, P, c1 - c0).transpose(1, 0, 2).reshape(P, nk * (c1 - c0))
    u = np.zeros((P, UNIT), w.dtype)
    u[:, :a.shape[1]] = a
    return u


def cut(w, width):
    return [unit_of(w, 0, w.shape[0], c, c + width) for c in range(0, w.shape[1], width)]


def ffn_units(wg, wu, wd):
    out = []
    for c in range(0, FF, 256):
        out += [unit_of(wg, 0, D, c, c + 256), unit_of(wu, 0, D, c, c + 256)]
    for c in range(0, D, 256):
        for k in range(0, FF, D):
            out.append(unit_of(wd, k, min(k + D, FF), c, c + 256))
    return out


def layer_units(w_in, w_a, w_b, w_o, w_ple, w_ple_gate):
    return cut(w_in, 256) + cut(w_a, 512) + cut(w_b, 512) + cut(w_o, 256) + cut(w_ple, 1024) + cut(w_ple_gate, 256)


def mixer_units(w_in, w_uq, w_uk, w_uv, w_a, w_b, w_o):
    u = [unit_of(w_in, 0, D, 0, 256), unit_of(w_in, 0, D, 256, 384), unit_of(w_in, 0, D, 384, 640),
         unit_of(w_in, 0, D, 576, 672)]
    u += [unit_of(w_in, 0, D, c, c + 256) for c in range(672, w_in.shape[1], 256)]
    return (u + cut(w_uq, 384) + cut(w_uk, 512) + cut(w_uv, 512)
            + cut(w_b, 512) + cut(w_a, 512) + cut(w_o, 256))


N_LAYER_U = 20 + 2 + 2 + 4 + 1
N_PLE_U = 4
N_FFN_U = 22 + 12
N_MIX_U = 4 + 14 + 2 + 1 + 1 + 2 + 2 + 4
N_STREAM = LAYERS * (N_LAYER_U + N_PLE_U) + 2 * N_FFN_U + N_MIX_U


def shape_constants():
    i = np.arange(P)
    ident = (i[:, None] == i[None, :]).astype(np.float32)
    ones = np.ones((P, P), np.float32)
    ntri = -(i[:, None] >= i[None, :]).astype(np.float32)
    before = (i[:, None] < i[None, :]).astype(np.float32)

    def rotation(n, first, block, half):
        r = np.zeros((P, P), np.float32)
        for b in range(first, n, block):
            for d in range(half):
                r[b + d + half, b + d] = -1.0
                r[b + d, b + d + half] = 1.0
        return r
    rot = rotation(P, 0, HD, 8)
    rotm = rotation(DQK, NOPE, P, 16)
    mats = np.concatenate([ident, ones, -ones, ntri, before, rot, rotm], axis=1)
    da = np.zeros((P, S), np.float32)
    da[0:64, S - 64:] = BIG_NEG
    x = np.arange(S + 384)[None, :] - 384 - i[:, None]
    n = ((np.abs(x) <= 64).astype(int) + ((x % 4 == 0) & (np.abs(x) <= 256))
         + (x % 16 == 0))
    lnc = np.where(n > 0, np.log(np.maximum(n, 1)), BIG_NEG).astype(np.float32)
    inv1 = (np.float32(500000.0) ** (-np.arange(0, 16, 2, dtype=np.float32) / np.float32(16))).astype(np.float32)
    inv2 = (np.float32(1) / np.float32(500000.0) ** (np.arange(8, dtype=np.float32) / np.float32(8))).astype(np.float32)
    inv3 = (np.float32(1) / np.float32(10000.0) ** (np.arange(16, dtype=np.float32) / np.float32(16))).astype(np.float32)
    freq = np.zeros((P, 3), np.float32)
    for b in (0, 64):
        for h in (0, 8):
            freq[b + h:b + h + 8, 0] = inv1
            freq[b + h:b + h + 8, 1] = inv2
    freq[64:80, 2] = inv3
    freq[80:96, 2] = inv3
    rev = np.zeros((P, NG + NE), np.float32)
    rev[:, :NG] = NG - np.arange(NG)
    rev[:, NG:] = NE - np.arange(NE)
    blk = np.arange(NB, dtype=np.float32)[None, :]
    eps = np.tile(np.array([EPS, math.pi / 2], np.float32), (P, 1))
    tok = (np.arange(TT, dtype=np.int32)[None, :] * P + i[:, None]).astype(np.int32)
    return {"c_mats": mats, "c_da": da, "c_lnc": lnc, "c_freq": freq, "c_rev": rev, "c_blk": blk, "c_eps": eps, "c_tok": tok}


def build_program(nc, A, out):
    with ExitStack() as ctx:
        def sb(name, shape, dt=F32):
            return ctx.enter_context(nc.sbuf_tensor(name, shape, dt))

        XT = sb("XT", [P, KD, S])
        HT = sb("HT", [P, KD, S])
        ring = sb("ring", [P, RING, UNIT])
        BIG = sb("BIG", [P, 24, S])
        G = sb("G", [P, 16, S])
        ATT = sb("ATT", [P, 14 * S])
        MATS = sb("MATS", [P, 7 * P])
        DAM = sb("DAM", [P, S])
        COS = sb("COS", [P, S])
        SIN = sb("SIN", [P, S])
        RSTD = sb("RSTD", [P, S])
        TMP = sb("TMP", [P, 2, S])
        GC = sb("GC", [P, NGC])
        FREQ = sb("FREQ", [P, 3])
        WR = sb("WR", [P, LAYERS, KD, NG + NE])
        BR = sb("BR", [P, LAYERS, NG + NE])
        LAM = sb("LAM", [P, 8])
        SM = sb("SM", [P, 16])
        NBG = sb("NBG", [P, 16])
        IDENT, ONES, NONES, NTRI, BEFORE, ROT, ROTM = (MATS[:, i * P:(i + 1) * P] for i in range(7))
        PS = ctx.enter_context(nc.psum_tensor("PS", [P, 8, 512], F32))
        PSF = PS[:, :, :].rearrange("p b n -> p (b n)")

        SBQ, SBK, SBV = (BIG[:, 4 * i:4 * i + 4, :] for i in range(3))
        DAQ, DAK, DAV = (BIG[:, 12 + 4 * i:16 + 4 * i, :] for i in range(3))
        CQ, CKV, KR, ROPEM = BIG[:, 0:3, :], BIG[:, 3:5, :], BIG[0:DQK, 5, :], BIG[:, 6:8, :]
        KT, VA, MB = BIG[:, 16:24, :], BIG[:, 8:12, :], BIG[:, 0:8, :]
        DQ, DK, DV = (BIG[:, 12 + 4 * i:16 + 4 * i, :] for i in range(3))
        A3 = ATT[:, :].rearrange("p (a b) -> p a b", b=S)
        COSM, SINM = A3[:, 9, :], A3[:, 10, :]
        E_ = ATT[:, 8 * S:12 * S]
        TOEP = ATT[:, 12 * S:12 * S + S + 384]
        SQ = ATT[:, 0:2 * S].rearrange("p (a b) -> p a b", a=2)
        ACC = ATT[:, 2 * S:3 * S]
        BIGF = BIG[:, :, :].rearrange("p a b -> p (a b)")
        GF = G[:, :, :].rearrange("p a b -> p (a b)")

        HDR = nc.dram_tensor("h_tokens", (S, D), F32, kind="Internal").ap()
        YDR = nc.dram_tensor("expert_rows", (NB * CAP, D), F32, kind="Internal").ap()
        SLOTS = nc.dram_tensor("slot_tokens", (NBP * CAP, 1), I32, kind="Internal").ap()

        names = ("const_landed lin_ready lin_free gate_ready gate_free sq_ready sq_used rstd_ready h_ready "
                 "dve_step act_step z_ready soft_ready sp_ready sp_masked suffix_ready lw_ready w_ready "
                 "w_masked sc_ready g_exp mx_ready e_ready p_ready tr_ready tr_done raw_ready sub_sq sub_rs "
                 "sub_ready x_ready lg_ready route_exp rank_ready mask_ready slots_ready tok_scattered "
                 "h_stored idx_landed x_gather0 x_gather1 x_turned x_copied gu_ready e_gate hid_ready "
                 "hid_turned hidT_ready dn_ready y_ready y_store0 y_store1 y_gathered0 y_gathered1 y_gathered2 "
                 "y_gathered3 comb_ready blk_ready table_landed stored_out ang_ready trig_ready kr_copied "
                 "pl_landed x_landed pos_landed pos2_landed lam_exp zero_ready zero_stored").split()
        Q = {n: ctx.enter_context(nc.semaphore(n)) for n in names}
        w_landed = [ctx.enter_context(nc.semaphore(f"w_landed{i}")) for i in range(RING)]
        block = ctx.enter_context(nc.Block())

        class Ring:

            def __init__(self):
                self.place, self.fills = 0, [0] * RING

            def next(self):
                p = self.place
                self.fills[p] += 1
                self.place = (p + 1) % RING
                return p, self.fills[p]

            def align(self):
                while self.place % 3:
                    self.place = (self.place + 1) % RING

            def blocks(self):
                p, before = self.place, list(self.fills)
                for b in range(NB):
                    for j in range(3):
                        self.fills[(p + 3 * b + j) % RING] += 1
                self.place = (p + 3 * NB) % RING
                return p, before

        class Counts:

            def __init__(self):
                self.n = {"const_landed": N_CONST, "x_landed": X_LANDED}
                self.last = "x_landed"

            def count(self, name):
                return self.n.get(name, 0)

            def inc(self, name):
                self.n[name] = self.count(name) + 1
                self.last = name
                return 1

            def next(self, name, k=1):
                self.n[name] = self.count(name) + k
                return self.n[name]

            def prev(self):
                return Q[self.last], self.n[self.last]

            def skip(self, name, k=1):
                self.n[name] = self.count(name) + k

            def enter(self, i, per):
                self.saved, self.per = dict(self.n), per
                for k, d in per.items():
                    self.n[k] = i * d + self.count(k)

            def leave(self, turns):
                for k, d in self.per.items():
                    self.n[k] = self.saved.get(k, 0) + turns * d

        used = {}
        at = {}

        RT = {}
        _o = 0
        for _n, _w in (("mask", 128), ("logit", 144), ("gmax", 4), ("ge", 20), ("gsum", 4), ("eq", 16), ("pen", 16),
                       ("one1", 128), ("one2", 128), ("tmp", 128), ("m1", 4), ("m2", 4), ("s4", 4), ("rank", 128),
                       ("cnt", 32), ("nblk", 32), ("end", 32), ("over", 128), ("gate", 8), ("sum8", 8), ("adr", 8),
                       ("sloti", 8), ("adri", 8), ("idx", NBP), ("blkf", NB), ("blki", NB), ("one32", 32),
                       ("cmp", NB * NE)):
            RT[_n] = ATT[:, _o:_o + _w]
            _o += _w
        assert _o <= 14 * S
        TOK = ctx.enter_context(nc.sbuf_tensor("TOK", [P, TT], I32))
        XG = BIGF[:, 0:2 * D].rearrange("p (a d) -> p a d", a=2)
        XGT = BIGF[:, 2 * D:4 * D].rearrange("p (a n) -> p a n", a=2)
        YB = BIGF[:, 4 * D:6 * D].rearrange("p (a n) -> p a n", a=2)
        HID = BIGF[:, 6 * D:6 * D + 512].rearrange("p (a n) -> p a n", a=2)
        HIDT = BIGF[:, 6 * D + 512:7 * D].rearrange("p (a n) -> p a n", a=2)
        COMB = BIGF[:, 8 * D:12 * D].rearrange("p (t d) -> p t d", t=TT)
        HTOK = GF[:, 0:4 * D].rearrange("p (t d) -> p t d", t=TT)
        YG = GF[:, :].rearrange("p (j d) -> p j d", j=2 * TT)
        PLT = BIG[:, 16:18, :]
        HP = G[:, KD:2 * KD, :]
        REV = sb("REV", [P, NG + NE])
        BLK = sb("BLK", [1, NB])
        EPS_C = sb("EPS_C", [P, 2])

        @block.tensor
        def _(pe):
            now = Counts()
            st = {}
            plan = Ring()

            def unit():
                st["unit"] = plan.next()
                place, fill = st["unit"]
                pe.wait_ge(w_landed[place], 16 * fill)
                return ring[:, place, :]

            def unit_used(name, unit=None):
                used[unit or st["unit"]] = (name, now.count(name))

            def lin_open():
                t = now.count("lin_ready")
                if t >= 2:
                    pe.wait_ge(Q["lin_free"], t - 1)
                return PS[:, t % 2, :]

            def gate_open():
                t = now.count("gate_ready")
                if t >= 2:
                    pe.wait_ge(Q["gate_free"], t - 1)
                return PS[:, 2 + t % 2, :]

            opened = {"lin_ready": lin_open, "gate_ready": gate_open}

            def drained(name):
                pe.wait_ge(Q[{"lin_ready": "lin_free", "gate_ready": "gate_free"}[name]], now.count(name))

            def norm_sum(nt):
                ps = gate_open()
                pe.wait_ge(Q["sq_used"], now.next("sq_used", nt))
                pe.matmul(ps, ONES, ATT[:, 2 * S:3 * S], start=True, stop=True)\
                    .then_inc(Q["gate_ready"], now.inc("gate_ready"))

            def project(w, nk, width, rhs, ring_name, m=P, h_wait=False):
                wv = w[:, 0:nk * width].rearrange("p (k c) -> p k c", k=nk)
                for c in range(0, width, m):
                    ps = opened[ring_name]()
                    for k in range(nk):
                        if h_wait and c == 0:
                            pe.wait_ge(Q["h_ready"], now.next("h_ready"))
                        mm = pe.matmul(ps[0:m, :], wv[:, k, c:c + m], rhs[:, k, :], start=k == 0, stop=k == nk - 1)
                    mm.then_inc(Q[ring_name], now.inc(ring_name))
                unit_used(ring_name)

            def project_tokens(w, nk, width, lhs):
                wv = w[:, 0:nk * width].rearrange("p (k c) -> p k c", k=nk)
                for t in range(TT):
                    ps = lin_open()
                    for k in range(nk):
                        mm = pe.matmul(ps[:, 0:width], lhs[:, k, t * P:(t + 1) * P], wv[:, k, :],
                                       start=k == 0, stop=k == nk - 1)
                    mm.then_inc(Q["lin_ready"], now.inc("lin_ready"))
                unit_used("lin_ready")

            def project_tile(units, nk, width, rhs, m):
                if m * P % width == 0:
                    units["w"] = unit()
                w = units["w"][:, 0:nk * width].rearrange("p (k c) -> p k c", k=nk)
                c = m * P % width
                ps = lin_open()
                for k in range(nk):
                    mm = pe.matmul(ps, w[:, k, c:c + P], rhs[:, k, :], start=k == 0, stop=k == nk - 1)
                mm.then_inc(Q["lin_ready"], now.inc("lin_ready"))
                if c + P == width:
                    unit_used("lin_ready")

            def rotate(tiles, mat, rows=P):
                for t in tiles:
                    ps = lin_open()
                    pe.matmul(ps[0:rows, :], mat[0:rows, 0:rows], t, start=True, stop=True)\
                        .then_inc(Q["lin_ready"], now.inc("lin_ready"))

            gates = {}

            def stick_breaking():
                at[f"sb{L}"] = now.count("lin_ready")

                def z_bank(h):
                    return (2 + 3 * (h % 2)) * 512

                def off(kb, qb):
                    d = qb - kb
                    return (kb * P, 512 + kb * P, 1024 + kb * P, 896)[d]
                blocks = [(kb, kb + d) for d in (0, 1, 3, 2) for kb in range(4 - d)]

                def logits(h):
                    r = slice(64 * (h % 2), 64 * (h % 2) + 64)
                    if h >= 2:
                        pe.wait_ge(Q["w_ready"], base_w + h - 1)
                    for kb, qb in blocks:
                        o = off(kb, qb)
                        mm = pe.matmul(PSF[:, z_bank(h) + o:z_bank(h) + o + P],
                                       SBK[r, h // 2, kb * P:(kb + 1) * P], SBQ[r, h // 2, qb * P:(qb + 1) * P],
                                       start=o % 512 == 0, stop=False, skip_group_check=True)
                    mm.then_inc(Q["z_ready"], now.inc("z_ready"))

                def log_weights(h):
                    z = z_bank(h)
                    sp = ATT[:, (1280 * (1 + h % 2)):(1280 * (2 + h % 2))]
                    rd = ATT[:, 6400:6784]
                    pe.wait_ge(Q["suffix_ready"], now.next("suffix_ready"))
                    for a, b in ((0, 512), (512, 1024), (1024, 1280)):
                        pe.matmul(PSF[:, z + a:z + b], NTRI, sp[:, a:b], start=False, stop=False, skip_group_check=True)
                    for a, b, src in ((512, 896, sp[:, P:512]), (896, 1024, rd[:, 256:384]), (1024, 1280, rd[:, 0:256])):
                        mm = pe.matmul(PSF[:, z + a:z + b], NONES, src, start=False, stop=True, skip_group_check=True)
                    mm.then_inc(Q["lw_ready"], now.inc("lw_ready"))

                def values(h):
                    r = slice(64 * (h % 2), 64 * (h % 2) + 64)
                    w = ATT[:, (1280 * (3 + h % 2)):(1280 * (4 + h % 2))]
                    o = lin_open()
                    pe.wait_ge(Q["w_masked"], now.next("w_masked"))
                    first = True
                    for kb in range(TT):
                        for qb in range(kb, TT):
                            mm = pe.matmul(o[r, qb * P:(qb + 1) * P], SBV[:, kb, h * HD:(h + 1) * HD],
                                           w[:, off(kb, qb):off(kb, qb) + P], start=first,
                                           stop=kb == qb, skip_group_check=True)
                            first = False
                    mm.then_inc(Q["lin_ready"], now.inc("lin_ready"))

                base_w = now.count("w_ready")
                drained("gate_ready")
                logits(0)
                for h in range(SB_H):
                    if h + 1 < SB_H:
                        logits(h + 1)
                    project_tile(gates, KD, 256, HT, sum(SB_GATES[:h]))
                    log_weights(h)
                    if SB_GATES[h] == 2:
                        project_tile(gates, KD, 256, HT, sum(SB_GATES[:h]) + 1)
                    if h >= 1:
                        values(h - 1)
                values(SB_H - 1)
                now.skip("w_ready", SB_H)

            def attention(heads, score, nkeys, ahead, maps, values, taken, fill):
                jobs = [(h, qb) for h in range(heads) for qb in range(TT)]
                base = {k: now.count(k) for k in ("mx_ready", "e_ready", "tr_done", "p_ready")}

                def scores(u):
                    slots = 4 // maps
                    if u >= slots:
                        pe.wait_ge(Q[taken], base[taken] + u - slots + 1)
                    h, qb = jobs[u]
                    for m in range(maps):
                        b = 4 + (u % slots) * maps + m
                        mm = score(PS[:, b, 0:nkeys(qb)], h, m, qb)
                    mm.then_inc(Q["sc_ready"], now.inc("sc_ready"))

                def turn(u):
                    h, qb = jobs[u]
                    if u >= 2:
                        pe.wait_ge(Q["tr_done"], base["tr_done"] + u - 1)
                    pe.wait_ge(Q["p_ready"], now.next("p_ready"))
                    for kb in range(nkeys(qb) // P):
                        mm = pe.transpose(PS[:, 2 + u % 2, kb * P:(kb + 1) * P],
                                          E_[:, (u % 2) * maps * S + kb * P:(u % 2) * maps * S + (kb + 1) * P], IDENT)
                    mm.then_inc(Q["tr_ready"], now.inc("tr_ready"))

                def head_values(h):
                    pe.wait_ge(Q["tr_done"], base["tr_done"] + TT * (h + 1))
                    values(h, ATT[:, (h % 2) * 4 * S:(h % 2 + 1) * 4 * S].rearrange("p (k q) -> p k q", k=TT))

                drained("gate_ready")
                drained("lin_ready")
                for u in range(ahead):
                    scores(u)
                for u in range(len(jobs)):
                    if u + ahead < len(jobs):
                        scores(u + ahead)
                    fill(u)
                    turn(u)
                    if u % TT == 1 and u > TT:
                        head_values(u // TT - 1)
                head_values(heads - 1)
                now.skip("tr_done", len(jobs))
                now.skip("mx_ready", len(jobs))
                now.skip("e_ready", len(jobs))

            def pair_values(v):
                def run(h, pt):
                    r = slice(64 * (h % 2), 64 * (h % 2) + 64)
                    o = lin_open()
                    for kb in range(TT):
                        mm = pe.matmul(o[r, :], v[:, kb, h * HD:(h + 1) * HD], pt[:, kb, :],
                                       start=kb == 0, stop=kb == TT - 1, skip_group_check=True)
                    mm.then_inc(Q["lin_ready"], now.inc("lin_ready"))
                return run

            def differential():
                def score(o, h, m, qb):
                    r = slice(64 * m, 64 * m + 64)
                    return pe.matmul(o, DAQ[r, h, qb * P:(qb + 1) * P], DAK[r, h, 0:(qb + 1) * P],
                                     start=True, stop=True)

                def values(h, pt):
                    ps = lin_open()
                    for kb in range(TT):
                        mm = pe.matmul(ps[:, kb * P:S], DAV[:, kb, h * P:(h + 1) * P], pt[:, kb, kb * P:S],
                                       start=kb == 0, stop=kb == TT - 1, skip_group_check=True)
                    mm.then_inc(Q["lin_ready"], now.inc("lin_ready"))
                a = {}

                def fill(u):
                    if u in DA_BRANCH:
                        project_tile(a, 4, 512, SBQ, DA_BRANCH.index(u))
                    if u in DA_GATES:
                        project_tile(gates, KD, 256, HT, sum(SB_GATES) + DA_GATES.index(u))
                at[f"da{L}"] = now.count("lin_ready")
                attention(DA_H, score, lambda qb: (qb + 1) * P, 1, 2, values, "mx_ready", fill)
                for m in range(len(DA_BRANCH), KD):
                    project_tile(a, 4, 512, SBQ, m)
                for h in range(DA_H):
                    ps = gate_open()
                    pe.wait_ge(Q["sub_sq"], now.next("sub_sq"))
                    pe.matmul(ps, ONES, ATT[:, h * S:(h + 1) * S], start=True, stop=True)\
                        .then_inc(Q["gate_ready"], now.inc("gate_ready"))

            def branch(src):
                for _ in range(2):
                    project(unit(), 4, 512, src, "lin_ready")

            def moe(L):
                pe.wait_ge(Q["const_landed"], N_CONST)
                for t in range(TT):
                    for k in range(KD):
                        if t == 0:
                            pe.wait_ge(Q["h_ready"], now.next("h_ready"))
                        mm = pe.matmul(PS[:, 4, t * (NG + NE):(t + 1) * (NG + NE)], HT[:, k, t * P:(t + 1) * P],
                                       WR[:, L, k, :], start=(k == 0 and t == 0), stop=k == KD - 1,
                                       skip_group_check=True)
                mm.then_inc(Q["lg_ready"], now.inc("lg_ready"))
                for t in range(TT):
                    for f in range(0, KD, 4):
                        ps = lin_open()
                        for j in range(4):
                            mm = pe.transpose(ps[:, j * P:(j + 1) * P], HT[:, f + j, t * P:(t + 1) * P], IDENT)
                        mm.then_inc(Q["lin_ready"], now.inc("lin_ready"))
                pe.wait_ge(Q["mask_ready"], now.next("mask_ready"))
                M = ATT[:, 0:TT * NE].rearrange("p (t x) -> p t x", t=TT)
                first = True
                for t in range(TT):
                    for s in range(t + 1):
                        mm = pe.matmul(PS[:, 5, t * NE:(t + 1) * NE], BEFORE if s == t else ONES, M[:, s, :],
                                       start=first, stop=s == t, skip_group_check=True)
                        first = False
                for t in range(TT):
                    mm = pe.matmul(PS[:, 5, TT * NE:(TT + 1) * NE], ONES, M[:, t, :],
                                   start=False, stop=t == TT - 1, skip_group_check=True)
                mm.then_inc(Q["rank_ready"], now.inc("rank_ready"))
                pe.wait_ge(Q["pl_landed"], now.next("pl_landed", 16))
                project(unit(), 2, 1024, PLT, "lin_ready")
                drained("lin_ready")
                drained("gate_ready")

                plan.align()
                p0, before = plan.blocks()

                def landed(i, par, j):
                    place = (p0 + 3 * par + j) % RING
                    pe.wait_ge(w_landed[place], i * 16 + 16 * (before[place] + 1))
                    return ring[:, place, :]

                def turn_x(par):
                    g = f"x_gather{par}"
                    pe.wait_ge(Q[g], now.next(g, 16))
                    for k in range(KD):
                        mm = pe.transpose(PSF[:, 1024 + k * P:1024 + (k + 1) * P], XG[:, par, k * P:(k + 1) * P], IDENT)
                    mm.then_inc(Q["x_turned"], now.inc("x_turned"))

                def gate_up(i, par):
                    pe.wait_ge(Q["x_copied"], now.next("x_copied"))
                    landed(i, par, 0)
                    landed(i, par, 1)
                    s = (p0 + 3 * par) % RING
                    for k in range(KD):
                        w = ring[:, s:s + 2, k * EH:(k + 1) * EH]
                        mm = pe.matmul(PS[:, 4 + par, :], XGT[:, par, k * P:(k + 1) * P], w, start=k == 0, stop=k == KD - 1)
                    mm.then_inc(Q["gu_ready"], now.inc("gu_ready"))

                def turn_hidden(par):
                    pe.wait_ge(Q["hid_ready"], now.next("hid_ready"))
                    for j in range(2):
                        mm = pe.transpose(PS[:, 6, j * P:(j + 1) * P], HID[:, par, j * P:(j + 1) * P], IDENT)
                    mm.then_inc(Q["hid_turned"], now.inc("hid_turned"))

                def down(i, par, first=False):
                    w = landed(i, par, 2)
                    pe.wait_ge(Q["hidT_ready"], now.next("hidT_ready"))
                    if not first:
                        pe.wait_ge(Q["y_ready"], now.next("y_ready"))
                    for n in range(2):
                        for j in range(2):
                            mm = pe.matmul(PS[:, n, :], HIDT[:, par, j * P:(j + 1) * P],
                                           w[:, j * D + n * 512:j * D + (n + 1) * 512], start=j == 0, stop=j == 1)
                    mm.then_inc(Q["dn_ready"], now.inc("dn_ready"))

                for par in range(2):
                    for j in range(3):
                        place = (p0 + 3 * par + j) % RING
                        name = "dn_ready" if j == 2 else "gu_ready"
                        used[(place, plan.fills[place])] = (name, now.count(name) + NB - par)
                at[f"moe{L}"] = {n: now.count(n) for n in ("gu_ready", "dn_ready", "x_turned")}
                turn_x(0)
                gate_up(0, 0)
                turn_x(1)
                turn_hidden(0)
                gate_up(0, 1)
                turn_x(0)
                down(0, 0, first=True)
                turn_hidden(1)
                gate_up(1, 0)
                turn_x(1)
                down(0, 1)
                per = dict(x_gather0=16, x_gather1=16, x_turned=2, x_copied=2, gu_ready=2, hid_ready=2,
                           hid_turned=2, hidT_ready=2, dn_ready=2, y_ready=2)
                turns = (NB - 3) // 2
                with pe.Fori(0, turns) as i:
                    now.enter(i, per)
                    turn_hidden(0)
                    gate_up(i + 1, 1)
                    turn_x(0)
                    down(i + 1, 0)
                    turn_hidden(1)
                    gate_up(i + 2, 0)
                    turn_x(1)
                    down(i + 1, 1)
                now.leave(turns)
                turn_hidden(0)
                down((NB - 1) // 2, 0)
                pe.wait_ge(Q["y_ready"], now.next("y_ready"))
                pe.wait_ge(Q["x_copied"], now.next("x_copied"))
                pe.wait_ge(Q["comb_ready"], now.next("comb_ready", TT))
                for f in range(KD):
                    ps = lin_open()
                    for t in range(TT):
                        mm = pe.transpose(ps[:, t * P:(t + 1) * P], COMB[:, t, f * P:(f + 1) * P], IDENT)
                    mm.then_inc(Q["lin_ready"], now.inc("lin_ready"))

            def ffn():
                norm_sum(KD)
                at[f"ffn{st.setdefault('ffn', 0)}"] = now.count("lin_ready")
                st["ffn"] += 1
                for c in range(KF // 2):
                    for j in range(2):
                        w = unit()
                        wv = w.rearrange("p (k c) -> p k c", k=KD)
                        for m in range(2):
                            name = ("gate_ready", "lin_ready")[j]
                            ps = opened[name]()
                            for k in range(KD):
                                if c == 0 and j == 0 and m == 0:
                                    pe.wait_ge(Q["h_ready"], now.next("h_ready"))
                                mm = pe.matmul(ps, wv[:, k, m * P:(m + 1) * P], HT[:, k, :],
                                               start=k == 0, stop=k == KD - 1)
                            mm.then_inc(Q[name], now.inc(name))
                        unit_used(name)
                drained("lin_ready")
                for c in range(4):
                    tiles, units = [], []
                    for q in range(3):
                        w = unit()
                        units.append(st["unit"])
                        nk = min(KD, KF - q * KD)
                        wv = w[:, 0:nk * 256].rearrange("p (k c) -> p k c", k=nk)
                        for m in range(2):
                            if q == 0:
                                t = now.count("lin_ready") + m
                                if t >= 2:
                                    pe.wait_ge(Q["lin_free"], t - 1)
                                tiles.append(PS[:, t % 2, :])
                            for k in range(nk):
                                mm = pe.matmul(tiles[m], wv[:, k, m * P:(m + 1) * P], BIG[:, q * KD + k, :],
                                               start=(q == 0 and k == 0), stop=(q == 2 and k == nk - 1),
                                               skip_group_check=True)
                            if q == 2:
                                mm.then_inc(Q["lin_ready"], now.inc("lin_ready"))
                    for x in units:
                        unit_used("lin_ready", x)
                norm_sum(KD)

            pe.wait_ge(Q["x_landed"], X_LANDED)
            for L in range(LAYERS):
                norm_sum(KD)
                for n in range(4):
                    project(unit(), KD, 256, HT, "lin_ready", h_wait=n == 0)
                for n in range(2):
                    project_tokens(unit(), KD, 256, HT)
                for n in range(4):
                    project(unit(), KD, 256, HT, "lin_ready")
                qk = now.count("lin_ready")
                for n in range(2):
                    project_tokens(unit(), KD, 256, HT)
                pe.wait_ge(Q["lin_free"], qk)
                rotate([DAQ[:, t, :] for t in range(4)] + [DAK[:, t, :] for t in range(4)], ROT)
                stick_breaking()
                differential()
                pe.wait_ge(Q["sub_ready"], now.next("sub_ready", DA_H))
                branch(DAQ)
                drained("lin_ready")
                for n in range(4):
                    project(unit(), KD, 256, HT, "lin_ready")
                norm_sum(KD)
                moe(L)
                norm_sum(KD)
                for n in range(4):
                    project(unit(), KD, 256, HP, "gate_ready", h_wait=n == 0)
            norm_sum(KD)
            ffn()
            norm_sum(KD)
            project(unit(), KD, 256, HT, "lin_ready", h_wait=True)
            project(unit(), KD, 128, HT, "lin_ready")
            project(unit(), KD, 256, HT, "lin_ready")
            project(unit(), KD, 96, HT, "lin_ready", m=96)
            for n in range(4):
                project(unit(), KD, 256, HT, "lin_ready")
            qk = now.count("lin_ready")
            for n in range(2):
                project_tokens(unit(), KD, 256, HT)
            pe.wait_ge(Q["lin_free"], qk)
            rotate([DQ[:, t, :] for t in range(4)] + [DK[:, t, :] for t in range(4)], ROT)
            rotate([KR], ROTM, DQK)
            norm_sum(QR // P)
            norm_sum(KVR // P)

            def dil_score(o, h, m, qb):
                r = slice(64 * (h % 2), 64 * (h % 2) + 64)
                return pe.matmul(o, DQ[r, h // 2, qb * P:(qb + 1) * P], DK[r, h // 2, :], start=True, stop=True)

            def gate_fill(u):
                if u % 2:
                    project_tile(gates, KD, 256, HT, u // 2)
            at["dil"] = now.count("lin_ready")
            attention(MLA_H, dil_score, lambda qb: S, 2, 1, pair_values(DV), "mx_ready", gate_fill)
            pe.wait_ge(Q["h_ready"], now.next("h_ready", (QR + KVR) // P))
            for n in range(2):
                project(unit(), 3, 384, CQ, "lin_ready", m=96)
            drained("lin_ready")
            rotate([HT[0:DQK, h, :] for h in range(MLA_H)], ROTM, DQK)
            project(unit(), 2, 512, CKV, "lin_ready")
            project_tokens(unit(), 2, 512, CKV)
            pe.wait_ge(Q["kr_copied"], now.next("kr_copied", MLA_H))

            def mla_score(o, h, m, qb):
                return pe.matmul(o, HT[0:DQK, h, qb * P:(qb + 1) * P], KT[0:DQK, h, :], start=True, stop=True)

            b = {}

            def branch_fill(u):
                if u % 4 == 3:
                    project_tile(b, 4, 512, DQ, u // 4)
            at["mla"] = now.count("lin_ready")
            attention(MLA_H, mla_score, lambda qb: S, 2, 1, pair_values(VA), "e_ready", branch_fill)
            drained("lin_ready")
            branch(HT[:, 0:4, :])
            drained("lin_ready")
            for n in range(4):
                project(unit(), KD, 256, MB, "lin_ready")
            norm_sum(KD)
            ffn()
            at["pe"] = dict(now.n)

        @block.vector
        def _(v):
            now = Counts()
            st = {"norm": 0}

            def lin_take():
                t = now.count("lin_ready")
                v.wait_ge(Q["lin_ready"], now.next("lin_ready"))
                return PS[:, t % 2, :]

            def gate_tile():
                t = now.count("gate_ready")
                v.wait_ge(Q["gate_ready"], now.next("gate_ready"))
                return PS[:, 2 + t % 2, :]

            def begin_sum(source, nt=0):
                at[f"norm{st['norm']}"] = (source, now.count(source) - nt)
                st["norm"] += 1
                st["summed"] = 0

            def sum_square():
                k = st["summed"]
                st["summed"] += 1
                v.wait_ge(Q["sq_ready"], now.next("sq_ready"))
                if k == 0:
                    v.wait_ge(*now.prev())
                    v.tensor_copy(ACC, SQ[:, 0, :]).then_inc(Q["sq_used"], now.inc("sq_used"))
                else:
                    v.wait_ge(*now.prev())
                    v.tensor_tensor(ACC, ACC, SQ[:, k % 2, :], ALU.add).then_inc(Q["sq_used"], now.inc("sq_used"))

            def norm(src, nt, gain, dst=None, name="h_ready", add=None, then_sum=False):
                while st["summed"] < nt:
                    sum_square()
                now.skip("gate_ready")
                now.skip("gate_free")
                v.wait_ge(Q["rstd_ready"], now.next("rstd_ready"))
                if then_sum:
                    begin_sum("x_ready")
                for k in range(nt):
                    g = GC[:, GCOL[gain] + k:GCOL[gain] + k + 1]
                    if add is None:
                        v.wait_ge(*now.prev())
                        v.scalar_tensor_tensor(out=dst[:, k, :], in0=src[:, k, :], scalar=g, in1=RSTD[:, :],
                                               op0=ALU.mult, op1=ALU.mult)\
                            .then_inc(Q[name], now.inc(name))
                        if then_sum and k:
                            sum_square()
                    else:
                        v.wait_ge(*now.prev())
                        v.scalar_tensor_tensor(out=TMP[:, 0, :], in0=src[:, k, :], scalar=g, in1=RSTD[:, :],
                                               op0=ALU.mult, op1=ALU.mult)\
                            .then_inc(Q["dve_step"], now.inc("dve_step"))
                        v.wait_ge(*now.prev())
                        v.scalar_tensor_tensor(out=XT[:, k, :], in0=TMP[:, 0, :], scalar=add, in1=XT[:, k, :],
                                               op0=ALU.mult, op1=ALU.add)\
                            .then_inc(Q["x_ready"], now.inc("x_ready"))
                        if then_sum and k:
                            sum_square()

            def store(dst, n, rows=P, scale=None, then_sum=False):
                if then_sum:
                    begin_sum("lin_free")
                for k in range(n):
                    ps = lin_take()
                    if scale is None:
                        v.wait_ge(*now.prev())
                        v.tensor_copy(dst[0:rows, k, :], ps[0:rows, :]).then_inc(Q["lin_free"], now.inc("lin_free"))
                    else:
                        v.wait_ge(*now.prev())
                        v.tensor_scalar(dst[0:rows, k, :], ps[0:rows, :], scale, None, ALU.mult)\
                            .then_inc(Q["lin_free"], now.inc("lin_free"))
                    if then_sum and k:
                        sum_square()

            def store_tokens(dst, units, width):
                for n in range(units):
                    for t in range(TT):
                        ps = lin_take()
                        v.wait_ge(*now.prev())
                        v.tensor_copy(dst[:, t, n * width:(n + 1) * width], ps[:, 0:width])\
                            .then_inc(Q["lin_free"], now.inc("lin_free"))

            def rope(tiles, cos, sin, rows=P):
                for t in tiles:
                    ps = lin_take()
                    v.wait_ge(*now.prev())
                    v.tensor_tensor(TMP[0:rows, 0, :], ps[0:rows, :], sin[0:rows, :], ALU.mult)\
                        .then_inc(Q["dve_step"], now.inc("dve_step"))
                    v.wait_ge(*now.prev())
                    v.tensor_tensor(t, t, cos[0:rows, :], ALU.mult).then_inc(Q["dve_step"], now.inc("dve_step"))
                    v.wait_ge(*now.prev())
                    v.tensor_tensor(t, t, TMP[0:rows, 0, :], ALU.add).then_inc(Q["lin_free"], now.inc("lin_free"))

            def trig(cos, sin, col):
                two_pi = 2 * math.pi
                c1 = 6.28125
                c2 = float(np.float32(np.float32((two_pi - c1) * 2 ** 20).astype(np.int32) / 2 ** 20))
                c3 = two_pi - c1 - c2
                big = 12582912.0
                v.wait_ge(*now.prev())
                v.tensor_copy(cos, sin.bitcast(I32)).then_inc(Q["dve_step"], now.inc("dve_step"))
                v.wait_ge(*now.prev())
                v.tensor_scalar(TMP[:, 0, :], cos, FREQ[:, col:col + 1], None, ALU.mult)\
                    .then_inc(Q["dve_step"], now.inc("dve_step"))
                v.wait_ge(*now.prev())
                v.tensor_scalar(TMP[:, 1, :], TMP[:, 0, :], 1.0 / two_pi, None, ALU.mult)\
                    .then_inc(Q["dve_step"], now.inc("dve_step"))
                v.wait_ge(*now.prev())
                v.tensor_scalar(TMP[:, 1, :], TMP[:, 1, :], big, None, ALU.add)\
                    .then_inc(Q["dve_step"], now.inc("dve_step"))
                v.wait_ge(*now.prev())
                v.tensor_scalar(TMP[:, 1, :], TMP[:, 1, :], -big, None, ALU.add)\
                    .then_inc(Q["dve_step"], now.inc("dve_step"))
                for c in (c1, c2, c3):
                    v.wait_ge(*now.prev())
                    v.scalar_tensor_tensor(out=TMP[:, 0, :], in0=TMP[:, 1, :], scalar=-c, in1=TMP[:, 0, :],
                                           op0=ALU.mult, op1=ALU.add)\
                        .then_inc(Q["dve_step"], now.inc("dve_step"))
                v.wait_ge(*now.prev())
                v.tensor_scalar(TMP[:, 0, :], TMP[:, 0, :], 3.1415925, -3.1415925, ALU.min, ALU.max)\
                    .then_inc(Q["ang_ready"], now.inc("ang_ready"))
                v.wait_ge(Q["trig_ready"], now.next("trig_ready"))

            def sigmoid_tail(k):
                v.wait_ge(Q["gate_ready"], now.next("gate_ready"))
                v.wait_ge(Q["gate_free"], now.next("gate_free"))
                v.wait_ge(*now.prev())
                v.tensor_scalar(G[:, k, :], G[:, k, :], 1.0, None, ALU.add)\
                    .then_inc(Q["dve_step"], now.inc("dve_step"))
                v.wait_ge(*now.prev())
                v.reciprocal(G[:, k, :], G[:, k, :]).then_inc(Q["dve_step"], now.inc("dve_step"))

            def take_gate(k):
                ps = lin_take()
                v.wait_ge(*now.prev())
                v.tensor_copy(G[:, k, :], ps).then_inc(Q["lin_free"], now.inc("lin_free"))

            def sigmoid(k):
                v.wait_ge(Q["g_exp"], now.next("g_exp"))
                v.wait_ge(*now.prev())
                v.tensor_scalar(G[:, k, :], G[:, k, :], 1.0, None, ALU.add)\
                    .then_inc(Q["dve_step"], now.inc("dve_step"))
                v.wait_ge(*now.prev())
                v.reciprocal(G[:, k, :], G[:, k, :]).then_inc(Q["dve_step"], now.inc("dve_step"))

            def next_sigmoid():
                sigmoid(st["sigmoid"])
                st["sigmoid"] += 1

            def first_branch(dst, k, gate):
                ps = lin_take()
                v.wait_ge(*now.prev())
                v.tensor_tensor(dst[:, k, :], ps, G[:, gate, :], ALU.mult).then_inc(Q["lin_free"], now.inc("lin_free"))

            def second_branch(dst, k, gate):
                ps = lin_take()
                v.wait_ge(*now.prev())
                v.tensor_tensor(TMP[:, 0, :], ps, G[:, gate, :], ALU.mult)\
                    .then_inc(Q["dve_step"], now.inc("dve_step"))
                v.wait_ge(*now.prev())
                v.tensor_tensor(dst[:, k, :], dst[:, k, :], TMP[:, 0, :], ALU.add)\
                    .then_inc(Q["lin_free"], now.inc("lin_free"))

            def add_to_x():
                begin_sum("lin_free")
                for k in range(KD):
                    ps = lin_take()
                    v.wait_ge(*now.prev())
                    v.tensor_tensor(XT[:, k, :], ps, XT[:, k, :], ALU.add).then_inc(Q["lin_free"], now.inc("lin_free"))
                    if k:
                        sum_square()

            def stick_breaking():
                base = now.count("lw_ready")
                at_sp = now.count("sp_masked")

                def softplus(h):
                    z = (2 + 3 * (h % 2)) * 512
                    v.wait_ge(Q["z_ready"], now.next("z_ready"))
                    v.wait_ge(Q["soft_ready"], now.next("soft_ready"))
                    if h >= 2:
                        v.wait_ge(Q["lw_ready"], base + h - 1)
                    sp = ATT[:, (1280 * (1 + h % 2)):(1280 * (2 + h % 2))]
                    v.wait_ge(*now.prev())
                    v.scalar_tensor_tensor(out=sp, in0=PSF[:, z:z + 1280], scalar=0.0, in1=ATT[:, 0:1280],
                                           op0=ALU.max, op1=ALU.add)\
                        .then_inc(Q["sp_ready"], now.inc("sp_ready"))

                def suffix(h):
                    sp = ATT[:, (1280 * (1 + h % 2)):(1280 * (2 + h % 2))]
                    rd = ATT[:, 6400:6784]
                    v.wait_ge(Q["sp_masked"], now.next("sp_masked"))
                    if h >= 1:
                        v.wait_ge(Q["lw_ready"], base + h)
                    v.wait_ge(*now.prev())
                    v.tensor_tensor(rd[:, 0:256], sp[:, 640:896], sp[:, 256:512], ALU.add)\
                        .then_inc(Q["dve_step"], now.inc("dve_step"))
                    v.wait_ge(*now.prev())
                    v.tensor_tensor(rd[:, 256:384], sp[:, 1152:1280], rd[:, 128:256], ALU.add)\
                        .then_inc(Q["suffix_ready"], now.inc("suffix_ready"))

                def take_head(h):
                    r = slice(64 * (h % 2), 64 * (h % 2) + 64)
                    ps = lin_take()
                    v.wait_ge(*now.prev())
                    v.tensor_copy(SBQ[r, h // 2, :], ps[r, :]).then_inc(Q["lin_free"], now.inc("lin_free"))

                softplus(0)
                suffix(0)
                for h in range(SB_H):
                    if h >= 2:
                        next_sigmoid()
                    if h + 1 < SB_H:
                        softplus(h + 1)
                    take_gate(sum(SB_GATES[:h]))
                    if h + 1 < SB_H:
                        suffix(h + 1)
                    if SB_GATES[h] == 2:
                        take_gate(sum(SB_GATES[:h]) + 1)
                    if h >= 1:
                        take_head(h - 1)
                    if h >= 2 and SB_GATES[h - 2] == 2:
                        next_sigmoid()
                take_head(SB_H - 1)
                now.skip("lw_ready", SB_H)

            def attention(heads, nkeys, maps, scale, mask, L, head_done, take_fill, between=lambda u: None):
                jobs = [(h, qb) for h in range(heads) for qb in range(TT)]
                tr0 = now.count("tr_ready")
                slots = 4 // maps

                def maxima(u):
                    h, qb = jobs[u]
                    n = nkeys(qb)
                    s = SM[:, 8 * (u % 2):8 * (u % 2) + 8]
                    v.wait_ge(Q["sc_ready"], now.next("sc_ready"))
                    for m in range(maps):
                        ps = PS[:, 4 + (u % slots) * maps + m, 0:n]
                        if mask is None:
                            v.wait_ge(*now.prev())
                            v.tensor_reduce(s[:, m:m + 1], ps, AX, ALU.max).then_inc(Q["dve_step"], now.inc("dve_step"))
                        else:
                            if u >= 2:
                                v.wait_ge(Q["tr_ready"], tr0 + u - 1)
                            x = E_[:, ((u % 2) * maps + m) * S:((u % 2) * maps + m) * S + n]
                            v.wait_ge(*now.prev())
                            v.tensor_tensor_reduce(out=x, in0=ps, in1=mask(qb), scale=1.0, scalar=-3e38,
                                                   op0=ALU.add, op1=ALU.max, accum_out=s[:, m:m + 1])\
                                .then_inc(Q["dve_step"], now.inc("dve_step"))
                    v.wait_ge(*now.prev())
                    v.tensor_scalar(s[:, 0:maps], s[:, 0:maps], -scale, None, ALU.mult)\
                        .then_inc(Q["mx_ready"], now.inc("mx_ready"))

                def normalise(u):
                    h, qb = jobs[u]
                    n = nkeys(qb)
                    s = SM[:, 8 * (u % 2):8 * (u % 2) + 8]
                    x = [E_[:, ((u % 2) * maps + m) * S:((u % 2) * maps + m) * S + n] for m in range(maps)]
                    v.wait_ge(Q["e_ready"], now.next("e_ready"))
                    v.wait_ge(*now.prev())
                    v.reciprocal(s[:, 4:4 + maps], s[:, 2:2 + maps]).then_inc(Q["dve_step"], now.inc("dve_step"))
                    if maps == 1:
                        v.wait_ge(*now.prev())
                        v.tensor_scalar(x[0], x[0], s[:, 4:5], None, ALU.mult)\
                            .then_inc(Q["p_ready"], now.inc("p_ready"))
                    else:
                        v.wait_ge(*now.prev())
                        v.tensor_tensor(s[:, 5:6], s[:, 5:6], LAM[:, L:L + 1], ALU.mult)\
                            .then_inc(Q["dve_step"], now.inc("dve_step"))
                        v.wait_ge(*now.prev())
                        v.tensor_scalar(x[0], x[0], s[:, 4:5], None, ALU.mult)\
                            .then_inc(Q["dve_step"], now.inc("dve_step"))
                        v.wait_ge(*now.prev())
                        v.scalar_tensor_tensor(out=x[0], in0=x[1], scalar=s[:, 5:6], in1=x[0], op0=ALU.mult,
                                               op1=ALU.add)\
                            .then_inc(Q["p_ready"], now.inc("p_ready"))

                maxima(0)
                def take_done(u):
                    if u:
                        take_fill(u - 1)
                    if u % TT == 2 and u > TT:
                        head_done(u // TT - 1)

                for u in range(len(jobs)):
                    if maps == 2:
                        take_done(u)
                    if u + 1 < len(jobs):
                        maxima(u + 1)
                    normalise(u)
                    if maps == 1:
                        take_done(u)
                    between(u)
                take_fill(len(jobs) - 1)
                head_done(heads - 1)
                now.skip("tr_ready", len(jobs))

            def pair_done(dst):
                def run(h):
                    r = slice(64 * (h % 2), 64 * (h % 2) + 64)
                    ps = lin_take()
                    v.wait_ge(*now.prev())
                    v.tensor_copy(dst[r, h // 2, :], ps[r, :]).then_inc(Q["lin_free"], now.inc("lin_free"))
                return run

            def moe(L):
                r = {k: a for k, a in RT.items()}
                v3 = lambda a, t: a.rearrange("p (t x) -> p t x", t=t)
                v.wait_ge(Q["lg_ready"], now.next("lg_ready"))
                lg = v3(r["logit"], TT)
                for t in range(TT):
                    v.wait_ge(*now.prev())
                    v.tensor_tensor(lg[:, t, :], PS[:, 4, t * (NG + NE):(t + 1) * (NG + NE)], BR[:, L, :], ALU.add)\
                        .then_inc(Q["dve_step"], now.inc("dve_step"))
                gl, el = lg[:, :, 0:NG], lg[:, :, NG:NG + NE]
                wide = lambda a, n: a.unsqueeze(2).to_broadcast([P, TT, n])
                v.wait_ge(*now.prev())
                v.tensor_reduce(r["gmax"], gl, AX, ALU.max).then_inc(Q["dve_step"], now.inc("dve_step"))
                v.wait_ge(*now.prev())
                v.tensor_tensor(v3(r["ge"][:, 0:16], TT), gl, wide(r["gmax"], NG), ALU.subtract)\
                    .then_inc(Q["dve_step"], now.inc("dve_step"))
                v.wait_ge(*now.prev())
                v.tensor_tensor(v3(r["eq"], TT), gl, wide(r["gmax"], NG), ALU.is_ge)\
                    .then_inc(Q["dve_step"], now.inc("dve_step"))
                v.wait_ge(*now.prev())
                v.tensor_tensor(v3(r["eq"], TT), v3(r["eq"], TT),
                                REV[:, 0:NG].unsqueeze(1).to_broadcast([P, TT, NG]), ALU.mult)\
                    .then_inc(Q["dve_step"], now.inc("dve_step"))
                v.wait_ge(*now.prev())
                v.tensor_reduce(r["s4"], v3(r["eq"], TT), AX, ALU.max).then_inc(Q["dve_step"], now.inc("dve_step"))
                v.wait_ge(*now.prev())
                v.tensor_tensor(v3(r["pen"], TT), v3(r["eq"], TT), wide(r["s4"], NG), ALU.is_ge)\
                    .then_inc(Q["dve_step"], now.inc("dve_step"))
                v.wait_ge(*now.prev())
                v.tensor_scalar(r["pen"], r["pen"], 1e30, -1e30, ALU.mult, ALU.add)\
                    .then_inc(Q["dve_step"], now.inc("dve_step"))
                for t in range(TT):
                    em = el[:, t, :].rearrange("p (g x) -> p g x", g=NG)
                    pen = v3(r["pen"], TT)[:, t, :]
                    v.wait_ge(*now.prev())
                    v.tensor_tensor(em, em, pen.unsqueeze(2).to_broadcast([P, NG, NEG_]), ALU.add)\
                        .then_inc(Q["dve_step"], now.inc("dve_step"))
                rev = REV[:, NG:NG + NE].unsqueeze(1).to_broadcast([P, TT, NE])
                for mx, one in (("m1", "one1"), ("m2", "one2")):
                    o = v3(r[one], TT)
                    v.wait_ge(*now.prev())
                    v.tensor_reduce(r[mx], el, AX, ALU.max).then_inc(Q["dve_step"], now.inc("dve_step"))
                    v.wait_ge(*now.prev())
                    v.tensor_tensor(o, el, wide(r[mx], NE), ALU.is_ge).then_inc(Q["dve_step"], now.inc("dve_step"))
                    v.wait_ge(*now.prev())
                    v.tensor_tensor(o, o, rev, ALU.mult).then_inc(Q["dve_step"], now.inc("dve_step"))
                    v.wait_ge(*now.prev())
                    v.tensor_reduce(r["s4"], o, AX, ALU.max).then_inc(Q["dve_step"], now.inc("dve_step"))
                    v.wait_ge(*now.prev())
                    v.tensor_tensor(o, o, wide(r["s4"], NE), ALU.is_ge).then_inc(Q["dve_step"], now.inc("dve_step"))
                    if one == "one1":
                        for t in range(TT):
                            v.wait_ge(*now.prev())
                            v.scalar_tensor_tensor(out=el[:, t, :], in0=o[:, t, :], scalar=-3e30, in1=el[:, t, :],
                                                   op0=ALU.mult, op1=ALU.add)\
                                .then_inc(Q["dve_step"], now.inc("dve_step"))
                v.wait_ge(*now.prev())
                v.tensor_tensor(r["mask"], r["one1"], r["one2"], ALU.add)\
                    .then_inc(Q["mask_ready"], now.inc("mask_ready"))
                v.wait_ge(*now.prev())
                v.tensor_tensor(r["ge"][:, 16:20], r["m2"], r["m1"], ALU.subtract)\
                    .then_inc(Q["route_exp"], now.inc("route_exp"))
                for t in range(TT):
                    for f in range(2):
                        ps = lin_take()
                        v.wait_ge(*now.prev())
                        v.tensor_copy(HTOK[:, t, f * 512:(f + 1) * 512], ps)\
                            .then_inc(Q["lin_free"], now.inc("lin_free"))
                at[f"htok{L}"] = now.count("lin_free")
                v.wait_ge(Q["table_landed"], now.next("table_landed"))
                v.wait_ge(*now.prev())
                v.tensor_reduce(r["gsum"], v3(r["ge"][:, 0:16], TT), AX, ALU.add)\
                    .then_inc(Q["dve_step"], now.inc("dve_step"))
                v.wait_ge(*now.prev())
                v.tensor_scalar(r["s4"], r["ge"][:, 16:20], 1.0, None, ALU.add)\
                    .then_inc(Q["dve_step"], now.inc("dve_step"))
                v.wait_ge(*now.prev())
                v.tensor_tensor(r["gsum"], r["gsum"], r["s4"], ALU.mult).then_inc(Q["dve_step"], now.inc("dve_step"))
                gate = r["gate"].rearrange("p (t c) -> p t c", c=2)
                v.wait_ge(*now.prev())
                v.reciprocal(gate[:, :, 0], r["gsum"]).then_inc(Q["dve_step"], now.inc("dve_step"))
                v.wait_ge(*now.prev())
                v.tensor_tensor(gate[:, :, 1], gate[:, :, 0], r["ge"][:, 16:20], ALU.mult)\
                    .then_inc(Q["dve_step"], now.inc("dve_step"))
                v.wait_ge(Q["rank_ready"], now.next("rank_ready"))
                v.wait_ge(*now.prev())
                v.tensor_copy(r["rank"], PS[:, 5, 0:TT * NE]).then_inc(Q["dve_step"], now.inc("dve_step"))
                v.wait_ge(*now.prev())
                v.tensor_copy(r["cnt"], PS[:, 5, TT * NE:(TT + 1) * NE]).then_inc(Q["dve_step"], now.inc("dve_step"))
                v.wait_ge(*now.prev())
                v.tensor_scalar(r["nblk"], r["cnt"], 0.5, None, ALU.is_gt).then_inc(Q["dve_step"], now.inc("dve_step"))
                for j in range(1, TT):
                    v.wait_ge(*now.prev())
                    v.scalar_tensor_tensor(out=r["nblk"], in0=r["cnt"], scalar=j * CAP + 0.5, in1=r["nblk"],
                                           op0=ALU.is_gt, op1=ALU.add)\
                        .then_inc(Q["dve_step"], now.inc("dve_step"))
                v.wait_ge(*now.prev())
                v.tensor_scalar(r["one32"], r["cnt"], 0.0, None, ALU.mult).then_inc(Q["dve_step"], now.inc("dve_step"))
                v.wait_ge(*now.prev())
                v.tensor_tensor_scan(r["end"], r["nblk"], r["one32"], 0.0, ALU.add, ALU.add)\
                    .then_inc(Q["dve_step"], now.inc("dve_step"))
                cmp = r["cmp"][0:1, :].rearrange("p (b x) -> p b x", b=NB)
                v.wait_ge(*now.prev())
                v.tensor_tensor(cmp, BLK[0:1, :].unsqueeze(2).to_broadcast([1, NB, NE]),
                                r["end"][0:1, :].unsqueeze(1).to_broadcast([1, NB, NE]), ALU.is_ge)\
                    .then_inc(Q["dve_step"], now.inc("dve_step"))
                v.wait_ge(*now.prev())
                v.tensor_reduce(r["blkf"][0:1, :], cmp, AX, ALU.add).then_inc(Q["dve_step"], now.inc("dve_step"))
                v.wait_ge(*now.prev())
                v.tensor_scalar(r["blkf"][0:1, :], r["blkf"][0:1, :], float(NE - 1), None, ALU.min)\
                    .then_inc(Q["dve_step"], now.inc("dve_step"))
                v.wait_ge(*now.prev())
                v.tensor_copy(r["blki"][0:1, :].bitcast(I32), r["blkf"][0:1, :])\
                    .then_inc(Q["blk_ready"], now.inc("blk_ready"))
                v.wait_ge(*now.prev())
                v.tensor_tensor(r["end"], r["end"], r["nblk"], ALU.subtract)\
                    .then_inc(Q["dve_step"], now.inc("dve_step"))
                rank, over = r["rank"], r["over"]
                v.wait_ge(*now.prev())
                v.tensor_scalar(over, rank, CAP - 0.5, None, ALU.is_gt).then_inc(Q["dve_step"], now.inc("dve_step"))
                for j in range(2, TT):
                    v.wait_ge(*now.prev())
                    v.scalar_tensor_tensor(out=over, in0=rank, scalar=j * CAP - 0.5, in1=over, op0=ALU.is_gt,
                                           op1=ALU.add)\
                        .then_inc(Q["dve_step"], now.inc("dve_step"))
                start = r["end"].unsqueeze(1).to_broadcast([P, TT, NE])
                v.wait_ge(*now.prev())
                v.tensor_scalar(over, over, float(1 - CAP * NBP), None, ALU.mult)\
                    .then_inc(Q["dve_step"], now.inc("dve_step"))
                v.wait_ge(*now.prev())
                v.scalar_tensor_tensor(out=over, in0=rank, scalar=float(NBP), in1=over, op0=ALU.mult, op1=ALU.add)\
                    .then_inc(Q["dve_step"], now.inc("dve_step"))
                v.wait_ge(*now.prev())
                v.tensor_tensor(v3(over, TT), v3(over, TT), start, ALU.add).then_inc(Q["dve_step"], now.inc("dve_step"))
                for t in range(TT):
                    v.wait_ge(*now.prev())
                    v.scalar_tensor_tensor(out=v3(rank, TT)[:, t, :], in0=r["end"], scalar=float(CAP),
                                           in1=v3(rank, TT)[:, t, :], op0=ALU.mult, op1=ALU.add)\
                        .then_inc(Q["dve_step"], now.inc("dve_step"))
                for val, dst, ints in ((rank, "sum8", "sloti"), (over, "adr", "adri")):
                    d = r[dst].rearrange("p (t c) -> p t c", c=2)
                    for c, one in enumerate(("one1", "one2")):
                        v.wait_ge(*now.prev())
                        v.tensor_tensor(r["tmp"], val, r[one], ALU.mult).then_inc(Q["dve_step"], now.inc("dve_step"))
                        v.wait_ge(*now.prev())
                        v.tensor_reduce(d[:, :, c], v3(r["tmp"], TT), AX, ALU.add)\
                            .then_inc(Q["dve_step"], now.inc("dve_step"))
                    v.wait_ge(*now.prev())
                    v.tensor_copy(r[ints].bitcast(I32), r[dst])\
                        .then_inc(Q["dve_step" if ints == "sloti" else "slots_ready"], now.inc("dve_step" if ints == "sloti" else "slots_ready"))

                store(HT, KD)

                y0 = [now.count("y_store0"), now.count("y_store1")]

                def turned_hidden(par):
                    v.wait_ge(Q["hid_turned"], now.next("hid_turned"))
                    v.wait_ge(*now.prev())
                    v.tensor_copy(HIDT[:, par, :], PS[:, 6, 0:256]).then_inc(Q["hidT_ready"], now.inc("hidT_ready"))

                def hidden(par):
                    v.wait_ge(Q["gu_ready"], now.next("gu_ready"))
                    v.wait_ge(Q["e_gate"], now.next("e_gate"))
                    h = HID[:, par, :]
                    v.wait_ge(*now.prev())
                    v.tensor_scalar(h, h, 1.0, None, ALU.add).then_inc(Q["dve_step"], now.inc("dve_step"))
                    v.wait_ge(*now.prev())
                    v.reciprocal(h, h).then_inc(Q["dve_step"], now.inc("dve_step"))
                    v.wait_ge(*now.prev())
                    v.tensor_tensor(h, PS[:, 4 + par, 0:EH], h, ALU.mult).then_inc(Q["dve_step"], now.inc("dve_step"))
                    v.wait_ge(*now.prev())
                    v.tensor_tensor(h, PS[:, 4 + par, EH:2 * EH], h, ALU.mult)\
                        .then_inc(Q["hid_ready"], now.inc("hid_ready"))

                def rows(par, before):
                    v.wait_ge(Q["dn_ready"], now.next("dn_ready"))
                    if before is not None:
                        v.wait_ge(Q[f"y_store{par}"], before * 16 + y0[par])
                    v.wait_ge(*now.prev())
                    v.tensor_copy(YB[:, par, :], PSF[:, 0:D]).then_inc(Q["y_ready"], now.inc("y_ready"))

                hidden(0)
                turned_hidden(0)
                hidden(1)
                rows(0, None)
                turned_hidden(1)
                hidden(0)
                rows(1, None)
                turns = (NB - 3) // 2
                with v.Fori(0, turns) as i:
                    now.enter(i, dict(hid_turned=2, hidT_ready=2, gu_ready=2, e_gate=2, hid_ready=2, dve_step=6,
                                    dn_ready=2, y_ready=2))
                    turned_hidden(0)
                    hidden(1)
                    rows(0, i + 1)
                    turned_hidden(1)
                    hidden(0)
                    rows(1, i + 1)
                now.leave(turns)
                turned_hidden(0)
                rows(0, (NB - 1) // 2)
                now.skip("y_store0", 16 * ((NB + 1) // 2))
                now.skip("y_store1", 16 * (NB // 2))
                if L == LAYERS - 1:
                    v.wait_ge(Q["pos2_landed"], now.next("pos2_landed", 48))
                    trig(COS[:, :], SIN[:, :], 1)
                    trig(COSM, SINM, 2)
                for t in range(TT):
                    v.wait_ge(Q[f"y_gathered{t}"], now.next(f"y_gathered{t}", 32))
                    v.wait_ge(*now.prev())
                    v.tensor_scalar(COMB[:, t, :], YG[:, 2 * t, :], r["gate"][:, 2 * t:2 * t + 1], None, ALU.mult)\
                        .then_inc(Q["dve_step"], now.inc("dve_step"))
                    v.wait_ge(*now.prev())
                    v.scalar_tensor_tensor(out=COMB[:, t, :], in0=YG[:, 2 * t + 1, :],
                                           scalar=r["gate"][:, 2 * t + 1:2 * t + 2], in1=COMB[:, t, :],
                                           op0=ALU.mult, op1=ALU.add)\
                        .then_inc(Q["comb_ready"], now.inc("comb_ready"))
                add_to_x()

            def ffn(pre, post, then_sum):
                norm(XT, KD, pre, HT)
                for c in range(0, KF, 2):
                    for m in range(2):
                        k = c + m
                        a = A3[:, 3 + k % 2, :]
                        g = gate_tile()
                        v.wait_ge(Q["e_gate"], now.next("e_gate"))
                        v.wait_ge(*now.prev())
                        v.tensor_scalar(a, a, 1.0, None, ALU.add).then_inc(Q["dve_step"], now.inc("dve_step"))
                        v.wait_ge(*now.prev())
                        v.reciprocal(a, a).then_inc(Q["dve_step"], now.inc("dve_step"))
                        v.wait_ge(*now.prev())
                        v.tensor_tensor(a, g, a, ALU.mult).then_inc(Q["gate_free"], now.inc("gate_free"))
                        u = lin_take()
                        v.wait_ge(*now.prev())
                        v.tensor_tensor(BIG[:, k, :], u, a, ALU.mult).then_inc(Q["lin_free"], now.inc("lin_free"))
                store(G, KD, then_sum=True)
                norm(G, KD, post, add=0.5, then_sum=then_sum)

            v.wait_ge(Q["x_landed"], X_LANDED)
            begin_sum("const_landed")
            norm(XT, KD, "g_mix0", HT)
            v.wait_ge(Q["const_landed"], N_CONST)
            LV = BIGF[:, 0:4 * LAYERS * HD].rearrange("p (n x) -> p n x", x=HD)
            for L in range(LAYERS):
                for j in range(2):
                    v.wait_ge(*now.prev())
                    v.tensor_tensor_reduce( out=TMP[:, 0, 0:HD], in0=LV[:, (2 * j) * LAYERS + L, :],
                                           in1=LV[:, (2 * j + 1) * LAYERS + L, :], scale=1.0, scalar=0.0,
                                           op0=ALU.mult, op1=ALU.add,
                                           accum_out=LAM[:, 4 + 2 * L + j:5 + 2 * L + j])\
                        .then_inc(Q["dve_step"], now.inc("dve_step"))
            v.wait_ge(*now.prev())
            v.tensor_scalar(LAM[:, 0:1], LAM[:, 4:5], 0.0, None, ALU.mult)\
                .then_inc(Q["pos_landed"], now.inc("pos_landed"))
            v.wait_ge(Q["lam_exp"], now.next("lam_exp"))
            for L in range(LAYERS):
                init = 0.8 - 0.6 * math.exp(-0.3 * L)
                v.wait_ge(*now.prev())
                v.tensor_tensor(LAM[:, L:L + 1], LAM[:, 5 + 2 * L:6 + 2 * L], LAM[:, 4 + 2 * L:5 + 2 * L],
                                ALU.subtract)\
                    .then_inc(Q["dve_step"], now.inc("dve_step"))
                v.wait_ge(*now.prev())
                v.tensor_scalar(LAM[:, L:L + 1], LAM[:, L:L + 1], -init, None, ALU.add)\
                    .then_inc(Q["dve_step"], now.inc("dve_step"))
                v.wait_ge(*now.prev())
                v.tensor_scalar(LAM[:, 2 + L:3 + L], GC[:, GCOL[f"g_subln{L}"]:GCOL[f"g_subln{L}"] + 1],
                                1.0 - init, None, ALU.mult)\
                    .then_inc(Q["dve_step"], now.inc("dve_step"))
            v.wait_ge(*now.prev())
            v.tensor_scalar(NBG[:, :], GC[:, GCOL["b_gate"]:GCOL["b_gate"] + 16], -1.0, None, ALU.mult)\
                .then_inc(Q["raw_ready"], now.inc("raw_ready"))
            trig(COS[:, :], SIN[:, :], 0)
            v.wait_ge(Q["zero_stored"], now.next("zero_stored", 16))

            for L in range(LAYERS):
                if L:
                    norm(XT, KD, f"g_mix{L}", HT)
                store(SBQ, 4, scale=0.125)
                store(SBK, 4)
                store_tokens(SBV, 2, 256)
                store(DAQ, 4, scale=0.125)
                store(DAK, 4)
                store_tokens(DAV, 2, 256)
                rope([DAQ[:, t, :] for t in range(4)] + [DAK[:, t, :] for t in range(4)], COS, SIN)
                st["sigmoid"] = 0
                stick_breaking()

                def head_done(h):
                    ps = lin_take()
                    v.wait_ge(*now.prev())
                    v.tensor_copy(DAQ[:, h, :], ps).then_inc(Q["lin_free"], now.inc("lin_free"))

                def take_fill(u):
                    if u in DA_BRANCH:
                        first_branch(HT, DA_BRANCH.index(u), DA_BRANCH.index(u))
                    if u in DA_GATES:
                        take_gate(sum(SB_GATES) + DA_GATES.index(u))
                attention(DA_H, lambda qb: (qb + 1) * P, 2, 1.0, lambda qb: DAM[:, (3 - qb) * P:S], L, head_done,
                          take_fill, lambda u: next_sigmoid() if u in DA_SIGMOID else None)
                at[f"heads{L}"] = now.count("lin_free")
                for k in range(len(DA_BRANCH), KD):
                    first_branch(HT, k, k)
                now.skip("gate_ready", DA_H)
                now.skip("gate_free", DA_H)

                def sub_norm():
                    for h in range(DA_H):
                        v.wait_ge(Q["sub_rs"], now.next("sub_rs"))
                        v.wait_ge(*now.prev())
                        v.scalar_tensor_tensor(out=DAQ[:, h, :], in0=DAQ[:, h, :], scalar=LAM[:, 2 + L:3 + L],
                                               in1=ATT[:, (4 + h) * S:(5 + h) * S], op0=ALU.mult, op1=ALU.mult)\
                            .then_inc(Q["sub_ready"], now.inc("sub_ready"))
                sub_norm()
                while st["sigmoid"] < 2 * KD:
                    next_sigmoid()
                for k in range(KD):
                    second_branch(HT, k, KD + k)
                add_to_x()
                norm(XT, KD, f"g_ffn{L}", HT)
                moe(L)
                norm(XT, KD, f"g_ple{L}", HP)
                begin_sum("x_ready")
                for k in range(KD):
                    sigmoid_tail(k)
                    v.wait_ge(*now.prev())
                    v.tensor_tensor(TMP[:, 0, :], HT[:, k, :], G[:, k, :], ALU.mult)\
                        .then_inc(Q["dve_step"], now.inc("dve_step"))
                    v.wait_ge(*now.prev())
                    v.tensor_tensor(XT[:, k, :], XT[:, k, :], TMP[:, 0, :], ALU.add)\
                        .then_inc(Q["x_ready"], now.inc("x_ready"))
                    if k >= 2:
                        sum_square()
            norm(XT, KD, "g_final", XT, "x_ready", then_sum=True)
            ffn("ffn1_pre", "ffn1_post", True)
            norm(XT, KD, "mix_pre", HT)
            v.wait_ge(*now.prev())
            v.tensor_copy(ROPEM, A3[:, 9:11, :]).then_inc(Q["dve_step"], now.inc("dve_step"))
            store(CQ, 3)
            store(CKV, 2)
            store(BIG[:, 5:6, :], 1, rows=DQK)
            store(DQ, 4, scale=0.125)
            store(DK, 4)
            store_tokens(DV, 2, 256)
            rope([DQ[:, t, :] for t in range(4)] + [DK[:, t, :] for t in range(4)], COS, SIN)
            rope([KR], ROPEM[:, 0, :], ROPEM[:, 1, :], DQK)
            begin_sum("lin_free", QR // P)
            norm(CQ, QR // P, "q_norm", CQ)
            begin_sum("lin_free", KVR // P)
            norm(CKV, KVR // P, "kv_norm", CKV)

            def take_gate_fill(u):
                if u % 2:
                    take_gate(u // 2)
            attention(MLA_H, lambda qb: S, 1, 1.0, lambda qb: TOEP[:, (3 - qb) * P:(3 - qb) * P + S], 0, pair_done(DQ),
                      take_gate_fill, lambda u: sigmoid((u - 6) // 2) if u % 2 == 0 and u >= 6 else None)
            at["dil_done"] = now.count("lin_free")
            for k in range(2 * KD - 3, 2 * KD):
                sigmoid(k)
            store(HT, MLA_H, rows=DQK)
            rope([HT[0:DQK, h, :] for h in range(MLA_H)], ROPEM[:, 0, :], ROPEM[:, 1, :], DQK)
            for t in range(MLA_H // 2):
                ps = lin_take()
                v.wait_ge(*now.prev())
                v.tensor_copy(KT[0:HD, 2 * t, :], ps[0:HD, :]).then_inc(Q["dve_step"], now.inc("dve_step"))
                v.wait_ge(*now.prev())
                v.tensor_copy(KT[0:HD, 2 * t + 1, :], ps[HD:P, :]).then_inc(Q["lin_free"], now.inc("lin_free"))
            store_tokens(VA, 1, 512)

            def take_branch_fill(u):
                if u % 4 == 3:
                    first_branch(MB, u // 4, KD + u // 4)
            attention(MLA_H, lambda qb: S, 1, float(DQK) ** -0.5, None, 0, pair_done(HT), take_branch_fill)
            for k in range(KD):
                second_branch(MB, k, k)
            store(G, KD, then_sum=True)
            norm(G, KD, "mix_post", add=1.0, then_sum=True)
            ffn("ffn2_pre", "ffn2_post", False)
            at["out"] = now.count("x_ready")
            at["dve"] = dict(now.n)

        @block.scalar
        def _(act):
            now = Counts()
            st = {"norm": 0, "sq": 0}

            def square(src):
                if "k" not in st:
                    st["k"], st["sum"] = 0, at[f"norm{st['norm']}"]
                    st["norm"] += 1
                k = st["k"]
                st["k"] += 1
                sem, base = st["sum"]
                if sem != "const_landed":
                    act.wait_ge(Q[sem], base + k + 1)
                if now.count("sq_ready") >= 2:
                    act.wait_ge(Q["sq_used"], now.count("sq_ready") - 1)
                act.wait_ge(*now.prev())
                act.activation(SQ[:, k % 2, :], src[:, k, :], ACT.Square)\
                    .then_inc(Q["sq_ready"], now.inc("sq_ready"))

            def norm(src, nt, dim):
                while st.get("k", 0) < nt:
                    square(src)
                del st["k"]
                t = now.count("gate_ready")
                act.wait_ge(Q["gate_ready"], now.next("gate_ready"))
                act.wait_ge(*now.prev())
                act.activation(RSTD[:, :], PS[:, 2 + t % 2, :], ACT.Ln, bias=EPS_C[:, 0:1], scale=1.0 / dim)\
                    .then_inc(Q["gate_free"], now.inc("gate_free"))
                act.wait_ge(*now.prev())
                act.activation(RSTD[:, :], RSTD[:, :], ACT.Exp, scale=-0.5)\
                    .then_inc(Q["rstd_ready"], now.inc("rstd_ready"))

            def g_exp(k, taken, bias=False):
                act.wait_ge(Q["lin_free"], taken)
                kw = {"bias": NBG[:, k:k + 1]} if bias else {}
                act.wait_ge(*now.prev())
                act.activation(G[:, k, :], G[:, k, :], ACT.Exp, scale=-1.0, **kw).then_inc(Q["g_exp"], now.inc("g_exp"))

            def gate_exp(k):
                t = now.count("gate_ready")
                act.wait_ge(Q["gate_ready"], now.next("gate_ready"))
                act.wait_ge(*now.prev())
                act.activation(G[:, k, :], PS[:, 2 + t % 2, :], ACT.Exp, scale=-1.0)\
                    .then_inc(Q["gate_free"], now.inc("gate_free"))

            def fill_order(heads, fills):
                order = []
                for u in range(heads * TT):
                    order += [("fill", u)] * fills(u)
                    order += [("values", u // TT - 1)] if u % TT == 1 and u > TT else []
                return order + [("values", heads - 1)]

            def stick_breaking():
                lin0 = at[f"sb{st['L']}"]
                order = []
                for h in range(SB_H):
                    order += [("gate", sum(SB_GATES[:h]) + j) for j in range(SB_GATES[h])]
                    order += [("values", h - 1)] if h else []
                order.append(("values", SB_H - 1))

                def soft(h):
                    z = (2 + 3 * (h % 2)) * 512
                    act.wait_ge(Q["z_ready"], now.next("z_ready"))
                    if h >= 1:
                        act.wait_ge(Q["sp_ready"], now.next("sp_ready"))
                    t = ATT[:, 0:1280]
                    act.wait_ge(*now.prev())
                    act.activation(t, PSF[:, z:z + 1280], ACT.Abs).then_inc(Q["act_step"], now.inc("act_step"))
                    act.wait_ge(*now.prev())
                    act.activation(t, t, ACT.Exp, scale=-1.0).then_inc(Q["act_step"], now.inc("act_step"))
                    act.wait_ge(*now.prev())
                    act.activation(t, t, ACT.Ln, bias=1.0).then_inc(Q["soft_ready"], now.inc("soft_ready"))

                def weights(h):
                    z = (2 + 3 * (h % 2)) * 512
                    act.wait_ge(Q["lw_ready"], now.next("lw_ready"))
                    if h >= 2:
                        act.wait_ge(Q["lin_ready"], lin0 + order.index(("values", h - 2)) + 1)
                    act.wait_ge(*now.prev())
                    act.activation(ATT[:, (1280 * (3 + h % 2)):(1280 * (4 + h % 2))], PSF[:, z:z + 1280], ACT.Exp)\
                        .then_inc(Q["w_ready"], now.inc("w_ready"))
                soft(0)
                for h in range(SB_H):
                    if h + 1 < SB_H:
                        soft(h + 1)
                    weights(h)
                    if h:
                        for k in range(sum(SB_GATES[:h - 1]), sum(SB_GATES[:h])):
                            g_exp(k, lin0 + order.index(("gate", k)) + 1)
                for k in range(sum(SB_GATES[:-1]), sum(SB_GATES)):
                    g_exp(k, lin0 + order.index(("gate", k)) + 1)
                act.wait_ge(Q["sp_ready"], now.next("sp_ready"))

            def attention(heads, nkeys, maps, scale, masked, values_of, between=lambda u: None):
                jobs = [(h, qb) for h in range(heads) for qb in range(TT)]
                slots = 4 // maps
                tr0 = now.count("tr_ready")

                def exps(u):
                    h, qb = jobs[u]
                    n = nkeys(qb)
                    s = SM[:, 8 * (u % 2):8 * (u % 2) + 8]
                    act.wait_ge(Q["mx_ready"], now.next("mx_ready"))
                    if u >= 2:
                        act.wait_ge(Q["tr_ready"], tr0 + u - 1)
                    for m in range(maps):
                        x = E_[:, ((u % 2) * maps + m) * S:((u % 2) * maps + m) * S + n]
                        src = x if masked else PS[:, 4 + (u % slots) * maps + m, 0:n]
                        act.wait_ge(*now.prev())
                        act.activation(x, src, ACT.Exp, bias=s[:, m:m + 1], scale=scale,
                                       accum_out=s[:, 2 + m:3 + m])\
                            .then_inc(Q["act_step" if m < maps - 1 else "e_ready"], now.inc("act_step" if m < maps - 1 else "e_ready"))

                def turned(u):
                    h, qb = jobs[u]
                    nk = nkeys(qb) // P
                    act.wait_ge(Q["tr_ready"], now.next("tr_ready"))
                    if qb == 0 and h >= 2:
                        name, value = values_of(h - 2)
                        act.wait_ge(Q[name], value)
                    pt = ATT[:, (h % 2) * 4 * S:(h % 2 + 1) * 4 * S].rearrange("p (k q) -> p k q", k=TT)
                    act.wait_ge(*now.prev())
                    act.activation(pt[:, 0:nk, qb * P:(qb + 1) * P],
                                   PS[:, 2 + u % 2, 0:nk * P].rearrange("p (k q) -> p k q", q=P), ACT.Copy)\
                        .then_inc(Q["tr_done"], now.inc("tr_done"))
                exps(0)
                for u in range(len(jobs)):
                    if u + 1 < len(jobs):
                        exps(u + 1)
                    turned(u)
                    between(u)

            def moe(L):
                act.wait_ge(Q["route_exp"], L + 1)
                r = RT["ge"]
                act.wait_ge(*now.prev())
                act.activation(r[:, 0:20], r[:, 0:20], ACT.Exp).then_inc(Q["table_landed"], now.inc("table_landed"))

                def x_copy(par):
                    act.wait_ge(Q["x_turned"], now.next("x_turned"))
                    act.wait_ge(*now.prev())
                    act.activation(XGT[:, par, :], PSF[:, 1024:2048], ACT.Copy)\
                        .then_inc(Q["x_copied"], now.inc("x_copied"))

                def gate(par):
                    act.wait_ge(Q["gu_ready"], now.next("gu_ready"))
                    act.wait_ge(*now.prev())
                    act.activation(HID[:, par, :], PS[:, 4 + par, 0:EH], ACT.Exp, scale=-1.0)\
                        .then_inc(Q["e_gate"], now.inc("e_gate"))

                def store_rows(b, par):
                    act.wait_ge(Q["y_ready"], now.next("y_ready"))
                    act.wait_ge(Q["const_landed"], N_CONST)
                    if isinstance(b, int):
                        dst = YDR[b * CAP:(b + 1) * CAP, :]
                    else:
                        dst = YDR[bass.ds(b * CAP, CAP), :]
                    act.dma_start(dst, YB[:, par, :]).then_inc(Q[f"y_store{par}"], 16)
                x_copy(0)
                gate(0)
                x_copy(1)
                gate(1)
                x_copy(0)
                store_rows(0, 0)
                gate(0)
                x_copy(1)
                store_rows(1, 1)
                turns = (NB - 3) // 2
                with act.Fori(0, turns) as i:
                    now.enter(i, dict(x_turned=2, x_copied=2, gu_ready=2, e_gate=2, y_ready=2))
                    gate(1)
                    x_copy(0)
                    store_rows(i * 2 + 2, 0)
                    gate(0)
                    x_copy(1)
                    store_rows(i * 2 + 3, 1)
                now.leave(turns)
                store_rows(NB - 1, 0)
                if L == LAYERS - 1:
                    trig(COS[:, :], SIN[:, :])
                    trig(COSM, SINM)
                    act.preload_act_table_set("natural_log_exp_and_others")

            def ffn(dim=D):
                norm(XT, KD, D)
                for k in range(KF):
                    t = now.count("gate_ready")
                    act.wait_ge(Q["gate_ready"], now.next("gate_ready"))
                    if k >= 2:
                        act.wait_ge(Q["lin_free"], at[f"ffn{st['ffn']}"] + k - 1)
                    act.wait_ge(*now.prev())
                    act.activation(A3[:, 3 + k % 2, :], PS[:, 2 + t % 2, :], ACT.Exp, scale=-1.0)\
                        .then_inc(Q["e_gate"], now.inc("e_gate"))
                now.skip("gate_free", KF)
                st["ffn"] += 1
                norm(G, KD, D)

            st["ffn"] = 0
            act.wait_ge(Q["x_landed"], X_LANDED)
            norm(XT, KD, D)
            act.wait_ge(Q["pos_landed"], 1)
            act.wait_ge(*now.prev())
            act.activation(LAM[:, 4:8], LAM[:, 4:8], ACT.Exp).then_inc(Q["lam_exp"], now.inc("lam_exp"))

            def trig(cos, sin):
                act.wait_ge(Q["ang_ready"], now.next("ang_ready"))
                act.wait_ge(*now.prev())
                act.activation(sin, TMP[:, 0, :], ACT.Sin).then_inc(Q["act_step"], now.inc("act_step"))
                act.wait_ge(*now.prev())
                act.activation(TMP[:, 1, :], TMP[:, 0, :], ACT.Abs).then_inc(Q["act_step"], now.inc("act_step"))
                act.wait_ge(*now.prev())
                act.activation(cos, TMP[:, 1, :], ACT.Sin, scale=-1.0, bias=EPS_C[:, 1:2])\
                    .then_inc(Q["trig_ready"], now.inc("trig_ready"))
            trig(COS[:, :], SIN[:, :])
            act.preload_act_table_set("natural_log_exp_and_others")
            for L in range(LAYERS):
                st["L"] = L
                if L:
                    norm(XT, KD, D)
                stick_breaking()
                da0 = at[f"da{L}"]
                order = fill_order(DA_H, lambda u: (u in DA_BRANCH) + (u in DA_GATES))
                attention(DA_H, lambda qb: (qb + 1) * P, 2, 1.0, True,
                          lambda h: ("lin_ready", da0 + order.index(("values", h)) + 1),
                          lambda u: (g_exp(sum(SB_GATES) + DA_GATES.index(u - 2),
                                           da0 + order.index(("fill", u - 2)) + 1) if u - 2 in DA_GATES else None))
                for h in range(DA_H):
                    act.wait_ge(Q["lin_free"], at[f"heads{L}"])
                    act.wait_ge(*now.prev())
                    act.activation(ATT[:, h * S:(h + 1) * S], DAQ[:, h, :], ACT.Square)\
                        .then_inc(Q["sub_sq"], now.inc("sub_sq"))
                for h in range(DA_H):
                    t = now.count("gate_ready")
                    act.wait_ge(Q["gate_ready"], now.next("gate_ready"))
                    a = ATT[:, (4 + h) * S:(5 + h) * S]
                    act.wait_ge(*now.prev())
                    act.activation(a, PS[:, 2 + t % 2, :], ACT.Ln, bias=EPS_C[:, 0:1], scale=1.0 / P)\
                        .then_inc(Q["gate_free"], now.inc("gate_free"))
                    act.wait_ge(*now.prev())
                    act.activation(a, a, ACT.Exp, scale=-0.5).then_inc(Q["sub_rs"], now.inc("sub_rs"))
                norm(XT, KD, D)
                moe(L)
                norm(XT, KD, D)
                for k in range(KD):
                    gate_exp(k)
                    if k >= 2:
                        square(XT)
            norm(XT, KD, D)
            ffn()
            norm(XT, KD, D)
            norm(CQ, QR // P, QR)
            norm(CKV, KVR // P, KVR)
            dil = fill_order(MLA_H, lambda u: u % 2)
            mla = fill_order(MLA_H, lambda u: u % 4 == 3)

            def dil_gate(k):
                g_exp(k, at["dil"] + dil.index(("fill", 2 * k + 1)) + 1, bias=True)
            attention(MLA_H, lambda qb: S, 1, 1.0, True,
                      lambda h: ("lin_ready", at["dil"] + dil.index(("values", h)) + 1),
                      lambda u: dil_gate((u - 3) // 2) if u >= 3 and u % 2 else None)
            dil_gate(2 * KD - 1)
            attention(MLA_H, lambda qb: S, 1, float(DQK) ** -0.5, False,
                      lambda h: ("lin_ready", at["mla"] + mla.index(("values", h)) + 1))
            norm(G, KD, D)
            ffn()

        @block.gpsimd
        def _(pool):
            now = Counts()

            zeros = BIGF[:, 8 * S:8 * S + NBP].bitcast(I32)
            pool.memset(zeros, 0).then_inc(Q["zero_ready"], now.inc("zero_ready"))
            pool.wait_ge(*now.prev())
            pool.dma_start(SLOTS.rearrange("(p b) o -> p (b o)", p=P), zeros).then_inc(Q["zero_stored"], 16)
            pool.wait_ge(Q["zero_stored"], 16)

            def keep_later(a, name):
                pool.wait_ge(*now.prev())
                d = a[:, 0:512].rearrange("p (b q) -> p b q", b=TT)
                pool.affine_select(out=d, in_=d, compare_op=ALU.is_gt, fill=0.0, base=0,
                                   pattern=[[0, TT], [1, P]], channel_multiplier=-1)\
                    .then_inc(Q[name], now.inc(name))

            def softplus(h):
                pool.wait_ge(Q["sp_ready"], now.next("sp_ready"))
                keep_later(ATT[:, (1280 * (1 + h % 2)):(1280 * (2 + h % 2))], "sp_masked")

            def weights(h):
                pool.wait_ge(Q["w_ready"], now.next("w_ready"))
                keep_later(ATT[:, (1280 * (3 + h % 2)):(1280 * (4 + h % 2))], "w_masked")

            idx = RT["idx"].bitcast(U32)
            sloti, adri = RT["sloti"].bitcast(U32), RT["adri"].bitcast(U32)
            IOA = bass.IndirectOffsetOnAxis

            def gather(b):
                pool.indirect_dma_start(out=XG[:, b % 2, :], out_offset=None, in_=HDR,
                                        in_offset=IOA(ap=idx[:, b:b + 1], axis=0)).then_inc(Q[f"x_gather{b % 2}"], 16)

            pos2 = A["positions_2"].rearrange("a t -> (a t)").partition_broadcast(P)
            for L in range(LAYERS):
                softplus(0)
                for h in range(SB_H):
                    if h + 1 < SB_H:
                        softplus(h + 1)
                    weights(h)
                pool.wait_ge(Q["lin_free"], at[f"htok{L}"])
                pool.dma_start(HDR.rearrange("(t p) d -> p t d", p=P), HTOK).then_inc(Q["h_stored"], 16)
                pool.dma_start(PLT, A["pT"][L].rearrange("(k p) t -> p k t", p=P)).then_inc(Q["pl_landed"], 16)
                if L == LAYERS - 1:
                    for dst in (SIN[:, :], SINM):
                        pool.dma_start(dst.bitcast(I32), pos2).then_inc(Q["pos2_landed"], 16)
                    pool.dma_start(TOEP, A["c_lnc"]).then_inc(Q["pos2_landed"], 16)
                pool.wait_ge(Q["slots_ready"], now.next("slots_ready"))
                for j in range(2 * TT):
                    pool.indirect_dma_start(out=SLOTS, out_offset=IOA(ap=adri[:, j:j + 1], axis=0),
                                            in_=TOK[:, j // 2:j // 2 + 1], in_offset=None)\
                        .then_inc(Q["tok_scattered"], 16)
                pool.wait_ge(Q["tok_scattered"], now.next("tok_scattered", 16 * 2 * TT))
                pool.dma_start(RT["idx"].bitcast(I32), SLOTS.rearrange("(p b) o -> p (b o)", p=P))\
                    .then_inc(Q["idx_landed"], 16)
                pool.wait_ge(Q["idx_landed"], now.next("idx_landed", 16))
                pool.wait_ge(Q["h_stored"], now.next("h_stored", 16))
                x0 = at[f"moe{L}"]["x_turned"]
                for b in range(NBP):
                    if b >= 2:
                        pool.wait_ge(Q["x_turned"], x0 + b - 1)
                    gather(b)
                pool.wait_ge(Q["y_store0"], 16 * (L + 1) * ((NB + 1) // 2))
                pool.wait_ge(Q["y_store1"], 16 * (L + 1) * (NB // 2))
                for j in range(2 * TT):
                    pool.indirect_dma_start(out=YG[:, j, :], out_offset=None, in_=YDR,
                                            in_offset=IOA(ap=sloti[:, j:j + 1], axis=0))\
                        .then_inc(Q[f"y_gathered{j // 2}"], 16)
            pool.wait_ge(Q["pos2_landed"], 48)
            pool.wait_ge(Q["lin_free"], at["dil_done"])
            for h in range(MLA_H):
                pool.tensor_copy(KT[NOPE:DQK, h, :], KR[NOPE:DQK, :]).then_inc(Q["kr_copied"], now.inc("kr_copied"))

        @block.sync
        def _(sp):
            now = Counts()

            def const(dst, src):
                sp.dma_start(dst, src).then_inc(Q["const_landed"], 16)
            xv = A["xT"].rearrange("(k p) t -> p k t", p=P)
            for dst, src in ((XT[:, 0:4, :], xv[:, 0:4, :]), (XT[:, 4:8, :], xv[:, 4:8, :]), (GC[:, :], A["gains"]),
                             (EPS_C[:, :], A["c_eps"]), (MATS[:, :], A["c_mats"])):
                sp.dma_start(dst, src).then_inc(Q["x_landed"], 16)
            plan = Ring()
            n = [0]

            def load():
                place, fill = plan.next()
                if fill > 1:
                    name, value = used[(place, fill - 1)]
                    sp.wait_ge(Q[name], value)
                sp.dma_start(ring[:, place, :], A["stream"][n[0]]).then_inc(w_landed[place], 16)
                n[0] += 1

            for _ in range(3):
                load()
            const(FREQ[:, :], A["c_freq"])
            const(SIN[:, :].bitcast(I32), A["positions"].rearrange("a t -> (a t)").partition_broadcast(P))
            const(BIGF[:, 0:4 * LAYERS * HD], A["lam"].partition_broadcast(P))
            const(DAM[:, :], A["c_da"])
            const(REV[:, :], A["c_rev"])
            const(BLK[:, :], A["c_blk"])
            const(TOK[:, :], A["c_tok"])
            const(WR[:, :, :, :], A["w_router"])
            const(BR[:, :, :], A["b_router"].partition_broadcast(P))

            def experts(L):
                plan.align()
                p0, before = plan.blocks()
                first = at[f"moe{L}"]
                sp.wait_ge(Q["blk_ready"], L + 1)

                def block_load(i, par, prior):
                    if isinstance(i, int):
                        b = RT["blki"].bitcast(I32)[0:1, 2 * i + par:2 * i + par + 1]
                    else:
                        b = RT["blki"].bitcast(I32)[0:1, bass.ds(i * 2 + par, 1)]
                    x = sp.value_load(b, min_val=0, max_val=NE - 1)
                    for j in range(3):
                        place = (p0 + 3 * par + j) % RING
                        if prior is None:
                            if before[place]:
                                name, value = used[(place, before[place])]
                                sp.wait_ge(Q[name], value)
                        else:
                            name = "dn_ready" if j == 2 else "gu_ready"
                            sp.wait_ge(Q[name], prior * 2 + (first[name] + par + 1))
                            sp.wait_ge(Q["const_landed"], N_CONST)
                        src = A["experts"][L, bass.ds(x, 1), j, :, :].rearrange("a p n -> (a p) n")
                        sp.dma_start(ring[:, place, :], src).then_inc(w_landed[place], 16)
                block_load(0, 0, None)
                block_load(0, 1, None)
                with sp.Fori(0, NB // 2 - 1) as i:
                    block_load(i + 1, 0, i)
                    block_load(i + 1, 1, i)
                block_load(NB // 2, 0, NB // 2 - 1)

            for L in range(LAYERS):
                for _ in range(N_LAYER_U - n[0] if L == 0 else N_LAYER_U):
                    load()
                experts(L)
                for t in range(TT):
                    sp.wait_ge(Q[f"y_gathered{t}"], 32 * (L + 1))
                for _ in range(N_PLE_U):
                    load()
            for _ in range(2 * N_FFN_U + N_MIX_U):
                load()
            assert n[0] == N_STREAM
            sp.wait_ge(Q["x_ready"], at["out"])
            sp.dma_start(out.rearrange("(k p) t -> p k t", p=P), XT[:, :, :]).then_inc(Q["stored_out"], 16)
            sp.wait_ge(Q["stored_out"], 16)
            sp.wait_ge(Q["y_store0"], 16 * LAYERS * ((NB + 1) // 2))
            sp.wait_ge(Q["y_store1"], 16 * LAYERS * (NB // 2))


def host_arrays(x):
    a = {k: np.ascontiguousarray(v) for k, v in x.items()}
    out = {"xT": a["x"][0].T, "pT": a["p"][:, 0].transpose(0, 2, 1), "positions": a["positions"],
           "positions_2": a["positions_2"]}
    stream = []
    for i in range(LAYERS):
        stream += layer_units(a["w_in"][i], a["w_br_a"][i], a["w_br_b"][i], a["w_o"][i], a["w_ple"][i],
                              a["w_ple_gate"][i])
    f1 = ffn_units(a["ffn1_w_gate_2"][0], a["ffn1_w_up_2"][0], a["ffn1_w_down_2"][0])
    f2 = ffn_units(a["ffn2_w_gate_2"][0], a["ffn2_w_up_2"][0], a["ffn2_w_down_2"][0])
    mix = mixer_units(a["w_in_2"][0], a["w_uq_2"][0], a["w_uk_2"][0], a["w_uv_2"][0],
                      a["w_branch_a_2"][0], a["w_branch_b_2"][0], a["w_out_2"][0])
    out["stream"] = np.stack(stream + f1 + mix + f2)
    wg = a["w_exp_gate"].reshape(LAYERS, NE, KD, P, EH).transpose(0, 1, 3, 2, 4).reshape(LAYERS, NE, P, UNIT)
    wu = a["w_exp_up"].reshape(LAYERS, NE, KD, P, EH).transpose(0, 1, 3, 2, 4).reshape(LAYERS, NE, P, UNIT)
    wd = a["w_exp_down"].reshape(LAYERS, NE, 2, P, D).transpose(0, 1, 3, 2, 4).reshape(LAYERS, NE, P, UNIT)
    out["experts"] = np.stack([wg, wu, wd], axis=2)
    gains = []
    for name, length in GAINS:
        if name[-1].isdigit() and name[:-1] in ("g_mix", "g_ffn", "g_ple", "g_subln"):
            g = a[name[:-1]][int(name[-1])]
        elif name == "g_final":
            g = a[name]
        elif name == "b_gate":
            g = a["b_gate_2"][0]
        else:
            g = a[name + "_g_2"][0]
        gains.append(g.reshape(length // P, P).T)
    out["gains"] = np.concatenate(gains, axis=1)
    out["lam"] = np.concatenate([a[n].reshape(-1) for n in ("lam_q1", "lam_k1", "lam_q2", "lam_k2")])
    wr = np.concatenate([a["w_router_group"], a["w_router_expert"]], axis=2)
    out["w_router"] = wr.reshape(LAYERS, KD, P, NG + NE).transpose(2, 0, 1, 3)
    out["b_router"] = np.concatenate([a["b_router_group"], a["b_router_expert"]], axis=1)
    out.update(shape_constants())
    return {k: np.ascontiguousarray(v) for k, v in out.items()}


def kernel(**inputs):
    import concourse.bacc as bacc
    from concourse.bass_utils import run_bass_kernel_spmd

    nc = bacc.Bacc("TRN2", target_bir_lowering=False, num_devices=1)
    arrays, aps = {}, {}
    for name, a in host_arrays(inputs).items():
        arrays[f"in_{name}"] = a
        aps[name] = nc.dram_tensor(f"in_{name}", a.shape, mybir.dt.from_np(a.dtype), kind="ExternalInput").ap()
    out = nc.dram_tensor("out_T", (D, S), F32, kind="ExternalOutput").ap()
    build_program(nc, aps, out)
    r = run_bass_kernel_spmd(nc, [arrays], core_ids=[0])
    return np.ascontiguousarray(r.results[0]["out_T"].T).reshape(1, S, D)
```
